# Optimizing a Trainium2 kernel written in Bass

```python
import jax
import jax.numpy as jnp
from jax import lax
import numpy as np
import math
import jax, jax.numpy as jnp

D_MODEL = 1024
BATCH = 1
SEQ = 256
DEPTH = 1

D_MIX = 1024
HG_HEADS = 4
HG_KDIM = 128
HG_VDIM = 128
HG_WIDTH = HG_HEADS * HG_VDIM
HG_CHUNK = 64
SW_HEADS = 4
SW_HDIM = 64
SW_WIDTH = SW_HEADS * SW_HDIM
SW_PATTERNS = ((128, 1), (512, 4), (2048, 16))
SW_BLOCK = 128
RK_HEADS = 4
RK_HDIM = 64
RK_WIDTH = RK_HEADS * RK_HDIM
RK_DECAY_LORA = 64
RK_AAA_LORA = 64
RK_MV_LORA = 32
RK_GATE_LORA = 128
RK_GN_EPS = 64e-5
HG_IN = 4 * HG_WIDTH
SW_IN = 3 * SW_WIDTH
RK_IN = 3 * RK_WIDTH + RK_DECAY_LORA + RK_AAA_LORA + RK_GATE_LORA
N_IN = HG_IN + SW_IN + RK_IN
D_FF = 2816
CONV_W = 3
PLE_DIM = 256
NORM_EPS = 1e-6


def rmsnorm(x, g):
    xf = x.astype(jnp.float32)
    y = xf * lax.rsqrt(jnp.mean(xf * xf, axis=-1, keepdims=True) + NORM_EPS)
    return (y * g.astype(jnp.float32)).astype(x.dtype)

def hgrn2_mix(q_raw, f_raw, i_raw, g_raw, lower_bound, gnorm_g):
    f32 = jnp.float32
    B_, S_, _ = q_raw.shape
    nc = S_ // HG_CHUNK
    q = jax.nn.silu(q_raw.astype(f32))
    f = lower_bound + (1.0 - lower_bound) * jax.nn.sigmoid(f_raw.astype(f32))
    k = 1.0 - f
    log_f = jnp.log(f)

    def chunks(t):
        return t.reshape(B_, nc, HG_CHUNK, HG_HEADS, -1).transpose(1, 0, 3, 2, 4)

    causal = jnp.tril(jnp.ones((HG_CHUNK, HG_CHUNK), dtype=bool))

    def step(state, inp):
        qc, kc, vc, lfc = inp
        b = jnp.cumsum(lfc, axis=2)
        b_last = b[:, :, -1:, :]
        o_inter = jnp.einsum('bhck,bhkv->bhcv', qc * jnp.exp(b), state)
        rel = jnp.where(causal[:, :, None], b[:, :, :, None, :] - b[:, :, None, :, :], -jnp.inf)
        scores = jnp.einsum('bhik,bhjk,bhijk->bhij', qc, kc, jnp.exp(rel))
        o_intra = jnp.einsum('bhij,bhjv->bhiv', scores, vc)
        state = (jnp.exp(b_last[:, :, 0, :])[..., None] * state
                 + jnp.einsum('bhck,bhcv->bhkv', kc * jnp.exp(b_last - b), vc))
        return state, o_inter + o_intra

    s0 = jnp.zeros((B_, HG_HEADS, HG_KDIM, HG_VDIM), f32)
    _, o = lax.scan(step, s0, (chunks(q), chunks(k), chunks(i_raw.astype(f32)), chunks(log_f)))
    o = o.transpose(1, 0, 3, 2, 4).reshape(B_, S_, HG_HEADS, HG_VDIM)
    o = o * lax.rsqrt(jnp.mean(o * o, axis=-1, keepdims=True) + NORM_EPS)
    o = o.reshape(B_, S_, HG_WIDTH) * gnorm_g.astype(f32) * jax.nn.silu(g_raw.astype(f32))
    return o.astype(q_raw.dtype)

def banded_causal_attention(q, k, v, n_back):
    f32 = jnp.float32
    N, L, H, Dh = q.shape
    blk = SW_BLOCK
    nb = -(-L // blk)
    padw = ((0, 0), (0, nb * blk - L), (0, 0), (0, 0))
    qb = jnp.pad(q.astype(f32), padw).reshape(N, nb, blk, H, Dh)
    kb = jnp.pad(k.astype(f32), padw).reshape(N, nb, blk, H, Dh)
    vb = jnp.pad(v.astype(f32), padw).reshape(N, nb, blk, H, Dh)

    def with_prev(t):
        prev = jnp.pad(t, ((0, 0), (1, 0), (0, 0), (0, 0), (0, 0)))[:, :-1]
        return jnp.concatenate([prev, t], axis=2)

    kw, vw = with_prev(kb), with_prev(vb)
    s = jnp.einsum('nbqhd,nbkhd->nbhqk', qb, kw) * (Dh ** -0.5)
    qi = jnp.arange(blk)[:, None]
    kj = jnp.arange(2 * blk)[None, :]
    dist = qi - kj + blk
    kpos = jnp.arange(nb)[:, None, None] * blk + kj[None] - blk
    valid = (dist >= 0)[None] & (dist <= n_back)[None] & (kpos >= 0)
    s = jnp.where(valid[None, :, None], s, -jnp.inf)
    lse = jax.nn.logsumexp(s, axis=-1)
    prob = jnp.exp(s - lse[..., None])
    o = jnp.einsum('nbhqk,nbkhd->nbqhd', prob, vw).reshape(N, nb * blk, H, Dh)[:, :L]
    lse = lse.transpose(0, 1, 3, 2).reshape(N, nb * blk, H)[:, :L]
    return o, lse

def stride_gather(t, dil):
    B_, S_ = t.shape[:2]
    rest = t.shape[2:]
    return t.reshape((B_, S_ // dil, dil) + rest).swapaxes(1, 2).reshape((B_ * dil, S_ // dil) + rest)

def stride_scatter(t, B_, dil):
    L = t.shape[1]
    rest = t.shape[2:]
    return t.reshape((B_, dil, L) + rest).swapaxes(1, 2).reshape((B_, L * dil) + rest)

def dilated_window_mix(q_raw, k_raw, v_raw):
    B_, S_, _ = q_raw.shape
    q, k, v = (t.reshape(B_, S_, SW_HEADS, SW_HDIM) for t in (q_raw, k_raw, v_raw))
    outs, lses = [], []
    for window, dil in SW_PATTERNS:
        o, lse = banded_causal_attention(stride_gather(q, dil), stride_gather(k, dil),
                                         stride_gather(v, dil), window // dil)
        outs.append(stride_scatter(o, B_, dil))
        lses.append(stride_scatter(lse, B_, dil))
    wts = jax.nn.softmax(jnp.stack(lses, 0), axis=0)
    o = jnp.sum(wts[..., None] * jnp.stack(outs, 0), axis=0)
    return o.reshape(B_, S_, SW_WIDTH).astype(q_raw.dtype)

def rwkv7_mix(c, mu, w0, w2, a0, a2, g2, k_k, k_a, r_k, ln_w, ln_b, v_first, v_res):
    f32 = jnp.float32
    B_, S_, _ = c.shape
    cf = c.astype(f32)
    c_prev = jnp.pad(cf, ((0, 0), (1, 0), (0, 0)))[:, :-1]
    cm = cf + (c_prev - cf) * mu
    splits = [RK_WIDTH, 2 * RK_WIDTH, 3 * RK_WIDTH, 3 * RK_WIDTH + RK_DECAY_LORA,
              3 * RK_WIDTH + RK_DECAY_LORA + RK_AAA_LORA]
    r, k, v, wd, ad, gd = jnp.split(cm, splits, axis=-1)
    w = -jax.nn.softplus(-(w0 + jnp.tanh(wd) @ w2)) - 0.5
    decay = jnp.exp(-jnp.exp(w))
    a = jax.nn.sigmoid(a0 + ad @ a2)
    g = jax.nn.sigmoid(gd) @ g2
    if v_res is None:
        v_first = v
    else:
        v0, v1, v2 = v_res
        v = v + (v_first - v) * jax.nn.sigmoid(v0 + (v @ v1) @ v2)

    def heads(t):
        return t.reshape(B_, S_, RK_HEADS, RK_HDIM)

    kk = heads(k * k_k)
    kk = kk / jnp.maximum(jnp.linalg.norm(kk, axis=-1, keepdims=True), 1e-12)
    k = k * (1.0 + (a - 1.0) * k_a)
    rh, kh, vh, wh, ah = heads(r), heads(k), heads(v), heads(decay), heads(a)

    def step(state, inp):
        r_t, w_t, k_t, v_t, kk_t, a_t = inp
        sa = jnp.einsum('bhvk,bhk->bhv', state, -kk_t)
        state = (state * w_t[:, :, None, :] + sa[..., None] * (kk_t * a_t)[:, :, None, :]
                 + v_t[..., None] * k_t[:, :, None, :])
        return state, jnp.einsum('bhvk,bhk->bhv', state, r_t)

    s0 = jnp.zeros((B_, RK_HEADS, RK_HDIM, RK_HDIM), f32)
    xs = (rh.swapaxes(0, 1), wh.swapaxes(0, 1), kh.swapaxes(0, 1), vh.swapaxes(0, 1),
          kk.swapaxes(0, 1), ah.swapaxes(0, 1))
    _, y = lax.scan(step, s0, xs)
    y = y.swapaxes(0, 1)
    mean = jnp.mean(y, axis=-1, keepdims=True)
    var = jnp.mean((y - mean) ** 2, axis=-1, keepdims=True)
    y = ((y - mean) * lax.rsqrt(var + RK_GN_EPS)).reshape(B_, S_, RK_WIDTH) * ln_w + ln_b
    bonus = jnp.sum(rh * kh * r_k, axis=-1, keepdims=True) * vh
    y = (y + bonus.reshape(B_, S_, RK_WIDTH)) * g
    return y.astype(c.dtype), v_first

def conv_glu_ffn(hn, w_up, conv_w, conv_b, w_down):
    u = hn @ w_up
    S_ = u.shape[1]
    up = jnp.pad(u, ((0, 0), (CONV_W - 1, 0), (0, 0)))
    uc = conv_b + conv_w[0] * up[:, 0:S_]
    for j in range(1, CONV_W):
        uc = uc + conv_w[j] * up[:, j:j + S_]
    gate, val = jnp.split(uc, 2, axis=-1)
    return (jax.nn.silu(gate) * val) @ w_down

def first_inputs(seed: int = 0) -> dict:
    key = jax.random.key(seed)
    ks = iter(jax.random.split(key, 40))

    def nrm(shape, scale):
        return jax.random.normal(next(ks), shape, jnp.float32) * scale

    def unif(shape, lo, hi):
        return jax.random.uniform(next(ks), shape, jnp.float32, lo, hi)

    L = DEPTH
    return {
        'x': nrm((BATCH, SEQ, D_MODEL), 1.0),
        'p': nrm((DEPTH, BATCH, SEQ, PLE_DIM), 1.0),
        'w_in': nrm((L, D_MODEL, N_IN), D_MODEL ** -0.5),
        'w_out': nrm((L, D_MIX, D_MODEL), D_MIX ** -0.5),
        'norm_mix_g': 1.0 + nrm((L, D_MODEL), 0.02),
        'norm_ffn_g': 1.0 + nrm((L, D_MODEL), 0.02),
        'norm_ple_g': 1.0 + nrm((L, D_MODEL), 0.02),
        'final_norm_g': 1.0 + nrm((D_MODEL,), 0.02),
        'hgrn_lower_bounds': nrm((L, HG_HEADS * HG_KDIM), 0.5),
        'hgrn_gnorm_g': 1.0 + nrm((L, HG_WIDTH), 0.02),
        'rwkv_mu': unif((L, RK_IN), 0.0, 1.0),
        'rwkv_w0': unif((L, RK_WIDTH), -5.0, -0.5),
        'rwkv_w2': nrm((L, RK_DECAY_LORA, RK_WIDTH), 0.1 * RK_DECAY_LORA ** -0.5),
        'rwkv_a0': nrm((L, RK_WIDTH), 0.1),
        'rwkv_a2': nrm((L, RK_AAA_LORA, RK_WIDTH), 0.1 * RK_AAA_LORA ** -0.5),
        'rwkv_g2': nrm((L, RK_GATE_LORA, RK_WIDTH), RK_GATE_LORA ** -0.5),
        'rwkv_k_k': 0.85 + nrm((L, RK_WIDTH), 0.05),
        'rwkv_k_a': 1.0 + nrm((L, RK_WIDTH), 0.05),
        'rwkv_r_k': nrm((L, RK_HEADS, RK_HDIM), 0.1),
        'rwkv_ln_w': 1.0 + nrm((L, RK_WIDTH), 0.02),
        'rwkv_ln_b': nrm((L, RK_WIDTH), 0.02),
        'rwkv_v0': 1.0 + nrm((L - 1, RK_WIDTH), 0.1),
        'rwkv_v1': nrm((L - 1, RK_WIDTH, RK_MV_LORA), 0.1 * RK_WIDTH ** -0.5),
        'rwkv_v2': nrm((L - 1, RK_MV_LORA, RK_WIDTH), 0.1 * RK_MV_LORA ** -0.5),
        'ffn_up': nrm((L, D_MODEL, 2 * D_FF), D_MODEL ** -0.5),
        'ffn_conv_w': nrm((L, CONV_W, 2 * D_FF), CONV_W ** -0.5),
        'ffn_conv_b': nrm((L, 2 * D_FF), 0.02),
        'ffn_down': nrm((L, D_FF, D_MODEL), D_FF ** -0.5),
        'ple_proj': nrm((L, PLE_DIM, D_MODEL), PLE_DIM ** -0.5),
        'ple_gate': nrm((L, D_MODEL, D_MODEL), D_MODEL ** -0.5),
    }

def first_block(x, p, w_in, w_out, norm_mix_g, norm_ffn_g, norm_ple_g, final_norm_g,
              hgrn_lower_bounds, hgrn_gnorm_g, rwkv_mu, rwkv_w0, rwkv_w2, rwkv_a0, rwkv_a2,
              rwkv_g2, rwkv_k_k, rwkv_k_a, rwkv_r_k, rwkv_ln_w, rwkv_ln_b, rwkv_v0, rwkv_v1,
              rwkv_v2, ffn_up, ffn_conv_w, ffn_conv_b, ffn_down, ple_proj, ple_gate):
    lbs = jax.nn.softmax(hgrn_lower_bounds.astype(jnp.float32), axis=0)
    lbs = jnp.cumsum(lbs, axis=0) - lbs[0]
    splits = [HG_WIDTH, 2 * HG_WIDTH, 3 * HG_WIDTH, 4 * HG_WIDTH,
              HG_IN + SW_WIDTH, HG_IN + 2 * SW_WIDTH, HG_IN + 3 * SW_WIDTH]
    h = x
    v_first = None
    for l in range(DEPTH):
        z = rmsnorm(h, norm_mix_g[l]) @ w_in[l]
        a_q, a_f, a_i, a_g, b_q, b_k, b_v, c_in = jnp.split(z, splits, axis=-1)
        o_a = hgrn2_mix(a_q, a_f, a_i, a_g, lbs[l], hgrn_gnorm_g[l])
        o_b = dilated_window_mix(b_q, b_k, b_v)
        v_res = None if l == 0 else (rwkv_v0[l - 1], rwkv_v1[l - 1], rwkv_v2[l - 1])
        o_c, v_first = rwkv7_mix(c_in, rwkv_mu[l], rwkv_w0[l], rwkv_w2[l], rwkv_a0[l], rwkv_a2[l],
                                 rwkv_g2[l], rwkv_k_k[l], rwkv_k_a[l], rwkv_r_k[l], rwkv_ln_w[l],
                                 rwkv_ln_b[l], v_first, v_res)
        h = h + jnp.concatenate([o_a, o_b.astype(o_a.dtype), o_c.astype(o_a.dtype)], axis=-1) @ w_out[l]
        h = h + conv_glu_ffn(rmsnorm(h, norm_ffn_g[l]), ffn_up[l], ffn_conv_w[l], ffn_conv_b[l], ffn_down[l])
        gate = jax.nn.sigmoid(rmsnorm(h, norm_ple_g[l]) @ ple_gate[l])
        h = h + gate * (p[l] @ ple_proj[l])
    return rmsnorm(h, final_norm_g)


MEM_LEN = 256
EPS = 1e-6
NEG_INF = -1e30
CONV_WIDTH = 512
CONV_KERNEL = 31
NSA_HEADS = 8
HEAD_DIM = 64
NSA_WIDTH = NSA_HEADS * HEAD_DIM
NSA_KV_GROUPS = 2
HEADS_PER_GROUP = NSA_HEADS // NSA_KV_GROUPS
KV_WIDTH = NSA_KV_GROUPS * HEAD_DIM
MIX_WIDTH = CONV_WIDTH + NSA_WIDTH
ROT_DIM = HEAD_DIM // 4
ROPE_THETA = 500000.0
CMP_BLOCK = 32
CMP_STRIDE = 16
CMP_HIDDEN = 128
SEL_BLOCK = 64
N_SELECT = 16
N_LOCAL_SEL = 2
FORCED_SCORE = 1e9
WINDOW = 512
WIN_Q_BLOCK = 128
SEL_Q_CHUNK = 32
MEM_HEADS = 4
MEM_HEAD_DIM = D_MODEL // MEM_HEADS
PEER_HEADS = 8
PEER_KEYS = 128
PEER_EXPERTS = PEER_KEYS * PEER_KEYS
PEER_QDIM = 256
PEER_HALF = PEER_QDIM // 2
PEER_TOPK = 16
PEER_TOKEN_CHUNK = 128
IN_SIZES = [CONV_WIDTH, CONV_WIDTH, NSA_WIDTH,
            KV_WIDTH, KV_WIDTH, KV_WIDTH, KV_WIDTH, KV_WIDTH, KV_WIDTH,
            3 * NSA_HEADS]
IN_COLS = sum(IN_SIZES)
IN_SPLITS = [sum(IN_SIZES[:i + 1]) for i in range(len(IN_SIZES) - 1)]


def rmsnorm_2(x, g):
    xf = x.astype(jnp.float32)
    y = xf * lax.rsqrt(jnp.mean(xf * xf, axis=-1, keepdims=True) + EPS)
    return (y * g.astype(jnp.float32)).astype(x.dtype)

def layernorm(x, g, b):
    xf = x.astype(jnp.float32)
    mu = jnp.mean(xf, axis=-1, keepdims=True)
    var = jnp.mean(jnp.square(xf - mu), axis=-1, keepdims=True)
    y = (xf - mu) * lax.rsqrt(var + EPS) * g.astype(jnp.float32) + b.astype(jnp.float32)
    return y.astype(x.dtype)

def masked_softmax(s, mask):
    s = jnp.where(mask, s.astype(jnp.float32), NEG_INF)
    return jax.nn.softmax(s, axis=-1) * mask

def partial_rope(x, positions):
    half = ROT_DIM // 2
    inv = ROPE_THETA ** (-(jnp.arange(half, dtype=jnp.float32) * 2.0 / ROT_DIM))
    ang = positions.astype(jnp.float32)[..., None] * inv
    cos = jnp.cos(ang)[:, :, None, :]
    sin = jnp.sin(ang)[:, :, None, :]
    xr = x[..., :ROT_DIM].astype(jnp.float32)
    x1, x2 = xr[..., :half], xr[..., half:]
    rot = jnp.concatenate([x1 * cos - x2 * sin, x2 * cos + x1 * sin], axis=-1).astype(x.dtype)
    return jnp.concatenate([rot, x[..., ROT_DIM:]], axis=-1)

def conformer_conv(a, b, w_dw, b_dw, ln_g, ln_b):
    u = a * jax.nn.sigmoid(b)
    y = lax.conv_general_dilated(
        u, w_dw[:, None, :], window_strides=(1,), padding=[(CONV_KERNEL - 1, 0)],
        dimension_numbers=('NWC', 'WIO', 'NWC'), feature_group_count=CONV_WIDTH)
    y = layernorm(y + b_dw, ln_g, ln_b)
    return jax.nn.silu(y)

def compress_tokens(kv, pos_emb, w1, b1, w2, b2):
    B, T, G, dh = kv.shape
    n_cmp = (T - CMP_BLOCK) // CMP_STRIDE + 1
    idx = jnp.arange(n_cmp)[:, None] * CMP_STRIDE + jnp.arange(CMP_BLOCK)[None, :]
    blk = kv[:, idx] + pos_emb[:, None, :]
    blk = blk.transpose(0, 1, 3, 2, 4).reshape(B, n_cmp, G, CMP_BLOCK * dh)
    hdn = jax.nn.gelu(blk @ w1 + b1)
    return hdn @ w2 + b2

def nsa_mixer(q, k_c, v_c, k_s, v_s, k_w, v_w, gate_logits, positions,
              cmp_pos, cmp_w1, cmp_b1, cmp_w2, cmp_b2):
    B, T = q.shape[:2]
    G, Hg, dh = NSA_KV_GROUPS, HEADS_PER_GROUP, HEAD_DIM
    scale = dh ** -0.5
    t_idx = jnp.arange(T)
    kvr = lambda t: t.reshape(B, T, G, dh)
    k_c, v_c, k_s, v_s, k_w, v_w = map(kvr, (k_c, v_c, k_s, v_s, k_w, v_w))

    qg = q.reshape(B, T, G, Hg, dh)
    kc = compress_tokens(k_c, cmp_pos[0], cmp_w1[0], cmp_b1[0], cmp_w2[0], cmp_b2[0])
    vc = compress_tokens(v_c, cmp_pos[1], cmp_w1[1], cmp_b1[1], cmp_w2[1], cmp_b2[1])
    n_cmp = kc.shape[1]
    c_start = jnp.arange(n_cmp) * CMP_STRIDE
    s_c = jnp.einsum('btghd,bcgd->bghtc', qg, kc) * scale
    p_c = masked_softmax(s_c, (c_start + CMP_BLOCK - 1)[None, :] <= t_idx[:, None])
    o_cmp = jnp.einsum('bghtc,bcgd->btghd', p_c.astype(vc.dtype), vc)

    n_blk = T // SEL_BLOCK
    s_start = jnp.arange(n_blk) * SEL_BLOCK
    overlap = ((c_start[:, None] <= s_start[None, :] + SEL_BLOCK - 1)
               & (c_start[:, None] + CMP_BLOCK - 1 >= s_start[None, :])).astype(jnp.float32)
    imp = jnp.einsum('bghtc,cs->bgts', p_c, overlap)
    cur = t_idx // SEL_BLOCK
    blk = jnp.arange(n_blk)
    valid = blk[None, :] <= cur[:, None]
    dist = cur[:, None] - blk[None, :]
    forced = (blk[None, :] == 0) | ((dist >= 0) & (dist < N_LOCAL_SEL))
    imp = jnp.where(forced, FORCED_SCORE, jnp.where(valid, imp, -1.0))
    n_sel = min(N_SELECT, n_blk)
    _, sel_idx = lax.top_k(imp, n_sel)

    q_r = partial_rope(q.reshape(B, T, NSA_HEADS, dh), positions).reshape(B, T, G, Hg, dh)
    k_s = partial_rope(k_s, positions)
    k_w = partial_rope(k_w, positions)

    k_blocks = k_s.reshape(B, n_blk, SEL_BLOCK, G, dh).transpose(0, 3, 1, 2, 4)
    v_blocks = v_s.reshape(B, n_blk, SEL_BLOCK, G, dh).transpose(0, 3, 1, 2, 4)
    b_ix = jnp.arange(B)[:, None, None, None]
    g_ix = jnp.arange(G)[None, :, None, None]
    n_keys_sel = n_sel * SEL_BLOCK

    def sel_chunk(ci):
        s0 = ci * SEL_Q_CHUNK
        qc = lax.dynamic_slice_in_dim(q_r, s0, SEL_Q_CHUNK, axis=1)
        ic = lax.dynamic_slice_in_dim(sel_idx, s0, SEL_Q_CHUNK, axis=2)
        kg = k_blocks[b_ix, g_ix, ic].reshape(B, G, SEL_Q_CHUNK, n_keys_sel, dh)
        vg = v_blocks[b_ix, g_ix, ic].reshape(B, G, SEL_Q_CHUNK, n_keys_sel, dh)
        kpos = (ic[..., None] * SEL_BLOCK + jnp.arange(SEL_BLOCK)).reshape(B, G, SEL_Q_CHUNK, n_keys_sel)
        qpos = s0 + jnp.arange(SEL_Q_CHUNK)
        s = jnp.einsum('bqghd,bgqkd->bghqk', qc, kg) * scale
        p = masked_softmax(s, (kpos <= qpos[None, None, :, None])[:, :, None])
        return jnp.einsum('bghqk,bgqkd->bqghd', p.astype(vg.dtype), vg)

    o_slc = lax.map(sel_chunk, jnp.arange(T // SEL_Q_CHUNK))
    o_slc = jnp.moveaxis(o_slc, 0, 1).reshape(B, T, G, Hg, dh)

    k_pad = jnp.pad(k_w, ((0, 0), (WINDOW, 0), (0, 0), (0, 0)))
    v_pad = jnp.pad(v_w, ((0, 0), (WINDOW, 0), (0, 0), (0, 0)))
    band = WINDOW + WIN_Q_BLOCK

    def win_block(bi):
        s0 = bi * WIN_Q_BLOCK
        qb = lax.dynamic_slice_in_dim(q_r, s0, WIN_Q_BLOCK, axis=1)
        kb = lax.dynamic_slice_in_dim(k_pad, s0, band, axis=1)
        vb = lax.dynamic_slice_in_dim(v_pad, s0, band, axis=1)
        kpos = s0 - WINDOW + jnp.arange(band)
        qpos = s0 + jnp.arange(WIN_Q_BLOCK)
        mask = ((kpos[None, :] <= qpos[:, None]) & (kpos[None, :] > qpos[:, None] - WINDOW)
                & (kpos[None, :] >= 0))
        s = jnp.einsum('bqghd,bkgd->bghqk', qb, kb) * scale
        p = masked_softmax(s, mask)
        return jnp.einsum('bghqk,bkgd->bqghd', p.astype(vb.dtype), vb)

    o_win = lax.map(win_block, jnp.arange(T // WIN_Q_BLOCK))
    o_win = jnp.moveaxis(o_win, 0, 1).reshape(B, T, G, Hg, dh)

    g = jax.nn.sigmoid(gate_logits).reshape(B, T, G, Hg, 3)
    out = g[..., 0:1] * o_cmp + g[..., 1:2] * o_slc + g[..., 2:3] * o_win
    return out.reshape(B, T, NSA_WIDTH)

def memory_attention(hn, mem_n, w_q, w_k, w_v, w_o):
    B, T, D = hn.shape
    M = mem_n.shape[1]
    q = (hn @ w_q).reshape(B, T, MEM_HEADS, MEM_HEAD_DIM)
    k = (mem_n @ w_k).reshape(B, M, MEM_HEADS, MEM_HEAD_DIM)
    v = (mem_n @ w_v).reshape(B, M, MEM_HEADS, MEM_HEAD_DIM)
    s = jnp.einsum('bthd,bmhd->bhtm', q, k).astype(jnp.float32) * (MEM_HEAD_DIM ** -0.5)
    p = jax.nn.softmax(s, axis=-1).astype(v.dtype)
    o = jnp.einsum('bhtm,bmhd->bthd', p, v).reshape(B, T, D)
    return o @ w_o

def peer(hn, w_q, sub_keys, u_emb, v_emb):
    B, T, D = hn.shape
    q = (hn @ w_q).reshape(B, T, PEER_HEADS, 2, PEER_HALF)
    s = jnp.einsum('bthpd,hpkd->bthpk', q, sub_keys).astype(jnp.float32)
    s_top, i_top = lax.top_k(s, PEER_TOPK)
    cand = s_top[..., 0, :, None] + s_top[..., 1, None, :]
    cand_idx = i_top[..., 0, :, None] * PEER_KEYS + i_top[..., 1, None, :]
    n_cand = PEER_TOPK * PEER_TOPK
    best, pos = lax.top_k(cand.reshape(B, T, PEER_HEADS, n_cand), PEER_TOPK)
    experts = jnp.take_along_axis(cand_idx.reshape(B, T, PEER_HEADS, n_cand), pos, axis=-1)
    gates = jax.nn.softmax(best, axis=-1).astype(hn.dtype)
    n_tok = B * T
    n_ret = PEER_HEADS * PEER_TOPK
    xs = hn.reshape(n_tok // PEER_TOKEN_CHUNK, PEER_TOKEN_CHUNK, D)
    es = experts.reshape(n_tok // PEER_TOKEN_CHUNK, PEER_TOKEN_CHUNK, n_ret)
    gs = gates.reshape(n_tok // PEER_TOKEN_CHUNK, PEER_TOKEN_CHUNK, n_ret)

    def chunk(args):
        xc, ec, gc = args
        u = u_emb[ec]
        a = jax.nn.gelu(jnp.einsum('nd,nkd->nk', xc, u))
        return jnp.einsum('nk,nkd->nd', gc * a, v_emb[ec])

    y = lax.map(chunk, (xs, es, gs))
    return y.reshape(B, T, D)

def second_inputs(seed: int = 0) -> dict:
    key = jax.random.key(seed)
    ks = jax.random.split(key, 32)
    L, D = DEPTH, D_MODEL
    nrm = lambda k, shape, sc: jax.random.normal(k, shape, jnp.float32) * sc
    gain = lambda k, shape: 1.0 + 0.02 * jax.random.normal(k, shape, jnp.float32)
    return {
        "x": nrm(ks[0], (BATCH, SEQ, D), 1.0),
        "mem": nrm(ks[1], (BATCH, MEM_LEN, D), 1.0),
        "positions": jnp.broadcast_to(jnp.arange(SEQ, dtype=jnp.int32), (BATCH, SEQ)),
        "mix_norm_g": gain(ks[2], (L, D)),
        "w_in": nrm(ks[3], (L, D, IN_COLS), D ** -0.5),
        "conv_dw_w": nrm(ks[4], (L, CONV_KERNEL, CONV_WIDTH), CONV_KERNEL ** -0.5),
        "conv_dw_b": nrm(ks[5], (L, CONV_WIDTH), 0.02),
        "conv_ln_g": gain(ks[6], (L, CONV_WIDTH)),
        "conv_ln_b": nrm(ks[7], (L, CONV_WIDTH), 0.02),
        "cmp_pos": nrm(ks[8], (L, 2, CMP_BLOCK, HEAD_DIM), 0.02),
        "cmp_w1": nrm(ks[9], (L, 2, CMP_BLOCK * HEAD_DIM, CMP_HIDDEN), (CMP_BLOCK * HEAD_DIM) ** -0.5),
        "cmp_b1": nrm(ks[10], (L, 2, CMP_HIDDEN), 0.02),
        "cmp_w2": nrm(ks[11], (L, 2, CMP_HIDDEN, HEAD_DIM), CMP_HIDDEN ** -0.5),
        "cmp_b2": nrm(ks[12], (L, 2, HEAD_DIM), 0.02),
        "w_out": nrm(ks[13], (L, MIX_WIDTH, D), MIX_WIDTH ** -0.5),
        "mem_q_norm_g": gain(ks[14], (L, D)),
        "mem_kv_norm_g": gain(ks[15], (L, D)),
        "w_mem_q": nrm(ks[16], (L, D, D), D ** -0.5),
        "w_mem_k": nrm(ks[17], (L, D, D), D ** -0.5),
        "w_mem_v": nrm(ks[18], (L, D, D), D ** -0.5),
        "w_mem_o": nrm(ks[19], (L, D, D), D ** -0.5),
        "peer_norm_g": gain(ks[20], (L, D)),
        "peer_w_q": nrm(ks[21], (L, D, PEER_HEADS * PEER_QDIM), D ** -0.5),
        "peer_sub_keys": nrm(ks[22], (L, PEER_HEADS, 2, PEER_KEYS, PEER_HALF), PEER_HALF ** -0.5),
        "peer_u": nrm(ks[23], (L, PEER_EXPERTS, D), D ** -0.5),
        "peer_v": nrm(ks[24], (L, PEER_EXPERTS, D), D ** -0.5),
        "final_norm_g": gain(ks[25], (D,)),
    }

def second_block(x, mem, positions, mix_norm_g, w_in, conv_dw_w, conv_dw_b, conv_ln_g, conv_ln_b,
              cmp_pos, cmp_w1, cmp_b1, cmp_w2, cmp_b2, w_out,
              mem_q_norm_g, mem_kv_norm_g, w_mem_q, w_mem_k, w_mem_v, w_mem_o,
              peer_norm_g, peer_w_q, peer_sub_keys, peer_u, peer_v, final_norm_g):
    h = x
    for l in range(DEPTH):
        hn = rmsnorm_2(h, mix_norm_g[l])
        proj = hn @ w_in[l]
        conv_a, conv_b, q, k_c, v_c, k_s, v_s, k_w, v_w, gate_logits = jnp.split(proj, IN_SPLITS, axis=-1)
        y_conv = conformer_conv(conv_a, conv_b, conv_dw_w[l], conv_dw_b[l], conv_ln_g[l], conv_ln_b[l])
        y_nsa = nsa_mixer(q, k_c, v_c, k_s, v_s, k_w, v_w, gate_logits, positions,
                          cmp_pos[l], cmp_w1[l], cmp_b1[l], cmp_w2[l], cmp_b2[l])
        h = h + jnp.concatenate([y_conv, y_nsa], axis=-1) @ w_out[l]
        h = h + memory_attention(rmsnorm_2(h, mem_q_norm_g[l]), rmsnorm_2(mem, mem_kv_norm_g[l]),
                                 w_mem_q[l], w_mem_k[l], w_mem_v[l], w_mem_o[l])
        h = h + peer(rmsnorm_2(h, peer_norm_g[l]), peer_w_q[l], peer_sub_keys[l], peer_u[l], peer_v[l])
    return rmsnorm_2(h, final_norm_g)


def setup_inputs(seed=0):
    out = dict(first_inputs(seed))
    for name, value in second_inputs(seed + 1).items():
        if name != "x":
            out[name + "_2"] = value
    return out


def reference(
    x, p, w_in, w_out, norm_mix_g, norm_ffn_g, norm_ple_g, final_norm_g, hgrn_lower_bounds,
    hgrn_gnorm_g, rwkv_mu, rwkv_w0, rwkv_w2, rwkv_a0, rwkv_a2, rwkv_g2, rwkv_k_k, rwkv_k_a,
    rwkv_r_k, rwkv_ln_w, rwkv_ln_b, rwkv_v0, rwkv_v1, rwkv_v2, ffn_up, ffn_conv_w, ffn_conv_b,
    ffn_down, ple_proj, ple_gate, mem_2, positions_2, mix_norm_g_2, w_in_2, conv_dw_w_2,
    conv_dw_b_2, conv_ln_g_2, conv_ln_b_2, cmp_pos_2, cmp_w1_2, cmp_b1_2, cmp_w2_2, cmp_b2_2,
    w_out_2, mem_q_norm_g_2, mem_kv_norm_g_2, w_mem_q_2, w_mem_k_2, w_mem_v_2, w_mem_o_2,
    peer_norm_g_2, peer_w_q_2, peer_sub_keys_2, peer_u_2, peer_v_2, final_norm_g_2,
):
    x = first_block(
        x, p, w_in, w_out, norm_mix_g, norm_ffn_g, norm_ple_g, final_norm_g, hgrn_lower_bounds,
        hgrn_gnorm_g, rwkv_mu, rwkv_w0, rwkv_w2, rwkv_a0, rwkv_a2, rwkv_g2, rwkv_k_k, rwkv_k_a,
        rwkv_r_k, rwkv_ln_w, rwkv_ln_b, rwkv_v0, rwkv_v1, rwkv_v2, ffn_up, ffn_conv_w,
        ffn_conv_b, ffn_down, ple_proj, ple_gate,
    )
    return second_block(
        x, mem_2, positions_2, mix_norm_g_2, w_in_2, conv_dw_w_2, conv_dw_b_2, conv_ln_g_2,
        conv_ln_b_2, cmp_pos_2, cmp_w1_2, cmp_b1_2, cmp_w2_2, cmp_b2_2, w_out_2, mem_q_norm_g_2,
        mem_kv_norm_g_2, w_mem_q_2, w_mem_k_2, w_mem_v_2, w_mem_o_2, peer_norm_g_2, peer_w_q_2,
        peer_sub_keys_2, peer_u_2, peer_v_2, final_norm_g_2,
    )


_drawn_inputs = setup_inputs


def setup_inputs(seed=0):
    import zlib

    import numpy as np

    out = dict(_drawn_inputs(seed))
    spreads = {}
    factors = {'norm_mix_g': 3.71,
     'norm_ffn_g': 4.109,
     'norm_ple_g': 8.0,
     'final_norm_g': 2.787,
     'hgrn_gnorm_g': 7.196,
     'rwkv_w2': 8.0,
     'rwkv_a0': 4.623,
     'rwkv_a2': 5.119,
     'rwkv_k_k': 6.656,
     'rwkv_k_a': 4.307,
     'rwkv_ln_w': 8.0,
     'rwkv_ln_b': 8.0,
     'ffn_conv_b': 4.439,
     'mix_norm_g_2': 5.917,
     'conv_dw_b_2': 3.35,
     'conv_ln_g_2': 6.249,
     'conv_ln_b_2': 7.512,
     'cmp_pos_2': 8.0,
     'cmp_b1_2': 8.0,
     'cmp_b2_2': 8.0,
     'mem_q_norm_g_2': 8.0,
     'mem_kv_norm_g_2': 8.0,
     'peer_norm_g_2': 8.0,
     'peer_w_q_2': 4.173,
     'peer_sub_keys_2': 4.145,
     'peer_u_2': 4.582,
     'peer_v_2': 4.157,
     'final_norm_g_2': 2.823}
    for name, (base, spread) in spreads.items():
        noise = np.random.default_rng([zlib.crc32(name.encode()), seed]).standard_normal(out[name].shape)
        drawn = base * np.exp(spread * noise) if base else spread * noise
        out[name] = jnp.asarray(drawn.astype(out[name].dtype))
    for name, factor in factors.items():
        out[name] = (out[name] * factor).astype(out[name].dtype)
    return out
```

```python
import concourse.bass as bass
import numpy as np
from concourse import mybir
from contextlib import ExitStack

F32 = mybir.dt.float32
I32 = mybir.dt.int32
U32 = mybir.dt.uint32
ALU = mybir.AluOpType
ACT = mybir.ActivationFunctionType
AX = mybir.AxisListType

P = 128
T = 256
TT = T // P
D = 1024
KD = D // P
CW = 512
CHUNK = KD * CW
EPS = 1e-6
NEG = -1e30
HG_H, HG_K, HG_C = 4, 128, 64
RK_H, RK_N, RK_C = 4, 64, 64
RK_GN_EPS = 64e-5
RK_DECAY_SCALE = float(np.exp(-0.5))
SW_H, SW_D = 4, 64
SW_PATTERNS = ((128, 1), (512, 4), (2048, 16))
D_FF = 2816
NF = D_FF // P
CONV_K, CONV_T = 31, 4
NSA_H, NSA_G, NSA_D = 8, 2, 64
CMP_B, CMP_S = 32, 16
N_CMP = (T - CMP_B) // CMP_S + 1
ROPE_HALF = 8
ROPE_THETA = 500000.0
MEM_H = 4
PEER_H, PEER_K, PEER_TOP = 8, 128, 16
N_RET = PEER_H * PEER_TOP
LEVELS = 6

STREAM = {}
_at = 0
for _name, _count in (("w_in feature", 5), ("w_in token", 3), ("w_out", 2), ("ffn_up", 11), ("ffn_down", 6),
                      ("ple_gate", 2), ("ple_proj", 1), ("w_in_2 feature", 2), ("w_in_2 token", 3),
                      ("cmp_w1", 1), ("w_out_2", 2), ("mem_q", 2), ("mem_k", 2), ("mem_v", 2), ("mem_o", 2),
                      ("peer_q", 4), ("peer_keys", 1), ("peer", 65)):
    STREAM[_name] = (_at, _count)
    _at += _count
N_CHUNKS = _at


def columns_plan():
    plan, at = {}, 0
    for name, n in (("norm_mix_g", 8), ("norm_ffn_g", 8), ("norm_ple_g", 8), ("rwkv_mu", 8), ("rwkv_w0", 2),
                    ("rwkv_a0", 2), ("rwkv_k_k", 2), ("rwkv_k_a", 2), ("rwkv_r_k", 2),
                    ("ffn_conv", 4 * 2 * NF), ("mix_norm_g_2", 8), ("conv_dw_w_2", CONV_K * CONV_T),
                    ("conv_dw_b_2", CONV_T), ("conv_ln_g_2", CONV_T), ("conv_ln_b_2", CONV_T), ("cmp_b1_2", 2),
                    ("cmp_b2_2", 1), ("cmp_pos_2", 32), ("mem_q_norm_g_2", 8), ("mem_kv_norm_g_2", 8),
                    ("peer_norm_g_2", 8), ("eps", 1), ("gn_eps", 1), ("one", 1)):
        plan[name] = (at, n)
        at += n
    return plan, at


COLS, N_COLS = columns_plan()
ROWS_1 = {"hgrn_gnorm_g": (0, 512), "rwkv_ln_w": (512, 256), "rwkv_ln_b": (768, 256), "final_norm_g": (1024, 1024)}
ROWS_2 = {"cmp_b2_v": (0, 64), "final_norm_g_2": (1024, 1024)}


def shape_constants():
    i = np.arange(P)
    token = np.arange(T)
    always = [np.eye(P), np.broadcast_to(i, (P, P))]
    first = []
    for level in range(LEVELS):
        b = 2 << level
        left, right = i % b < b // 2, i % b >= b // 2
        first.append((i[:, None] // b == i[None] // b) & left[:, None] & right[None])
    first.append(np.eye(P))
    same = i[:, None] // RK_C == i[None] // RK_C
    first.append(same & (i[:, None] < i[None]))
    first.append(same & (i[:, None] <= i[None]))
    first.append(i[:, None] // RK_N == i[None] // RK_N)
    first.append(np.broadcast_to(np.arange(D) % HG_C != 0, (P, D)))
    q, k = token[:, None], token[None]
    held = np.zeros((T, T))
    for window, dil in SW_PATTERNS:
        held += (k <= q) & ((q - k) % dil == 0) & ((q - k) // dil <= window // dil)
    rows = lambda a: a.reshape(TT, P, -1).transpose(1, 0, 2).reshape(P, -1)
    first += [rows(held), rows(np.where(held > 0, 0.0, NEG))]
    first.append(np.stack([i < RK_N, i >= RK_N], 1))
    c = np.arange(16)
    seen = (c[None] * CMP_S + CMP_B - 1 <= token[:, None]) & (c[None] < N_CMP)
    second = [rows(np.where(k <= q, 0.0, NEG)), rows(seen * 1.0), rows(np.where(seen, 0.0, NEG))]
    inv = np.float32(ROPE_THETA) ** -(np.arange(ROPE_HALF, dtype=np.float32) * 2.0 / (2 * ROPE_HALF))
    second.append(np.broadcast_to(inv, (P, ROPE_HALF)))
    join = lambda parts: np.ascontiguousarray(np.concatenate([np.asarray(a, np.float32) for a in parts], 1))
    return join(always), join(first), join(second)


CONSTS = shape_constants()


class Lane:

    def __init__(self, sem, chained):
        self.sem, self.chained, self.n, self.steps, self.known = sem, chained, 0, [], {}

    def now(self):
        return (self.sem, self.n)

    def wait(self, *needs):
        for need in needs:
            if need is None or need[1] <= 0:
                continue
            sem, value = need
            if self.known.get(id(sem), 0) < value:
                self.known[id(sem)] = value
                self.steps.append(lambda e, sem=sem, value=value: e.wait_ge(sem, value))

    def do(self, f, *needs, own=None):
        self.wait(*needs)
        if self.chained if own is None else own:
            self.wait(self.now())
        self.n += 1
        self.steps.append(lambda e: f(e).then_inc(self.sem, 1))
        return self.now()

    def quiet(self, f, *needs):
        self.wait(*needs)
        self.steps.append(f)

    def emit(self, e):
        for step in self.steps:
            step(e)


class Banks:

    def __init__(self, tensor):
        self.tensor, self.free, self.turn = tensor, [()] * 4, 0

    def take(self, n=1):
        if n == 2 and self.turn % 2:
            self.turn += 1
        at = self.turn % 4
        self.turn += n
        needs = [x for b in range(at, at + n) for x in self.free[b]]
        return at, self.tensor[:, at:at + n, :].rearrange("p b n -> p (b n)"), needs

    def release(self, at, n, *tokens):
        for b in range(at, at + n):
            self.free[b] = tokens


def build(nc, stream, cols, rows, consts0, consts1, consts2, x, mem, positions, small_w, cmp_w2, out):
    ctx = ExitStack()
    with ctx:
        def sb(name, shape, dt=F32):
            return ctx.enter_context(nc.sbuf_tensor(name, shape, dt))

        def sem(name):
            return ctx.enter_context(nc.semaphore(name))

        ring = [sb(f"ring{i}", [P, CHUNK]) for i in range(2)]
        arena = sb("arena", [P, P * T])
        h = sb("h", [P, TT, D])
        xn = sb("xn", [P, TT, D])
        xT = sb("xT", [P, KD, T])
        col = sb("col", [P, N_COLS])
        row = sb("row", [P, 2048])
        ident_iota = sb("ident_iota", [P, 2 * P])
        smallw = sb("smallw", [P, 2 * 256])
        cmpw2 = sb("cmpw2", [P, 2 * NSA_D])
        picks = sb("picks", [P, 3, T])
        ss = sb("ss", [P, 8])
        ident, iota = ident_iota[:, 0:P], ident_iota[:, P:2 * P]
        ps_chunk = [ctx.enter_context(nc.psum_tensor(f"ps_chunk{i}", [P, 1024], F32)) for i in range(2)]
        ps_misc = ctx.enter_context(nc.psum_tensor("ps_misc", [P, 4, 512], F32))
        banks = Banks(ps_misc)

        s_w = [sem("s_w0"), sem("s_w1")]
        s_mm = sem("s_mm")
        s_ev = sem("s_ev")
        s_out = sem("s_out")
        pe = Lane(sem("s_pe"), False)
        dve = Lane(sem("s_dve"), True)
        act = Lane(sem("s_act"), True)
        pool = Lane(sem("s_pool"), True)
        sp = Lane(sem("s_sp"), False)
        work = (pe, dve, act, pool)

        def c(name, i=0, n=1):
            return col[:, COLS[name][0] + i:COLS[name][0] + i + n]

        def r(plan, name):
            at, n = plan[name]
            return row[:, at:at + n]

        used = [0]

        def cut(*shape):
            n = int(np.prod(shape))
            at = used[0]
            used[0] += n
            assert used[0] <= P * T, used
            a = arena[:, at:at + n]
            if len(shape) == 2:
                a = a.rearrange("p (a b) -> p a b", b=shape[1])
            if len(shape) == 3:
                a = a.rearrange("p (a b c) -> p a b c", b=shape[1], c=shape[2])
            return a

        chunk_at = [0]

        def fence():
            totals = [lane.now() for lane in work] + [(s_mm, chunk_at[0]), (s_ev, chunk_at[0])]
            for lane in work + (sp,):
                lane.wait(*totals)
            for b in range(4):
                banks.free[b] = ()

        def mm(out, lhsT, rhs, start=True, stop=True):
            return lambda e: e.matmul(out, lhsT, rhs, start=start, stop=stop, skip_group_check=True)

        rows_at = [0]

        def rows_from(base):
            moved, rows_at[0] = base != rows_at[0], base
            return pe.now() if moved else None

        sent = {}

        def load(name, dst, src, *needs):
            if name not in sent:
                sent[name] = [sem("s_load_" + name), 0]
            group = sent[name]
            group[1] += 16
            act.quiet(lambda e: e.dma_start(dst, src).then_inc(group[0], 16), *needs)
            return tuple(group)

        load("first", h[:, :, :], x.rearrange("(t p) n -> p t n", p=P))
        load("first", ident_iota[:, :], consts0)
        load("first", col[:, :], cols)
        load("first", smallw[:, :], small_w)
        have_first = load("first", cmpw2[:, :], cmp_w2)
        have_rows = load("rows", row[:, :], rows[0:1, :].broadcast_to([P, 2048]))

        def feed(e):
            def put(slot, n):
                src = stream[n, :, :] if isinstance(n, int) else stream[bass.ds(n, 1), :, :].rearrange("a p n -> p (a n)")
                e.dma_start(ring[slot][:, :], src).then_inc(s_w[slot], 16)

            put(0, 0)
            put(1, 1)
            total = chunk_at[0]
            with e.Fori(1, total // 2) as i:
                for slot in range(2):
                    e.wait_ge(s_mm, i * 2 + (slot - 1))
                    put(slot, i * 2 + slot)
            if total % 2:
                e.wait_ge(s_mm, total - 2)
                put(0, total - 1)

        sp.steps.append(feed)

        def over_chunks(lane, first, count, body):
            def run(e):
                n, end = first, first + count
                while n < end and (n % 2 or n == 0):
                    for _ in range(2 if n == 0 else 1):
                        if n < end:
                            body(e, n % 2, n, n // 2)
                            n += 1
                pairs = (end - n) // 2
                if pairs > 1:
                    with e.Fori(0, pairs) as i:
                        for slot in range(2):
                            body(e, slot, i * 2 + (n + slot), i + n // 2)
                    n += 2 * pairs
                while n < end:
                    body(e, n % 2, n, n // 2)
                    n += 1
            lane.steps.append(run)

        def landed(e, slot, half):
            e.wait_ge(s_w[slot], half * 16 + 16)

        def room(e, n):
            if not isinstance(n, int) or n > 1:
                e.wait_ge(s_ev, n - 1)

        def project(name, src, token_major, *needs, tiles=KD):
            first, count = STREAM[name]
            chunk_at[0] = first + count
            pe.wait(*needs)

            def body(e, slot, n, half):
                landed(e, slot, half)
                room(e, n)
                w = ring[slot][:, :].rearrange("p (k n) -> p k n", k=tiles)
                for piece in range(TT if token_major else CW // P):
                    for k in range(tiles):
                        if token_major:
                            o, a, b = ps_chunk[slot][:, piece * CW:(piece + 1) * CW], src[:, k, piece * P:(piece + 1) * P], w[:, k, :]
                        else:
                            o, a, b = ps_chunk[slot][:, piece * T:(piece + 1) * T], w[:, k, piece * P:(piece + 1) * P], src[:, k, :]
                        last = e.matmul(o, a, b, start=k == 0, stop=k == tiles - 1)
                last.then_inc(s_mm, 1)

            over_chunks(pe, first, count, body)
            return first, count

        def evacuate(lane, n, f):
            lane.wait((s_mm, n + 1), (s_ev, n))
            lane.quiet(lambda e: f(e, ps_chunk[n % 2]).then_inc(s_ev, 1))
            return (s_ev, n + 1)

        def copy_out(lane, n, dst):
            if lane is act:
                return evacuate(lane, n, lambda e, ps: e.activation(dst, ps[:, :], ACT.Copy))
            return evacuate(lane, n, lambda e, ps: e.tensor_copy(dst, ps[:, :]))

        def rms_scale(src, *needs):
            for t in range(TT):
                act.do(lambda e, t=t: e.activation(xn[:, t, :], src[:, t, :], ACT.Square, accum_out=ss[:, t:t + 1]),
                       *needs)
            root = act.do(lambda e: e.activation(ss[:, 2:4], ss[:, 0:2], ACT.Sqrt, scale=1.0 / D, bias=c("eps")))
            dve.do(lambda e: e.reciprocal(ss[:, 4:6], ss[:, 2:4]), root)
            for t in range(TT):
                done = dve.do(lambda e, t=t: e.tensor_scalar(xn[:, t, :], src[:, t, :], ss[:, 4 + t:5 + t], None,
                                                             ALU.mult), *needs)
            return done

        def turn(srcs, needs, evac, rows_out=P, banks_n=1):
            at, ps, free = banks.take(banks_n)
            for i, s in enumerate(srcs):
                done = pe.do(lambda e, i=i, s=s: e.transpose(ps[0:rows_out, i * P:(i + 1) * P], s, ident),
                             *needs, *free)
            tokens = evac(ps[0:rows_out, 0:len(srcs) * P], done)
            banks.release(at, banks_n, *tokens)
            return tokens

        def feature_major(src, dst, gain, needs):
            tokens = []
            for b in range(KD // 2):
                def evac(ps, done, b=b):
                    for i in range(2):
                        k, piece = 2 * b + i, ps[:, i * T:(i + 1) * T]
                        if b % 2:
                            last = act.do(lambda e, k=k, piece=piece: e.activation(
                                dst[:, k, :], piece, ACT.Copy, scale=gain(k)), done, own=False)
                        else:
                            last = dve.do(lambda e, k=k, piece=piece: e.tensor_scalar(
                                dst[:, k, :], piece, gain(k), None, ALU.mult), done, own=False)
                    return (last,)
                pieces = [src[:, t, k * P:(k + 1) * P] for k in (2 * b, 2 * b + 1) for t in range(TT)]
                tokens += turn(pieces, needs, evac)
            return tokens

        def copy_evac(lane, dst):
            def evac(ps, done):
                if lane is act:
                    return (act.do(lambda e: e.activation(dst, ps, ACT.Copy), done),)
                return (dve.do(lambda e: e.tensor_copy(dst, ps), done),)
            return evac

        def softmax(products, heads, length, scale, add, mult, gate, weights, needs, stats):
            at, ps, free = banks.take(2)
            done = products(ps, list(needs) + list(free))
            s = ps[:, 0:heads * length].rearrange("p (h l) -> p h l", h=heads)
            if add is not None:
                read = dve.do(lambda e: e.scalar_tensor_tensor(
                    out=weights, in0=s, scalar=scale, in1=add.unsqueeze(1).broadcast_to([P, heads, length]),
                    op0=ALU.mult, op1=ALU.add), done)
            else:
                read = dve.do(lambda e: e.tensor_scalar(weights, s, scale, None, ALU.mult), done)
            banks.release(at, 2, read)
            top, den = stats[:, 0:heads], stats[:, heads:2 * heads]
            wide = lambda a: a.unsqueeze(2).broadcast_to([P, heads, length])
            dve.do(lambda e: e.tensor_reduce(top, weights, AX.X, ALU.max))
            v = dve.do(lambda e: e.tensor_tensor(weights, weights, wide(top), ALU.subtract))
            a = act.do(lambda e: e.activation(weights, weights, ACT.Exp), v)
            dve.wait(a)
            if mult is not None:
                dve.do(lambda e: e.tensor_tensor(weights, weights, mult.unsqueeze(1).broadcast_to([P, heads, length]),
                                                 ALU.mult))
            dve.do(lambda e: e.tensor_reduce(den, weights, AX.X, ALU.add))
            dve.do(lambda e: e.reciprocal(den, den))
            if gate is not None:
                dve.do(lambda e: e.tensor_tensor(den, den, gate, ALU.mult))
            return dve.do(lambda e: e.tensor_tensor(weights, weights, wide(den), ALU.mult))

        def add_projection(name, *needs):
            first, count = project(name, xT, True, *needs)
            for n in range(first, first + count):
                at = (n - first) * CW
                done = evacuate(dve, n, lambda e, ps, at=at: e.tensor_tensor(
                    h[:, :, at:at + CW], h[:, :, at:at + CW],
                    ps[:, :].rearrange("p (t n) -> p t n", t=TT), ALU.add))
            return done

        Z = cut(8, 1024)
        k1 = cut(consts1.shape[1])
        have_k1 = load("k1", k1, consts1)
        masks = k1[:, 0:10 * P].rearrange("p (m n) -> p m n", m=10)
        strict, inclusive, head_ones = masks[:, 7, :], masks[:, 8, :], masks[:, 9, :]
        restart = k1[:, 10 * P:10 * P + D]
        sw_held = k1[:, 10 * P + D:10 * P + D + 512].rearrange("p (t n) -> p t n", t=TT)
        sw_add = k1[:, 10 * P + D + 512:10 * P + D + 1024].rearrange("p (t n) -> p t n", t=TT)
        head_pick = k1[:, 10 * P + D + 1024:10 * P + D + 1026]
        mixed = xn

        dve.wait(have_first)
        act.wait(have_first)
        pe.wait(have_first)
        scaled = rms_scale(h)
        turned = feature_major(xn, xT, lambda k: c("norm_mix_g", k), [scaled])
        project("w_in feature", xT, False, *turned)
        project("w_in token", xT, True)
        z_at = {}
        for n in range(8):
            z_at[n] = copy_out(act, n, Z[:, n, :])
        fence()
        act.wait(have_rows, have_k1)
        dve.wait(have_rows, have_k1)
        pe.wait(have_k1)

        zc = Z[:, 0:2, :].rearrange("p c (k t) -> p (c k) t", t=T)
        zq, zf = Z[:, 2, :], Z[:, 3, :]
        zb = Z[:, 4, :].rearrange("p (k t) -> p k t", t=T)
        zi, zg = (Z[:, n, :].rearrange("p (t n) -> p t n", t=TT) for n in (5, 6))
        zv = Z[:, 7, :].rearrange("p (t n) -> p t n", t=TT)

        base = used[0]

        def hgrn():
            K, LF, B, E = cut(D), cut(D), cut(D), cut(D)
            QL, KL, QE = cut(D), cut(D), cut(D)
            S = cut(8, P)
            KT = cut(TT, 512)
            state = cut(HG_H, P)
            EL = cut(16)
            O = cut(TT, 512)
            by_head = lambda a: a.rearrange("p (h t) -> p h t", h=HG_H)
            act.do(lambda e: e.activation(K, zf, ACT.Sigmoid, scale=-1.0))
            act.do(lambda e: e.activation(zq, zq, ACT.Silu))
            g = act.do(lambda e: e.activation(Z[:, 6, :], Z[:, 6, :], ACT.Silu))
            act.do(lambda e: e.activation(LF, zf, ACT.Abs))
            act.do(lambda e: e.activation(LF, LF, ACT.Exp, scale=-1.0))
            a = act.do(lambda e: e.activation(LF, LF, ACT.Ln, bias=c("one")))
            dve.do(lambda e: e.scalar_tensor_tensor(out=LF, in0=zf, scalar=0.0, in1=LF, op0=ALU.min,
                                                    op1=ALU.subtract), a)
            dve.do(lambda e: e.tensor_tensor_scan(B, restart, LF, 0.0, ALU.mult, ALU.add))
            dve.do(lambda e: e.memset(S, 0.0))
            for level in range(-1, LEVELS):
                if level < 0:
                    q_l, k_l, mask, v = zq, K, masks[:, 6, :], dve.now()
                else:
                    b = 2 << level
                    view = lambda a, b=b: a.rearrange("p (m b) -> p m b", b=b)
                    mid = view(B)[:, :, b // 2 - 1:b // 2].broadcast_to([P, D // b, b])
                    v = dve.do(lambda e, view=view, mid=mid: e.tensor_tensor(view(E), view(B), mid, ALU.subtract),
                               act.now())
                    act.do(lambda e: e.activation(E, E, ACT.Abs), v)
                    a = act.do(lambda e: e.activation(E, E, ACT.Exp, scale=-1.0))
                    dve.do(lambda e: e.tensor_tensor(QL, zq, E, ALU.mult), a, pe.now())
                    v = dve.do(lambda e: e.tensor_tensor(KL, K, E, ALU.mult))
                    q_l, k_l, mask = QL, KL, masks[:, level, :]
                at, ps, free = banks.take(2)
                for i in range(8):
                    lo = i * P
                    done = pe.do(mm(ps[:, lo:lo + P], k_l[:, lo:lo + P], q_l[:, lo:lo + P]), v, act.now(), *free)
                v = dve.do(lambda e, ps=ps, mask=mask: e.copy_predicated(
                    S, mask.bitcast(U32).unsqueeze(1).broadcast_to([P, 8, P]),
                    ps.rearrange("p (a b) -> p a b", b=P)), done)
                banks.release(at, 2, v)
            a = act.do(lambda e: e.activation(E, B, ACT.Exp), dve.now())
            dve.do(lambda e: e.tensor_tensor(QE, zq, E, ALU.mult), a)
            view = lambda a: a.rearrange("p (m b) -> p m b", b=HG_C)
            last = view(B)[:, :, HG_C - 1:HG_C]
            v = dve.do(lambda e: e.tensor_tensor(view(E), last.broadcast_to([P, 16, HG_C]), view(B), ALU.subtract))
            act.do(lambda e: e.activation(E, E, ACT.Exp), v)
            a = act.do(lambda e: e.activation(EL.unsqueeze(2), last, ACT.Exp))
            v = dve.do(lambda e: e.tensor_tensor(KL, K, E, ALU.mult), a, pe.now())
            for t in range(TT):
                turn([KL[:, hd * T + t * P:hd * T + (t + 1) * P] for hd in range(HG_H)], [v],
                     copy_evac(act, KT[:, t, :]))
            for t in range(TT):
                at, ps, free = banks.take()
                for hd in range(HG_H):
                    done = pe.do(mm(ps[:, hd * P:(hd + 1) * P], S[:, 2 * hd + t, :], zi[:, t, hd * P:(hd + 1) * P]),
                                 dve.now(), *free)
                a = act.do(lambda e, ps=ps, t=t: e.activation(O[:, t, :], ps, ACT.Copy), done)
                banks.release(at, 1, a)
            dve.do(lambda e: e.memset(state, 0.0))
            for n in range(T // HG_C):
                t, lo = n // 2, HG_C * (n % 2)
                if n:
                    at, ps, free = banks.take()
                    for hd in range(HG_H):
                        done = pe.do(mm(ps[lo:lo + HG_C, hd * P:(hd + 1) * P],
                                        QE[:, hd * T + n * HG_C:hd * T + (n + 1) * HG_C], state[:, hd, :]),
                                     dve.now(), *free)
                    v = dve.do(lambda e, ps=ps, t=t, lo=lo: e.tensor_tensor(
                        O[lo:lo + HG_C, t, :], O[lo:lo + HG_C, t, :], ps[lo:lo + HG_C, :], ALU.add), done, act.now())
                    banks.release(at, 1, v)
                if n < T // HG_C - 1:
                    at, ps, free = banks.take()
                    for hd in range(HG_H):
                        done = pe.do(mm(ps[:, hd * P:(hd + 1) * P], KT[lo:lo + HG_C, t, hd * P:(hd + 1) * P],
                                        zi[lo:lo + HG_C, t, hd * P:(hd + 1) * P]), act.now(), *free)
                    for hd in range(HG_H):
                        at_l = hd * 4 + n
                        v = dve.do(lambda e, ps=ps, hd=hd, at_l=at_l: e.scalar_tensor_tensor(
                            out=state[:, hd, :], in0=state[:, hd, :], scalar=EL[:, at_l:at_l + 1],
                            in1=ps[:, hd * P:(hd + 1) * P], op0=ALU.mult, op1=ALU.add), done)
                    banks.release(at, 1, v)
            Of = O.rearrange("p t n -> p (t n)")
            O8 = Of.rearrange("p (a b) -> p a b", b=P)
            dve.do(lambda e: e.tensor_tensor(E, Of, Of, ALU.mult))
            v = dve.do(lambda e: e.tensor_reduce(EL[:, 0:8], E.rearrange("p (a b) -> p a b", b=P), AX.X, ALU.add))
            a = act.do(lambda e: e.activation(EL[:, 8:16], EL[:, 0:8], ACT.Sqrt, scale=1.0 / P, bias=c("eps")), v)
            dve.do(lambda e: e.reciprocal(EL[:, 0:8], EL[:, 8:16]), a)
            dve.do(lambda e: e.tensor_tensor(O8, O8, EL[:, 0:8].unsqueeze(2).broadcast_to([P, 8, P]), ALU.mult))
            dve.do(lambda e: e.tensor_tensor(
                zg, zg, r(ROWS_1, "hgrn_gnorm_g").unsqueeze(1).broadcast_to([P, TT, 512]), ALU.mult), g)
            dve.do(lambda e: e.tensor_tensor(mixed[:, :, 0:512], O, zg, ALU.mult))

        def windows():
            W = cut(4, T)
            PT = cut(TT, 512)
            stats = cut(8)
            for t in range(TT):
                length = (t + 1) * P

                def products(ps, needs, t=t, length=length):
                    for hd in (0, 2, 1, 3):
                        j, lo = hd // 2, SW_D * (hd % 2)
                        done = pe.do(mm(ps[:, hd * length:(hd + 1) * length], zb[lo:lo + SW_D, j, t * P:(t + 1) * P],
                                        zb[lo:lo + SW_D, 2 + j, 0:length]), *needs, rows_from(lo))
                    return done

                w = W[:, :, 0:length]
                v = softmax(products, SW_H, length, SW_D ** -0.5, sw_add[:, t, 0:length], sw_held[:, t, 0:length],
                            None, w, [pe.now()], stats)
                for k in range(t + 1):
                    turn([w[:, hd, k * P:(k + 1) * P] for hd in range(SW_H)], [v], copy_evac(act, PT[:, k, :]))
                at, ps, free = banks.take()
                for hd in range(SW_H):
                    for k in range(t + 1):
                        done = pe.do(mm(ps[:, hd * SW_D:(hd + 1) * SW_D], PT[:, k, hd * P:(hd + 1) * P],
                                        zv[:, k, hd * SW_D:(hd + 1) * SW_D], k == 0, k == t), act.now(), *free)
                v = dve.do(lambda e, ps=ps, t=t: e.tensor_copy(mixed[:, t, 512:768], ps[:, 0:256]), done)
                banks.release(at, 1, v)

        def rwkv():
            CM = cut(8, T)
            two = lambda: cut(512)
            A, LW, B, KK, PX, AB, KB, R, K2, X1, X2, X3 = (two() for _ in range(12))
            VT, ABT, KBT, G, Y = (cut(TT, T) for _ in range(5))
            S0 = cut(2, RK_N)
            U, RH = cut(T), cut(T)
            EL, BS = cut(8), cut(8)
            MT, NT, RAT, RKT, MX, MXT, Y1, ML = (cut(8, P) for _ in range(8))
            flat = lambda a: a.rearrange("p a b -> p (a b)")
            place = lambda hd, t: (hd % 2) * 4 + (hd // 2) * 2 + t
            dve.do(lambda e: e.tensor_tensor(CM[:, :, 1:T], zc[:, :, 0:T - 1], zc[:, :, 1:T], ALU.subtract))
            dve.do(lambda e: e.tensor_scalar(CM[:, :, 0:1], zc[:, :, 0:1], -1.0, None, ALU.mult))
            for k in range(8):
                dve.do(lambda e, k=k: e.scalar_tensor_tensor(out=CM[:, k, :], in0=CM[:, k, :], scalar=c("rwkv_mu", k),
                                                             in1=zc[:, k, :], op0=ALU.mult, op1=ALU.add))
            cm_done = dve.now()
            rr, kk, vv = (CM[:, 2 * n:2 * n + 2, :] for n in range(3))
            rr, kk = flat(rr), flat(kk)
            th, sg = X1[:, 0:T], X1[:, T:2 * T]
            act.do(lambda e: e.activation(th[0:64, :], CM[0:64, 6, :], ACT.Tanh), cm_done)
            a = act.do(lambda e: e.activation(sg, CM[:, 7, :], ACT.Sigmoid))
            wa, g2 = smallw[:, 0:256], smallw[:, 256:512]
            at, ps, free = banks.take(2)
            for j in range(2):
                pe.do(mm(ps[:, j * T:(j + 1) * T], wa[0:64, j * P:(j + 1) * P], th[0:64, :]), a, *free)
            for j in range(2):
                done = pe.do(mm(ps[:, 512 + j * T:512 + (j + 1) * T], wa[64:128, j * P:(j + 1) * P], CM[64:128, 6, :]))
            for j in range(2):
                act.do(lambda e, j=j, ps=ps: e.activation(LW[:, j * T:(j + 1) * T], ps[:, j * T:(j + 1) * T], ACT.Sigmoid,
                                                   bias=c("rwkv_w0", j)), done)
                a = act.do(lambda e, j=j, ps=ps: e.activation(A[:, j * T:(j + 1) * T], ps[:, 512 + j * T:512 + (j + 1) * T],
                                                       ACT.Sigmoid, bias=c("rwkv_a0", j)))
            banks.release(at, 2, a)
            gate_at, gps, free = banks.take()
            for t in range(TT):
                gdone = pe.do(mm(gps[:, t * T:(t + 1) * T], sg[:, t * P:(t + 1) * P], g2), *free)
            g_tok = act.do(lambda e: e.activation(flat(G), gps, ACT.Copy), gdone)
            banks.release(gate_at, 1, g_tok)
            dve.do(lambda e: e.tensor_scalar(LW, LW, -RK_DECAY_SCALE, None, ALU.mult), a)
            dve.do(lambda e: e.tensor_tensor_scan(B, restart[:, 0:512], LW, 0.0, ALU.mult, ALU.add))
            for j in range(2):
                s = slice(j * T, (j + 1) * T)
                dve.do(lambda e, s=s, j=j: e.tensor_scalar(KK[:, s], kk[:, s], c("rwkv_k_k", j), None, ALU.mult))
            v = dve.do(lambda e: e.tensor_tensor(X2, KK, KK, ALU.mult))
            at, ps, free = banks.take()
            done = pe.do(mm(ps, head_ones, X2), v, *free)
            a = act.do(lambda e, ps=ps: e.activation(X2, ps, ACT.Sqrt), done)
            banks.release(at, 1, a)
            dve.do(lambda e: e.tensor_scalar(X2, X2, 1e-12, None, ALU.max), a)
            dve.do(lambda e: e.reciprocal(X2, X2))
            dve.do(lambda e: e.tensor_tensor(KK, KK, X2, ALU.mult))
            for j in range(2):
                s = slice(j * T, (j + 1) * T)
                dve.do(lambda e, s=s, j=j: e.tensor_scalar(K2[:, s], A[:, s], 1.0, c("rwkv_k_a", j), ALU.subtract,
                                                           ALU.mult))
            dve.do(lambda e: e.scalar_tensor_tensor(out=K2, in0=K2, scalar=1.0, in1=kk, op0=ALU.add, op1=ALU.mult))
            v = dve.do(lambda e: e.tensor_tensor(X2, B, LW, ALU.subtract))
            act.do(lambda e: e.activation(X2, X2, ACT.Exp), v)
            act.do(lambda e: e.activation(X3, B, ACT.Exp))
            last = B.rearrange("p (m b) -> p m b", b=RK_C)[:, :, RK_C - 1:RK_C]
            act.do(lambda e: e.activation(EL.unsqueeze(2), last, ACT.Exp))
            a = act.do(lambda e: e.activation(X1, B, ACT.Exp, scale=-1.0), gdone)
            dve.do(lambda e: e.tensor_tensor(PX, KK, X2, ALU.mult), a)
            dve.do(lambda e: e.tensor_tensor(R, rr, X3, ALU.mult))
            dve.do(lambda e: e.tensor_tensor(KB, K2, X1, ALU.mult))
            dve.do(lambda e: e.tensor_tensor(AB, KK, A, ALU.mult))
            v = dve.do(lambda e: e.tensor_tensor(AB, AB, X1, ALU.mult))
            for src, dst in ((flat(vv), VT), (AB, ABT), (KB, KBT)):
                turn([src[:, j * T + t * P:j * T + (t + 1) * P] for t in range(TT) for j in range(2)], [v],
                     copy_evac(act, flat(dst)))
            turned = act.now()
            for j in range(2):
                s = slice(j * T, (j + 1) * T)
                dve.do(lambda e, s=s, j=j: e.scalar_tensor_tensor(out=X2[:, s], in0=rr[:, s], scalar=c("rwkv_r_k", j),
                                                                  in1=K2[:, s], op0=ALU.mult, op1=ALU.mult))
            v = dve.now()
            at, ps, free = banks.take()
            for t in range(TT):
                for j in range(2):
                    lo = t * 4 + 2 * j
                    done = pe.do(mm(ps[:, lo:lo + 2], X2[:, j * T + t * P:j * T + (t + 1) * P], head_pick), v, *free)
            v = dve.do(lambda e, ps=ps: e.tensor_copy(BS, ps[:, 0:8]), done)
            banks.release(at, 1, v)
            for dst, left, right, mask in ((MT, AB, PX, strict), (NT, KB, PX, strict), (RAT, AB, R, inclusive),
                                           (RKT, KB, R, inclusive)):
                at, ps, free = banks.take(2)
                for hd in range(RK_H):
                    j, lo = hd // 2, RK_N * (hd % 2)
                    for t in range(TT):
                        s = slice(j * T + t * P, j * T + (t + 1) * P)
                        i = place(hd, t)
                        done = pe.do(mm(ps[:, i * P:(i + 1) * P], left[lo:lo + RK_N, s], right[lo:lo + RK_N, s]), *free)
                v = dve.do(lambda e, ps=ps, dst=dst, mask=mask: e.tensor_tensor(
                    dst, ps.rearrange("p (a b) -> p a b", b=P), mask.unsqueeze(1).broadcast_to([P, 8, P]), ALU.mult),
                    done)
                banks.release(at, 2, v)
            eye8 = ident.unsqueeze(1).broadcast_to([P, 8, P])
            dve.do(lambda e: e.tensor_copy(MX, eye8))
            dve.do(lambda e: e.tensor_copy(MXT, eye8))
            for level in range(LEVELS):
                v = dve.do(lambda e, level=level: e.tensor_tensor(
                    ML, MT, masks[:, level, :].unsqueeze(1).broadcast_to([P, 8, P]), ALU.mult), pe.now())
                at, ps, free = banks.take(2)
                for i in range(8):
                    done = pe.do(mm(ps[:, i * P:(i + 1) * P], ML[:, i, :], MX[:, i, :]), v, *free)
                a = act.do(lambda e, ps=ps: e.activation(flat(Y1), ps, ACT.Copy), done)
                banks.release(at, 2, a)
                for dst, left, right in ((MX, MXT, Y1), (MXT, Y1, MXT)):
                    at, ps, free = banks.take(2)
                    for i in range(8):
                        done = pe.do(mm(ps[:, i * P:(i + 1) * P], left[:, i, :], right[:, i, :]), a, *free)
                    dst_done = (at, ps, dst, done)
                    if dst is MX:
                        first_half = dst_done
                for at, ps, dst, done in (first_half, dst_done):
                    v = dve.do(lambda e, ps=ps, dst=dst: e.tensor_tensor(flat(dst), flat(dst), ps, ALU.subtract),
                               dst_done[3])
                    banks.release(at, 2, v)
            dve.do(lambda e: e.memset(S0, 0.0))
            for n in range(T // RK_C):
                t, lo = n // 2, RK_C * (n % 2)
                tok = slice(lo, lo + RK_C)
                heads = [(hd, hd // 2, RK_N * (hd % 2)) for hd in (0, 2, 1, 3)]
                col_of = lambda j, n=n: slice(j * T + n * RK_C, j * T + (n + 1) * RK_C)
                vs = lambda hd: slice(hd * RK_N, (hd + 1) * RK_N)
                at, ps, free = banks.take()
                ready = dve.now()
                for hd, j, kb in heads:
                    done = pe.do(mm(ps[tok, vs(hd)], PX[kb:kb + RK_N, col_of(j)], S0[kb:kb + RK_N, j, :], hd == 0, False),
                                 ready, *free, rows_from(kb))
                for hd, j, kb in heads:
                    done = pe.do(mm(ps[tok, vs(hd)], NT[tok, place(hd, t), tok], VT[tok, t, vs(hd)], False, True), done,
                                 rows_from(lo))
                v = dve.do(lambda e, ps=ps, tok=tok: e.tensor_scalar(RH[tok, :], ps[tok, 0:T], -1.0, None, ALU.mult),
                           done)
                banks.release(at, 1, v)
                at, ps, free = banks.take()
                for hd, j, kb in heads:
                    done = pe.do(mm(ps[tok, vs(hd)], MXT[tok, place(hd, t), tok], RH[tok, vs(hd)]), v, *free, rows_from(lo))
                v = dve.do(lambda e, ps=ps, tok=tok: e.tensor_copy(U[tok, :], ps[tok, 0:T]), done)
                banks.release(at, 1, v)
                at, ps, free = banks.take()
                for hd, j, kb in heads:
                    done = pe.do(mm(ps[tok, vs(hd)], R[kb:kb + RK_N, col_of(j)], S0[kb:kb + RK_N, j, :], hd == 0, False),
                                 *free, rows_from(kb))
                for hd, j, kb in heads:
                    pe.do(mm(ps[tok, vs(hd)], RAT[tok, place(hd, t), tok], U[tok, vs(hd)], False, False), done, v, rows_from(lo))
                    ydone = pe.do(mm(ps[tok, vs(hd)], RKT[tok, place(hd, t), tok], VT[tok, t, vs(hd)], False, True))
                a = act.do(lambda e, ps=ps, tok=tok, t=t: e.activation(Y[tok, t, :], ps[tok, 0:T], ACT.Copy), ydone)
                banks.release(at, 1, a)
                if n < T // RK_C - 1:
                    at, ps, free = banks.take()
                    for hd, j, kb in heads:
                        o = ps[kb:kb + RK_N, j * RK_N:(j + 1) * RK_N]
                        pe.do(mm(o, ABT[tok, t, vs(hd)], U[tok, vs(hd)], True, False), *free)
                        done = pe.do(mm(o, KBT[tok, t, vs(hd)], VT[tok, t, vs(hd)], False, True))
                    dve.do(lambda e, ps=ps: e.tensor_tensor(flat(S0), flat(S0), ps[:, 0:P], ALU.add), done)
                    e_last = EL.rearrange("p (j n) -> p j n", j=2)[:, :, n:n + 1].broadcast_to([P, 2, RK_N])
                    v = dve.do(lambda e, e_last=e_last: e.tensor_tensor(S0, S0, e_last, ALU.mult))
                    banks.release(at, 1, v)
            Y8 = flat(Y).rearrange("p (a b) -> p a b", b=RK_N)
            wide = lambda a: a.unsqueeze(2).broadcast_to([P, 8, RK_N])
            m, sq = EL, X1.rearrange("p (a b) -> p a b", b=RK_N)
            dve.do(lambda e: e.tensor_reduce(m, Y8, AX.X, ALU.add), act.now())
            dve.do(lambda e: e.tensor_scalar(m, m, 1.0 / RK_N, None, ALU.mult))
            dve.do(lambda e: e.tensor_tensor(Y8, Y8, wide(m), ALU.subtract))
            dve.do(lambda e: e.tensor_tensor(sq, Y8, Y8, ALU.mult))
            v = dve.do(lambda e: e.tensor_reduce(m, sq, AX.X, ALU.add))
            a = act.do(lambda e: e.activation(m, m, ACT.Sqrt, scale=1.0 / RK_N, bias=c("gn_eps")), v)
            dve.do(lambda e: e.reciprocal(m, m), a)
            dve.do(lambda e: e.tensor_tensor(Y8, Y8, wide(m), ALU.mult))
            across = lambda name: r(ROWS_1, name).unsqueeze(1).broadcast_to([P, TT, T])
            dve.do(lambda e: e.tensor_tensor(Y, Y, across("rwkv_ln_w"), ALU.mult))
            dve.do(lambda e: e.tensor_tensor(Y, Y, across("rwkv_ln_b"), ALU.add))
            dve.do(lambda e: e.tensor_tensor(sq, flat(VT).rearrange("p (a b) -> p a b", b=RK_N), wide(BS), ALU.mult),
                   turned)
            dve.do(lambda e: e.tensor_tensor(Y8, Y8, sq, ALU.add))
            dve.do(lambda e: e.tensor_tensor(mixed[:, :, 768:1024], Y, G, ALU.mult), g_tok)

        hgrn()
        fence()
        used[0] = base
        windows()
        fence()
        used[0] = base
        rwkv()
        fence()

        plain = lambda k: c("one")

        sp_out = [0]

        t = feature_major(mixed, xT, plain, [dve.now()])
        summed = add_projection("w_out", *t)
        fence()

        def ffn():
            used[0] = 0
            GT = cut(NF, T)
            UC = cut(2, 4, T)
            scaled = rms_scale(h)
            t = feature_major(xn, xT, lambda k: c("norm_ffn_g", k), [scaled])
            first, count = project("ffn_up", xT, False, *t)
            tap0 = COLS["ffn_conv"][0]

            act_0, dve_0 = act.n, dve.n

            def conv_act(e, slot, n, half):
                i = n - first
                e.wait_ge(s_mm, n + 1)
                e.wait_ge(dve.sem, i * 9 + (dve_0 - 9))
                for piece in range(4):
                    at = i * 16 + (tap0 + 4 * piece)
                    e.activation(UC[:, slot, piece, :], ps_chunk[slot][:, piece * T:(piece + 1) * T], ACT.Identity,
                                 scale=col[:, bass.ds(at + 2, 1)], bias=col[:, bass.ds(at + 3, 1)]).then_inc(act.sem, 1)
                e.wait_ge(dve.sem, i * 9 + (dve_0 + 8))
                gates = UC[:, slot, 0:2, :]
                e.activation(gates, gates, ACT.Silu).then_inc(act.sem, 1)

            def conv_dve(e, slot, n, half):
                i = n - first
                for piece in range(4):
                    at = i * 16 + (tap0 + 4 * piece)
                    e.wait_ge(act.sem, i * 5 + (act_0 + (2 if piece < 2 else 4)))
                    for lag in (1, 2):
                        if lag == 2:
                            e.wait_ge(dve.sem, i * 9 + (dve_0 + 2 * piece + 1))
                        o = UC[:, slot, piece, lag:T]
                        e.scalar_tensor_tensor(out=o, in0=ps_chunk[slot][:, piece * T:(piece + 1) * T - lag],
                                               scalar=col[:, bass.ds(at + (2 - lag), 1)], in1=o, op0=ALU.mult,
                                               op1=ALU.add).then_inc(dve.sem, 1)
                e.wait_ge(dve.sem, i * 9 + (dve_0 + 8))
                e.wait_ge(act.sem, i * 5 + (act_0 + 5))
                gt = GT[:, bass.ds(i * 2, 2), :]
                e.tensor_tensor(gt, UC[:, slot, 0:2, :], UC[:, slot, 2:4, :], ALU.mult).then_inc(dve.sem, 1)
                e.wait_ge(dve.sem, i * 9 + (dve_0 + 9))
                e.sem_inc(s_ev, 1)

            over_chunks(act, first, count, conv_act)
            over_chunks(dve, first, count, conv_dve)
            act.n += 5 * count
            dve.n += 9 * count
            fence()
            ffn_down(GT)

        def ffn_down(GT):
            first, count = STREAM["ffn_down"]
            chunk_at[0] = first + count

            def down(e):
                for n in range(first, first + count):
                    slot = n % 2
                    landed(e, slot, n // 2)
                    for kk in range(4):
                        k = 4 * (n - first) + kk
                        if k >= NF:
                            continue
                        for t in range(TT):
                            for half in range(2):
                                last = e.matmul(ps_misc[:, 2 * t + half, :], GT[:, k, t * P:(t + 1) * P],
                                                ring[slot][:, kk * D + half * CW:kk * D + (half + 1) * CW],
                                                start=k == 0, stop=k == NF - 1)
                    last.then_inc(s_mm, 1)

            pe.steps.append(down)
            dve.wait((s_mm, first + count))
            dve.do(lambda e: e.tensor_tensor(h[:, :, :].rearrange("p t n -> p (t n)"),
                                             h[:, :, :].rearrange("p t n -> p (t n)"),
                                             ps_misc[:, :, :].rearrange("p b n -> p (b n)"), ALU.add))
            dve.quiet(lambda e: e.sem_inc(s_ev, count), dve.now())
            fence()
        ffn()
        def ple_and_norm():
            used[0] = 0
            gate = cut(TT, D)
            scaled = rms_scale(h)
            t = feature_major(xn, xT, lambda k: c("norm_ple_g", k), [scaled])
            first, count = project("ple_gate", xT, True, *t)
            for n in range(first, first + count):
                at = (n - first) * CW
                evacuate(act, n, lambda e, ps, at=at: e.activation(
                    gate[:, :, at:at + CW], ps[:, :].rearrange("p (t n) -> p t n", t=TT), ACT.Sigmoid))
            n = STREAM["ple_proj"][0]
            chunk_at[0] = n + 1
            w = ring[n % 2]

            def ple(e):
                landed(e, n % 2, n // 2)
                for t in range(TT):
                    for half in range(2):
                        for k in range(2):
                            last = e.matmul(ps_misc[:, 2 * t + half, :],
                                            w[:, 2 * D + k * T + t * P:2 * D + k * T + (t + 1) * P],
                                            w[:, k * D + half * CW:k * D + (half + 1) * CW], start=k == 0, stop=k == 1)
                last.then_inc(s_mm, 1)

            pe.wait(*[x for b in range(4) for x in banks.free[b]])
            pe.steps.append(ple)
            gf = gate.rearrange("p t n -> p (t n)")
            dve.wait((s_mm, n + 1), (s_ev, n))
            dve.do(lambda e: e.tensor_tensor(gf, gf, ps_misc[:, :, :].rearrange("p b n -> p (b n)"), ALU.mult))
            dve.quiet(lambda e: e.sem_inc(s_ev, 1), dve.now())
            hf = h[:, :, :].rearrange("p t n -> p (t n)")
            v = dve.do(lambda e: e.tensor_tensor(hf, hf, gf, ALU.add))
            rms_scale(h, v)
            dve.do(lambda e: e.tensor_tensor(h[:, :, :], xn[:, :, :], r(ROWS_1, "final_norm_g").unsqueeze(1)
                                             .broadcast_to([P, TT, D]), ALU.mult), have_rows)
            fence()
        ple_and_norm()
        def mixers_2():
            used[0] = 0
            Z2 = cut(5, 1024)
            k2 = cut(consts2.shape[1])
            pos_raw = cut(TT)
            load("second", k2, consts2)
            load("second", pos_raw.bitcast(I32), positions)
            have = load("second", row[:, :], rows[1:2, :].broadcast_to([P, 2048]))
            act.wait(have)
            dve.wait(have)
            causal = k2[:, 0:512].rearrange("p (t n) -> p t n", t=TT)
            seen = k2[:, 512:544].rearrange("p (t n) -> p t n", t=TT)
            seen_add = k2[:, 544:576].rearrange("p (t n) -> p t n", t=TT)
            inv = k2[:, 576:584]
            scaled = rms_scale(h)
            t = feature_major(xn, xT, lambda k: c("mix_norm_g_2", k), [scaled])
            project("w_in_2 feature", xT, False, *t)
            project("w_in_2 token", xT, True)
            first = STREAM["w_in_2 feature"][0]
            got = [copy_out(act, first + n, Z2[:, n, :]) for n in range(5)]
            convolved = conv_module(Z2, got)
            nsa(Z2, got, causal, seen, seen_add, inv, pos_raw)
            turned = []
            conv_norm(convolved)

        def conv_module(Z2, got):
            pad = CONV_K - 1
            U = cut(CONV_T, T + pad)
            Y = cut(CONV_T, T)
            tiles = lambda n: Z2[:, n, :].rearrange("p (k t) -> p k t", t=T)
            a = act.do(lambda e: e.activation(Z2[:, 1, :], Z2[:, 1, :], ACT.Sigmoid), got[1])
            dve.do(lambda e: e.memset(U[:, :, 0:pad], 0.0))
            dve.do(lambda e: e.tensor_tensor(U[:, :, pad:pad + T], tiles(0), tiles(1), ALU.mult), a, got[0])
            tap0 = COLS["conv_dw_w_2"][0]
            for k in range(CONV_T):
                dve.do(lambda e, k=k: e.tensor_scalar(Y[:, k, :], U[:, k, 0:T], col[:, tap0 + k:tap0 + k + 1],
                                                      c("conv_dw_b_2", k), ALU.mult, ALU.add))
            before = dve.n - CONV_T

            def taps(e):
                with e.Fori(1, CONV_K) as j:
                    for k in range(CONV_T):
                        e.wait_ge(dve.sem, j * CONV_T + (before - CONV_T + k + 1))
                        e.scalar_tensor_tensor(out=Y[:, k, :], in0=U[:, k, bass.ds(j, T)],
                                               scalar=col[:, bass.ds(j * CONV_T + (tap0 + k), 1)], in1=Y[:, k, :],
                                               op0=ALU.mult, op1=ALU.add).then_inc(dve.sem, 1)

            dve.steps.append(taps)
            dve.n += CONV_T * (CONV_K - 1)
            return Y, dve.now()

        def conv_norm(convolved):
            Y, ready = convolved
            YT, SQ = cut(TT, 512), cut(TT, 512)
            st = cut(8)
            for t in range(TT):
                turn([Y[:, k, t * P:(t + 1) * P] for k in range(CONV_T)], [ready], copy_evac(act, YT[:, t, :]))
            m, q = st[:, 0:2], st[:, 2:4]
            wide = lambda a: a.unsqueeze(2).broadcast_to([P, TT, 512])
            dve.do(lambda e: e.tensor_reduce(m, YT, AX.X, ALU.add), act.now())
            dve.do(lambda e: e.tensor_scalar(m, m, 1.0 / 512, None, ALU.mult))
            dve.do(lambda e: e.tensor_tensor(YT, YT, wide(m), ALU.subtract))
            dve.do(lambda e: e.tensor_tensor(SQ, YT, YT, ALU.mult))
            v = dve.do(lambda e: e.tensor_reduce(q, SQ, AX.X, ALU.add))
            a = act.do(lambda e: e.activation(q, q, ACT.Sqrt, scale=1.0 / 512, bias=c("eps")), v)
            dve.do(lambda e: e.reciprocal(q, q), a)
            v = dve.do(lambda e: e.tensor_tensor(YT, YT, wide(q), ALU.mult))
            for b in range(2):
                def evac(ps, done, b=b):
                    for i in range(2):
                        k = 2 * b + i
                        last = act.do(lambda e, k=k, i=i: e.activation(
                            xT[:, k, :], ps[:, i * T:(i + 1) * T], ACT.Silu, scale=c("conv_ln_g_2", k),
                            bias=c("conv_ln_b_2", k)), done, own=False)
                    return (last,)
                turn([YT[:, t, k * P:(k + 1) * P] for k in (2 * b, 2 * b + 1) for t in range(TT)], [v], evac)

        def nsa(Z2, got, causal, seen, seen_add, inv, pos_raw):
            zq = Z2[:, 2, :].rearrange("p (t h d) -> p t h d", t=TT, h=NSA_H)
            zkv = Z2[:, 3, :].rearrange("p (t n) -> p t n", t=TT)
            zw = Z2[:, 4, :].rearrange("p (t n) -> p t n", t=TT)
            rope_at = cut(TT)
            angle, CS, N1 = cut(TT, 8), cut(2, TT, 8), cut(TT, 8)
            QR = cut(1024)
            QU, QT = cut(NSA_H, T), cut(NSA_H, T)
            KST, KWT = cut(NSA_G, T), cut(NSA_G, T)
            GA = cut(TT, 24)
            W = [cut(4, T) for _ in range(2)]
            stats = [cut(16) for _ in range(2)]
            PT = cut(4, NSA_H * P)
            PC, PCT = cut(NSA_H, P), cut(NSA_H * P)
            VC = cut(NSA_G, NSA_D)
            NS = cut(TT, 512)
            R4 = cut(4, 128)
            for n in (2, 3, 4):
                dve.wait(got[n])
            dve.do(lambda e: e.tensor_copy(rope_at, pos_raw.bitcast(I32)))
            dve.do(lambda e: e.tensor_tensor(angle, rope_at.unsqueeze(2).broadcast_to([P, TT, 8]),
                                             inv.unsqueeze(1).broadcast_to([P, TT, 8]), ALU.mult))
            two_pi, high = 2 * np.pi, 6.28125
            magic = 1.5 * 2.0 ** 23
            for i, quarter in ((0, 0.25), (1, 0.0)):
                dve.do(lambda e, quarter=quarter: e.tensor_scalar(N1, angle, 1 / two_pi, quarter, ALU.mult, ALU.add))
                dve.do(lambda e: e.tensor_scalar(N1, N1, magic, None, ALU.add))
                dve.do(lambda e: e.tensor_scalar(N1, N1, -magic, None, ALU.add))
                dve.do(lambda e, i=i: e.scalar_tensor_tensor(out=CS[:, i, :, :], in0=N1, scalar=-high, in1=angle,
                                                             op0=ALU.mult, op1=ALU.add))
                dve.do(lambda e, i=i: e.scalar_tensor_tensor(out=CS[:, i, :, :], in0=N1, scalar=high - two_pi,
                                                             in1=CS[:, i, :, :], op0=ALU.mult, op1=ALU.add))
                dve.do(lambda e, i=i, quarter=quarter: e.tensor_scalar(CS[:, i, :, :], CS[:, i, :, :],
                                                                       quarter * two_pi, None, ALU.add))
            flat_cs = CS.rearrange("p i t d -> p (i t d)")
            v = dve.do(lambda e: e.tensor_scalar(flat_cs, flat_cs, 3.1415925, -3.1415925, ALU.min, ALU.max))
            cs_ready = act.do(lambda e: e.activation(flat_cs, flat_cs, ACT.Sin), v)
            gates_ready = act.do(lambda e: e.activation(GA, zw[:, :, 256:280], ACT.Sigmoid))

            def heads_turned(src, count, dst, needs):
                for hd in range(0, count, 2):
                    turn([src(hd + i, t) for i in range(2) for t in range(TT)], needs,
                         copy_evac(act, dst[0:64, hd:hd + 2, :].rearrange("p h t -> p (h t)")), rows_out=64)

            heads_turned(lambda hd, t: zq[:, t, hd, :], NSA_H, QU, [got[2]])

            def rope(x, count):
                r4 = [R4[:, i, 0:TT * count * 8].rearrange("p (t h d) -> p t h d", t=TT, h=count) for i in range(4)]
                x1, x2 = x[:, :, :, 0:8], x[:, :, :, 8:16]
                cos, sin = (CS[:, i, :, :].unsqueeze(2).broadcast_to([P, TT, count, 8]) for i in range(2))
                dve.wait(cs_ready)
                for o, a, b in ((r4[0], x1, cos), (r4[1], x2, sin), (r4[2], x2, cos), (r4[3], x1, sin)):
                    dve.do(lambda e, o=o, a=a, b=b: e.tensor_tensor(o, a, b, ALU.mult))
                dve.do(lambda e: e.tensor_tensor(x1, r4[0], r4[1], ALU.subtract))
                return dve.do(lambda e: e.tensor_tensor(x2, r4[2], r4[3], ALU.add))

            dve.do(lambda e: e.tensor_copy(QR, Z2[:, 2, :]))
            qr = QR.rearrange("p (t h d) -> p t h d", t=TT, h=NSA_H)
            group = lambda z, at: z[:, :, at:at + 128].rearrange("p t (g d) -> p t g d", g=NSA_G)
            v = rope(qr, NSA_H)
            heads_turned(lambda hd, t: qr[:, t, hd, :], NSA_H, QT, [v])
            ks, kw = group(zkv, 256), group(zw, 0)
            v = rope(ks, NSA_G)
            heads_turned(lambda g, t: ks[:, t, g, :], NSA_G, KST, [v])
            v = rope(kw, NSA_G)
            heads_turned(lambda g, t: kw[:, t, g, :], NSA_G, KWT, [v])

            KD2 = cut(TT, 4, 128)
            XK = cut(4, T)
            X = cut(2, 16, 30)
            HD, KCT = cut(60), cut(30)
            for copy in range(2):
                v = dve.do(lambda e, copy=copy: e.tensor_copy(
                    KD2[:, :, :, copy * 64:copy * 64 + 64], zkv[:, :, 0:256].rearrange("p t (m d) -> p t m d", d=64)))
            dve.do(lambda e: e.memset(VC, 0.0))
            dve.do(lambda e: e.memset(PC, 0.0))
            for m in (0, 2):
                def evac(ps, done, m=m):
                    ps = ps.rearrange("p (m t) -> p m t", t=T)
                    act.do(lambda e: e.activation(XK[0:64, m:m + 2, :], ps[0:64, :, :], ACT.Copy), done)
                    return (act.do(lambda e: e.activation(XK[64:128, m:m + 2, 0:T - 1], ps[64:128, :, 1:T], ACT.Copy)),)
                turn([KD2[:, t, i, :] for i in (m, m + 1) for t in range(TT)], [v], evac)
            for kv in range(2):
                for mh in range(2):
                    x_in = XK[:, 2 * kv:2 * kv + 2, 16 * mh:16 * mh + 240].rearrange(
                        "p g (c m two) -> p m g c two", c=N_CMP, two=2)[:, :, :, :, 0]
                    pos = c("cmp_pos_2", kv * 16 + mh * 8, 8).unsqueeze(2).unsqueeze(3).broadcast_to([P, 8, 2, N_CMP])
                    x_out = X[:, kv, mh * 8:mh * 8 + 8, :].rearrange("p m (g c) -> p m g c", g=2)
                    v = dve.do(lambda e, x_in=x_in, pos=pos, x_out=x_out: e.tensor_tensor(x_out, x_in, pos, ALU.add),
                               act.now())
            n = STREAM["cmp_w1"][0]
            chunk_at[0] = n + 1
            w1 = ring[n % 2][:, 0:4096].rearrange("p (v m n) -> p v m n", v=2, m=16)
            at, ps, free = banks.take()
            pe.wait((s_w[n % 2], 16 * (n // 2) + 16))
            for kv in range(2):
                for m in range(16):
                    done = pe.do(mm(ps[:, kv * 30:kv * 30 + 30], w1[:, kv, m, :], X[:, kv, m, :], m == 0, m == 15),
                                 v, *free)
            pe.quiet(lambda e: e.sem_inc(s_mm, 1), done)
            for kv in range(2):
                a = act.do(lambda e, kv=kv, ps=ps: e.activation(
                    HD[:, kv * 30:kv * 30 + 30], ps[:, kv * 30:kv * 30 + 30], ACT.Gelu_apprx_tanh,
                    bias=c("cmp_b1_2", kv)), done)
            act.quiet(lambda e: e.sem_inc(s_ev, 1), a, (s_ev, n))
            banks.release(at, 1, a)
            at, ps, free = banks.take()
            pe.do(mm(ps[0:64, 0:30], cmpw2[:, 0:64], HD[:, 0:30]), a, *free)
            for g in range(NSA_G):
                done = pe.do(mm(ps[0:N_CMP, 64 + g * 64:128 + g * 64], HD[:, 30 + g * N_CMP:30 + (g + 1) * N_CMP],
                                cmpw2[:, 64:128]))
            dve.do(lambda e, ps=ps: e.tensor_scalar(KCT[0:64, :], ps[0:64, 0:30], c("cmp_b2_2")[0:64, :], None,
                                                    ALU.add), done)
            v = dve.do(lambda e, ps=ps: e.tensor_tensor(
                VC[0:N_CMP, :, :], ps[0:N_CMP, 64:192].rearrange("p (g d) -> p g d", g=NSA_G),
                row[0:N_CMP, 0:64].unsqueeze(1).broadcast_to([N_CMP, NSA_G, NSA_D]), ALU.add))
            banks.release(at, 1, v)

            scale = NSA_D ** -0.5
            gate = lambda t, b, lo, hi: GA[:, t, :].rearrange("p (h b) -> p h b", b=3)[:, lo:hi, b]
            dve.wait(gates_ready)
            turn_w = 0
            for t in range(TT):
                def products(ps, needs, t=t):
                    for hd in range(NSA_H):
                        done = pe.do(mm(ps[:, hd * N_CMP:(hd + 1) * N_CMP], QU[0:64, hd, t * P:(t + 1) * P],
                                        KCT[0:64, (hd // 4) * N_CMP:(hd // 4 + 1) * N_CMP]), *needs)
                    return done
                pc = PC[:, :, 0:N_CMP]
                softmax(products, NSA_H, N_CMP, scale, seen_add[:, t, 0:N_CMP], None, gate(t, 0, 0, 8), pc,
                        [v, act.now()], stats[0])
                v = dve.do(lambda e, t=t, pc=pc: e.tensor_tensor(
                    pc, pc, seen[:, t, 0:N_CMP].unsqueeze(1).broadcast_to([P, NSA_H, N_CMP]), ALU.mult))
                for half in range(2):
                    turn([PC[:, 4 * half + i, :] for i in range(4)], [v],
                         copy_evac(act, PCT[:, half * 512:(half + 1) * 512]))
                length = (t + 1) * P
                for b, keys in ((0, KST), (1, KWT)):
                    for g in range(NSA_G):
                        def products(ps, needs, t=t, keys=keys, g=g, length=length):
                            for i in range(4):
                                done = pe.do(mm(ps[:, i * length:(i + 1) * length],
                                                QT[0:64, 4 * g + i, t * P:(t + 1) * P], keys[0:64, g, 0:length]),
                                             *needs)
                            return done
                        w = W[turn_w % 2][:, :, 0:length]
                        v = softmax(products, 4, length, scale, causal[:, t, 0:length], None,
                                    gate(t, 1 + b, 4 * g, 4 * g + 4), w, [act.now()], stats[turn_w % 2])
                        turn_w += 1
                        for k in range(t + 1):
                            turn([w[:, i, k * P:(k + 1) * P] for i in range(4)], [v],
                                 copy_evac(act, PT[:, 2 * b + k, g * 512:(g + 1) * 512]))
                at, ps, free = banks.take()
                for hd in range(NSA_H):
                    g = hd // 4
                    s = slice(hd * P, (hd + 1) * P)
                    o = ps[:, hd * 64:(hd + 1) * 64]
                    terms = [(PCT[:, s], VC[:, g, :])]
                    for k in range(t + 1):
                        terms.append((PT[:, k, s], zkv[:, k, 384 + g * 64:448 + g * 64]))
                        terms.append((PT[:, 2 + k, s], zw[:, k, 128 + g * 64:192 + g * 64]))
                    for i, (a, b) in enumerate(terms):
                        done = pe.do(mm(o, a, b, i == 0, i == len(terms) - 1), act.now(), *free)
                v = dve.do(lambda e, ps=ps, t=t: e.tensor_copy(NS[:, t, :], ps), done)
                banks.release(at, 1, v)
            for b in range(2):
                turn([NS[:, t, k * P:(k + 1) * P] for k in (2 * b, 2 * b + 1) for t in range(TT)], [v],
                     copy_evac(act, xT[:, 4 + 2 * b:6 + 2 * b, :].rearrange("p k t -> p (k t)")))

        def memory():
            used[0] = 0
            M = cut(TT, D)
            MTT = cut(KD, T)
            QM, KM, VM = cut(8, T), cut(8, T), cut(TT, D)
            W = cut(MEM_H, T)
            PT = cut(TT, MEM_H * P)
            OM = cut(TT, D)
            stats = cut(8)
            have = load("memory", M.rearrange("p t n -> p (t n)"), mem.rearrange("(t p) n -> p t n", p=P))
            scaled = rms_scale(h)
            t = feature_major(xn, xT, lambda k: c("mem_q_norm_g_2", k), [scaled])
            q_first, _ = project("mem_q", xT, False, *t)
            dve.wait(pe.now())
            act.wait(pe.now())
            act.wait(have)
            dve.wait(have)
            scaled = rms_scale(M, dve.now())
            t = feature_major(xn, MTT, lambda k: c("mem_kv_norm_g_2", k), [scaled])
            k_first, _ = project("mem_k", MTT, False, *t)
            v_first, _ = project("mem_v", MTT, True)
            for first, dst in ((q_first, QM), (k_first, KM)):
                for i in range(2):
                    copy_out(act, first + i, dst[:, 4 * i:4 * i + 4, :].rearrange("p k t -> p (k t)"))
            for i in range(2):
                evacuate(act, v_first + i, lambda e, ps, i=i: e.activation(
                    VM[:, :, i * CW:(i + 1) * CW], ps[:, :].rearrange("p (t n) -> p t n", t=TT), ACT.Copy))
            ready = (s_ev, v_first + 2)
            for t in range(TT):
                def products(ps, needs, t=t):
                    for hd in range(MEM_H):
                        for k in range(2):
                            done = pe.do(mm(ps[:, hd * T:(hd + 1) * T], QM[:, 2 * hd + k, t * P:(t + 1) * P],
                                            KM[:, 2 * hd + k, :], k == 0, k == 1), *needs)
                    return done
                v = softmax(products, MEM_H, T, 256 ** -0.5, None, None, None, W, [ready], stats)
                for k in range(TT):
                    turn([W[:, hd, k * P:(k + 1) * P] for hd in range(MEM_H)], [v], copy_evac(act, PT[:, k, :]))
                at, ps, free = banks.take(2)
                for hd in range(MEM_H):
                    for k in range(TT):
                        done = pe.do(mm(ps[:, hd * T:(hd + 1) * T], PT[:, k, hd * P:(hd + 1) * P],
                                        VM[:, k, hd * T:(hd + 1) * T], k == 0, k == 1), act.now(), *free)
                v = dve.do(lambda e, ps=ps, t=t: e.tensor_copy(OM[:, t, :], ps), done)
                banks.release(at, 2, v)
            t = feature_major(OM, xT, plain, [v])
            add_projection("mem_o", *t)

        def peer_select():
            used[0] = 0
            QP = cut(16, T)
            SC, SR = cut(32, P), cut(32, P)
            V16 = cut(32, 16)
            I16 = cut(32, 16)
            IU = cut(32, 16)
            C, CR = cut(16, T), cut(16, T)
            B16, PU = cut(16, 16), cut(16, 16)
            EQ = cut(2048)
            AB = cut(2, T)
            PK = cut(3, T)
            st = cut(32)
            scaled = rms_scale(h)
            t = feature_major(xn, xT, lambda k: c("peer_norm_g_2", k), [scaled])
            first, count = project("peer_q", xT, False, *t)
            for n in range(count):
                copy_out(act, first + n, QP[:, 4 * n:4 * n + 4, :].rearrange("p k t -> p (k t)"))
            n = STREAM["peer_keys"][0]
            chunk_at[0] = n + 1
            pe.wait((s_w[n % 2], 16 * (n // 2) + 16))
            for t in range(TT):
                for b in range(4):
                    at, ps, free = banks.take()
                    for i in range(4):
                        hp = 4 * b + i
                        done = pe.do(mm(ps[:, i * P:(i + 1) * P], QP[:, hp, t * P:(t + 1) * P],
                                        ring[n % 2][:, hp * P:(hp + 1) * P]), (s_ev, first + count), *free)
                    lo = 16 * t + 4 * b
                    a = act.do(lambda e, ps=ps, lo=lo: e.activation(
                        SC[:, lo:lo + 4, :].rearrange("p a b -> p (a b)"), ps, ACT.Copy), done)
                    banks.release(at, 1, a)
            pe.quiet(lambda e: e.sem_inc(s_mm, 1), done)
            act.quiet(lambda e: e.sem_inc(s_ev, 1), a, (s_ev, n))

            def top16(src, rest, count, values, indices):
                iu = indices.bitcast(U32)
                passes = (
                    lambda e, i: e.max(values[:, i, 0:8], src[:, i, :]),
                    lambda e, i: e.match_replace(out=rest[:, i, :], in_to_replace=values[:, i, 0:8],
                                                 in_values=src[:, i, :], imm_value=-3e38),
                    lambda e, i: e.max(values[:, i, 8:16], rest[:, i, :]),
                    lambda e, i: e.max_index(iu[:, i, 0:8], values[:, i, 0:8], src[:, i, :]),
                    lambda e, i: e.max_index(iu[:, i, 8:16], values[:, i, 8:16], rest[:, i, :]))
                for step in passes:
                    before = dve.now()
                    for i in range(count):
                        dve.do(lambda e, step=step, i=i: step(e, i), before, own=False)

            dve.wait(a)
            top16(SC, SR, 32, V16, IU)
            dve.do(lambda e: e.tensor_copy(I16, IU.bitcast(U32)))
            v4 = V16.rearrange("p (t h s) k -> p t h s k", t=TT, s=2) if False else V16
            wide = [P, PEER_H, 16, 16]
            half = lambda a, t, s: a[:, 16 * t:16 * t + 16, :].rearrange("p (h s) k -> p h s k", s=2)[:, :, s, :]
            for t in range(TT):
                dve.do(lambda e, t=t: e.tensor_tensor(
                    C[:, 8 * t:8 * t + 8, :].rearrange("p h (a b) -> p h a b", a=16),
                    half(V16, t, 0).unsqueeze(3).broadcast_to(wide), half(V16, t, 1).unsqueeze(2).broadcast_to(wide),
                    ALU.add))
            top16(C, CR, 16, B16, PU)
            pos = PU.rearrange("p a b -> p (a b)").bitcast(U32)
            ab_u = CR[:, 0:2, :].bitcast(U32)
            dve.do(lambda e: e.tensor_scalar(ab_u[:, 0, :], pos, 4, None, ALU.logical_shift_right))
            dve.do(lambda e: e.tensor_scalar(ab_u[:, 1, :], pos, 15, None, ALU.bitwise_and))
            dve.do(lambda e: e.tensor_copy(AB, ab_u))
            eq = EQ.rearrange("p (h k j) -> p h k j", h=PEER_H, k=16)
            for s in range(2):
                for t in range(TT):
                    which = AB[:, s, t * P:(t + 1) * P].rearrange("p (h k) -> p h k", h=PEER_H)
                    dve.do(lambda e, which=which: e.tensor_tensor(
                        eq, iota[:, 0:16].unsqueeze(1).unsqueeze(1).broadcast_to(wide),
                        which.unsqueeze(3).broadcast_to(wide), ALU.is_equal))
                    dve.do(lambda e, t=t, s=s: e.tensor_tensor(
                        eq, eq, half(I16, t, s).unsqueeze(2).broadcast_to(wide), ALU.mult))
                    dve.do(lambda e, t=t, s=s: e.tensor_reduce(
                        PK[:, s, t * P:(t + 1) * P], EQ.rearrange("p (r j) -> p r j", j=16), AX.X, ALU.add))
            rows16 = PK[:, 2, :].rearrange("p (r k) -> p r k", k=16)
            v = dve.do(lambda e: e.tensor_tensor(rows16, B16, B16[:, :, 0:1].broadcast_to([P, 16, 16]), ALU.subtract))
            a = act.do(lambda e: e.activation(PK[:, 2, :], PK[:, 2, :], ACT.Exp), v)
            dve.do(lambda e: e.tensor_reduce(st[:, 0:16], rows16, AX.X, ALU.add), a)
            dve.do(lambda e: e.reciprocal(st[:, 0:16], st[:, 0:16]))
            v = dve.do(lambda e: e.tensor_tensor(rows16, rows16, st[:, 0:16].unsqueeze(2).broadcast_to([P, 16, 16]),
                                                 ALU.mult))
            for what in ((0, 1), (2,)):
                turn([PK[:, i, t * P:(t + 1) * P] for i in what for t in range(TT)], [v],
                     copy_evac(act, picks[:, what[0]:what[-1] + 1, :].rearrange("p a t -> p (a t)")))

        def peer_gates():
            G = arena[:, :].rearrange("p (s n) -> p s n", n=4 * P)
            cols_hot = [xn[:, 0, 512 * s:512 * s + 512].rearrange("p (a b) -> p a b", b=P) for s in range(2)]
            rows_hot = [xn[:, 1, 512 * s:512 * s + 512].rearrange("p (a b) -> p a b", b=P) for s in range(2)]
            s_rows, s_cols, s_made, s_kept = (sem(n) for n in ("s_rows", "s_cols", "s_made", "s_kept"))
            groups = T // 4
            wide = [P, 4, P]

            def loop(e, body):
                for g in range(4):
                    body(e, g, g)
                with e.Fori(1, groups // 4) as i:
                    for g in range(4):
                        body(e, i * 4 + g, g)

            def after(e, s, n, back):
                if not isinstance(n, int) or n >= back:
                    e.wait_ge(s, n - (back - 1))

            def hot_body(e, n, g):
                after(e, s_made, n, 2)
                r = picks[:, 0, bass.ds(n * 4, 4)] if not isinstance(n, int) else picks[:, 0, 4 * n:4 * n + 4]
                e.tensor_tensor(rows_hot[g % 2], iota.unsqueeze(1).broadcast_to(wide),
                                r.unsqueeze(2).broadcast_to(wide), ALU.is_equal).then_inc(s_rows, 1)

                for i in range(4):
                    at = n * 4 + i
                    pick = (lambda q: picks[:, q, at:at + 1]) if isinstance(at, int) else (
                        lambda q: picks[:, q, bass.ds(at, 1)])
                    last = e.tensor_scalar(cols_hot[g % 2][:, i, :], iota, pick(1), pick(2), ALU.is_equal, ALU.mult)
                last.then_inc(s_cols, 1)

            def made_body(e, n, g):
                e.wait_ge(s_rows, n + 1)
                e.wait_ge(s_cols, n + 1)
                after(e, s_kept, n, 4)
                for i in range(4):
                    last = e.matmul(ps_misc[:, g, i * P:(i + 1) * P], cols_hot[g % 2][:, i, :],
                                    rows_hot[g % 2][:, i, :], start=True, stop=True)
                last.then_inc(s_made, 1)

            def kept_body(e, n, g):
                e.wait_ge(s_made, n + 1)
                o = G[:, n, :] if isinstance(n, int) else G[:, bass.ds(n, 1), :].rearrange("p a n -> p (a n)")
                e.activation(o, ps_misc[:, g, :], ACT.Copy).then_inc(s_kept, 1)

            dve.steps.append(lambda e: loop(e, hot_body))
            pe.steps.append(lambda e: loop(e, made_body))
            act.steps.append(lambda e: loop(e, kept_body))
            for lane in work:
                lane.wait((s_kept, groups))

        def peer_experts():
            first, count = STREAM["peer"]
            chunk_at[0] = first + count
            G = arena[:, :].rearrange("p (t i) -> p t i", i=P)
            gel = [[xn[:, 0, (2 * s + b) * T:(2 * s + b + 1) * T] for b in range(2)] for s in range(2)]
            hid = [[xn[:, 1, (2 * s + b) * T:(2 * s + b + 1) * T] for b in range(2)] for s in range(2)]
            s_hid = sem("s_hid")

            def u_part(e, slot, n):
                room(e, n)
                for b in range(2):
                    for k in range(KD):
                        last = e.matmul(ps_chunk[slot][:, 512 * b:512 * b + T],
                                        ring[slot][:, (b * KD + k) * P:(b * KD + k + 1) * P], xT[:, k, :],
                                        start=k == 0, stop=k == KD - 1)
                    last.then_inc(s_u, 1)

            def v_part(e, slot, m, begin, end):
                for b in range(2):
                    e.wait_ge(s_hid, m * 2 + (b - 1))
                    for t in range(TT):
                        for half in range(2):
                            last = e.matmul(ps_misc[:, 2 * t + half, :], hid[1 - slot][b][:, t * P:(t + 1) * P],
                                            ring[slot][:, 2 * D + b * D + half * CW:2 * D + b * D + (half + 1) * CW],
                                            start=begin and b == 0, stop=end and b == 1)
                last.then_inc(s_mm, 1)

            s_u = sem("s_u")

            def pe_body(e, slot, n, half):
                m = n - first
                landed(e, slot, half)
                first_one, last_one = isinstance(m, int) and m == 0, isinstance(m, int) and m == count - 1
                if not last_one:
                    u_part(e, slot, n)
                if first_one:
                    e.wait_ge(s_u, 2)
                    e.sem_inc(s_mm, 1)
                else:
                    v_part(e, slot, m, isinstance(m, int) and m == 1, last_one)

            def act_body(e, slot, n, half):
                m = n - first
                if isinstance(m, int) and m == count - 1:
                    return
                for b in range(2):
                    e.wait_ge(s_u, m * 2 + (b + 1))
                    if not isinstance(m, int) or m >= 2:
                        e.wait_ge(s_hid, m * 2 + (b - 3))
                    o = e.activation(gel[slot][b], ps_chunk[slot][:, 512 * b:512 * b + T], ACT.Gelu_apprx_tanh)
                    o.then_inc(s_gel, 1)
                e.wait_ge(s_gel, m * 2 + 2)
                e.sem_inc(s_ev, 1)

            s_gel = sem("s_gel")

            def dve_body(e, slot, n, half):
                m = n - first
                if isinstance(m, int) and m == count - 1:
                    return
                if not isinstance(m, int) or m >= 2:
                    e.wait_ge(s_mm, n)
                for b in range(2):
                    e.wait_ge(s_gel, m * 2 + (b + 1))
                    i = m * 2 + b
                    g = G[:, :, i] if isinstance(i, int) else G[:, :, bass.ds(i, 1)].rearrange("p t a -> p (t a)")
                    e.tensor_tensor(hid[slot][b], gel[slot][b], g, ALU.mult).then_inc(s_hid, 1)

            for lane, body in ((pe, pe_body), (act, act_body), (dve, dve_body)):
                over_chunks(lane, first, 3, body)
                over_chunks(lane, first + 3, count - 4, body)
                over_chunks(lane, first + count - 1, 1, body)
            dve.wait((s_mm, first + count))
            hf = h[:, :, :].rearrange("p t n -> p (t n)")
            summed = dve.do(lambda e: e.tensor_tensor(hf, hf, ps_misc[:, :, :].rearrange("p b n -> p (b n)"), ALU.add))
            act.wait(summed)

        def finish():
            rms_scale(h)
            v = dve.do(lambda e: e.tensor_tensor(xn[:, :, :], xn[:, :, :], r(ROWS_2, "final_norm_g_2").unsqueeze(1)
                                                 .broadcast_to([P, TT, D]), ALU.mult))
            sp_out[0] += 16
            act.quiet(lambda e: e.dma_start(out.rearrange("(t p) n -> p t n", p=P), xn[:, :, :]).then_inc(s_out, 16), v)

        fence()
        mixers_2()
        add_projection("w_out_2", act.now(), dve.now())
        fence()
        memory()
        fence()
        peer_select()
        fence()
        peer_gates()
        peer_experts()
        finish()
        act.wait((s_out, sp_out[0]))

        with nc.Block() as block:
            @block.sync
            def _(e):
                sp.emit(e)

            @block.tensor
            def _(e):
                pe.emit(e)

            @block.vector
            def _(e):
                dve.emit(e)

            @block.scalar
            def _(e):
                act.emit(e)

            @block.gpsimd
            def _(e):
                pool.emit(e)




def chunked(w):
    rows, n = w.shape
    pad = -n % CW
    if pad:
        w = np.concatenate([w, np.zeros((rows, pad), w.dtype)], 1)
    return w.reshape(KD, P, -1, CW).transpose(2, 1, 0, 3).reshape(-1, P, CHUNK)


def padded(a):
    out = np.zeros(a.shape[:-1] + (CHUNK,), a.dtype)
    out[..., :a.shape[-1]] = a
    return out.reshape(-1, P, CHUNK)


def lay_out(a):
    w = a["w_in"][0]
    aq, af, ai, ag = (w[:, 512 * n:512 * (n + 1)] for n in range(4))
    bq, bk, bv, cc = w[:, 2048:2304], w[:, 2304:2560], w[:, 2560:2816], w[:, 2816:]
    parts = {}
    parts["w_in feature"] = chunked(np.concatenate([cc, aq, af, bq, bk], 1))
    parts["w_in token"] = chunked(np.concatenate([ai, ag, bv], 1))
    parts["w_out"] = chunked(a["w_out"][0])
    up = a["ffn_up"][0].reshape(D, 2, NF // 2, 2 * P).transpose(0, 2, 1, 3).reshape(D, 2 * D_FF)
    parts["ffn_up"] = chunked(up)
    down = np.zeros((24, P, D), np.float32)
    down[:NF] = a["ffn_down"][0].reshape(NF, P, D)
    parts["ffn_down"] = down.reshape(6, 4, P, D).transpose(0, 2, 1, 3).reshape(6, P, CHUNK)
    parts["ple_gate"] = chunked(a["ple_gate"][0])
    proj = a["ple_proj"][0].reshape(2, P, D).transpose(1, 0, 2).reshape(P, 2 * D)
    p_t = a["p"][0, 0].T.reshape(2, P, T).transpose(1, 0, 2).reshape(P, 2 * T)
    parts["ple_proj"] = padded(np.concatenate([proj, p_t], 1))
    w = a["w_in_2"][0]
    parts["w_in_2 feature"] = chunked(w[:, :2 * CW])
    parts["w_in_2 token"] = chunked(w[:, 2 * CW:])
    w1 = a["cmp_w1_2"][0].reshape(2, CMP_B // 2, P, P).transpose(2, 0, 1, 3).reshape(P, -1)
    parts["cmp_w1"] = padded(w1)
    parts["w_out_2"] = chunked(a["w_out_2"][0])
    for n in "qkvo":
        parts["mem_" + n] = chunked(a["w_mem_%s_2" % n][0])
    parts["peer_q"] = chunked(a["peer_w_q_2"][0])
    keys = a["peer_sub_keys_2"][0].reshape(16, P, P).transpose(2, 0, 1).reshape(P, 16 * P)
    parts["peer_keys"] = padded(keys)
    u = a["peer_u_2"][0].reshape(64, 2, P, KD, P).transpose(0, 4, 1, 3, 2)
    vv = a["peer_v_2"][0].reshape(64, 2, P, D).transpose(0, 2, 1, 3)
    peer = np.zeros((65, P, CHUNK), np.float32)
    peer[:64, :, :2 * D] = u.reshape(64, P, 2 * D)
    peer[1:, :, 2 * D:] = vv.reshape(64, P, 2 * D)
    parts["peer"] = peer
    stream = np.empty((N_CHUNKS, P, CHUNK), np.float32)
    for name, (first, count) in STREAM.items():
        assert parts[name].shape[0] == count, (name, parts[name].shape, count)
        stream[first:first + count] = parts[name]

    cols = np.zeros((P, N_COLS), np.float32)

    def put(name, value):
        at, n = COLS[name]
        cols[:, at:at + n] = value

    tiles = lambda v: v.reshape(-1, P).T
    for name, (at, n) in COLS.items():
        if name in a and name not in ("conv_dw_w_2", "cmp_b1_2", "cmp_b2_2", "cmp_pos_2"):
            put(name, tiles(a[name]))
    taps = np.concatenate([a["ffn_conv_w"][0], a["ffn_conv_b"]], 0)
    put("ffn_conv", taps.reshape(4, 2, NF // 2, 2, P).transpose(4, 2, 1, 3, 0).reshape(P, -1))
    put("conv_dw_w_2", a["conv_dw_w_2"][0].reshape(CONV_K, CONV_T, P).transpose(2, 0, 1).reshape(P, -1))
    put("cmp_b1_2", a["cmp_b1_2"][0].T)
    put("cmp_b2_2", np.concatenate([a["cmp_b2_2"][0, 0], np.zeros(64, np.float32)])[:, None])
    put("cmp_pos_2", a["cmp_pos_2"][0].reshape(2, CMP_B // 2, P).transpose(2, 0, 1).reshape(P, 32))
    put("eps", EPS)
    put("gn_eps", RK_GN_EPS)
    put("one", 1.0)
    rows = np.zeros((2, 2048), np.float32)
    for name, (at, n) in ROWS_1.items():
        rows[0, at:at + n] = a[name].reshape(-1)
    rows[1, 0:64] = a["cmp_b2_2"][0, 1]
    rows[1, 1024:2048] = a["final_norm_g_2"]
    small = np.zeros((P, 512), np.float32)
    small[:64, :256], small[64:, :256], small[:, 256:] = a["rwkv_w2"][0], a["rwkv_a2"][0], a["rwkv_g2"][0]
    return {"stream": stream, "cols": cols, "rows": rows, "consts0": CONSTS[0], "consts1": CONSTS[1],
            "consts2": CONSTS[2], "x": a["x"][0], "mem": a["mem_2"][0],
            "positions": np.ascontiguousarray(a["positions_2"].reshape(TT, P).T),
            "small_w": small, "cmp_w2": np.ascontiguousarray(a["cmp_w2_2"][0].transpose(1, 0, 2).reshape(P, 128))}


def kernel(**inputs):
    import concourse.bacc as bacc
    from concourse.bass_utils import run_bass_kernel_spmd

    arrays = lay_out({name: np.asarray(value) for name, value in inputs.items()})
    nc = bacc.Bacc("TRN2", target_bir_lowering=False, num_devices=1)
    aps = {name: nc.dram_tensor("in_" + name, a.shape, mybir.dt.from_np(a.dtype), kind="ExternalInput").ap()
           for name, a in arrays.items()}
    out = nc.dram_tensor("out", (T, D), F32, kind="ExternalOutput").ap()
    build(nc, out=out, **aps)
    result = run_bass_kernel_spmd(nc, [{"in_" + name: a for name, a in arrays.items()}], core_ids=[0])
    return result.results[0]["out"].reshape(1, T, D)
```

```python
import concourse.bass as bass
import numpy as np
from concourse import mybir
from contextlib import ExitStack

F32 = mybir.dt.float32
F32R = mybir.dt.float32r
I32 = mybir.dt.int32
U32 = mybir.dt.uint32
ALU = mybir.AluOpType
ACT = mybir.ActivationFunctionType
AX = mybir.AxisListType

P = 128
T = 256
TT = T // P
D = 1024
KD = D // P
CW = 512
UNIT = 1024
UNITS = 4
EPS = 1e-6
NEG = -1e30
HG_H, HG_K, HG_C = 4, 128, 64
RK_H, RK_N, RK_C = 4, 64, 64
RK_GN_EPS = 64e-5
RK_DECAY_SCALE = float(np.exp(-0.5))
SW_H, SW_D = 4, 64
SW_PATTERNS = ((128, 1), (512, 4), (2048, 16))
D_FF = 2816
NF = D_FF // P
CONV_K, CONV_T = 31, 4
NSA_H, NSA_G, NSA_D = 8, 2, 64
CMP_B, CMP_S = 32, 16
N_CMP = (T - CMP_B) // CMP_S + 1
ROPE_HALF = 8
ROPE_THETA = 500000.0
MEM_H = 4
PEER_H, PEER_K, PEER_TOP = 8, 128, 16
N_RET = PEER_H * PEER_TOP
LEVELS = 6

STREAM = {}
_at = 0
for _name, _count in (("w_in feature", 5), ("w_in token", 3), ("w_out", 2), ("ffn_up", 11), ("ffn_down, ple_proj", 6),
                      ("ple_gate", 2), ("w_in_2 feature", 2), ("w_in_2 token", 3), ("w_out_2", 2), ("mem_k", 2),
                      ("mem_v", 2), ("mem_q", 2), ("mem_o", 2), ("peer_q", 4), ("peer", 65)):
    STREAM[_name] = (_at, _count)
    _at += _count
N_CHUNKS = _at


def columns_plan():
    plan, at = {}, 0
    for name, n in (("norm_mix_g", 8), ("norm_ffn_g", 8), ("norm_ple_g", 8), ("rwkv_mu", 8), ("rwkv_w0", 2),
                    ("rwkv_a0", 2), ("rwkv_k_k", 2), ("rwkv_k_a", 2), ("rwkv_r_k", 2),
                    ("ffn_conv", 4 * 2 * NF), ("mix_norm_g_2", 8), ("conv_dw_w_2", CONV_K * CONV_T),
                    ("conv_dw_b_2", CONV_T), ("conv_ln_g_2", CONV_T), ("conv_ln_b_2", CONV_T), ("cmp_b1_2", 2),
                    ("cmp_b2_2", 1), ("cmp_pos_2", 32), ("mem_q_norm_g_2", 8), ("mem_kv_norm_g_2", 8),
                    ("peer_norm_g_2", 8), ("eps", 1), ("gn_eps", 1), ("one", 1)):
        plan[name] = (at, n)
        at += n
    return plan, at


COLS, N_COLS = columns_plan()
ROWS_1 = {"hgrn_gnorm_g": (0, 512), "rwkv_ln_w": (512, 256), "rwkv_ln_b": (768, 256)}


def shape_constants():
    i = np.arange(P)
    token = np.arange(T)
    always = [np.eye(P), np.broadcast_to(i, (P, P))]
    first = []
    for level in range(LEVELS):
        b = 2 << level
        left, right = i % b < b // 2, i % b >= b // 2
        first.append((i[:, None] // b == i[None] // b) & left[:, None] & right[None])
    first.append(np.eye(P))
    same = i[:, None] // RK_C == i[None] // RK_C
    first.append(same & (i[:, None] < i[None]))
    first.append(same & (i[:, None] <= i[None]))
    first.append(i[:, None] // RK_N == i[None] // RK_N)
    first.append(np.broadcast_to(np.arange(D) % HG_C != 0, (P, D)))
    q, k = token[:, None], token[None]
    held = np.zeros((T, T))
    for window, dil in SW_PATTERNS:
        held += (k <= q) & ((q - k) % dil == 0) & ((q - k) // dil <= window // dil)
    rows = lambda a: a.reshape(TT, P, -1).transpose(1, 0, 2).reshape(P, -1)
    first += [rows(held), rows(np.where(held > 0, 0.0, NEG))]
    first.append(np.stack([i < RK_N, i >= RK_N], 1))
    c = np.arange(16)
    seen = (c[None] * CMP_S + CMP_B - 1 <= token[:, None]) & (c[None] < N_CMP)
    second = [rows(np.where(k <= q, 0.0, NEG)), rows(seen * 1.0), rows(np.where(seen, 0.0, NEG))]
    inv = np.float32(ROPE_THETA) ** -(np.arange(ROPE_HALF, dtype=np.float32) * 2.0 / (2 * ROPE_HALF))
    second.append(np.broadcast_to(inv, (P, ROPE_HALF)))
    join = lambda parts: np.ascontiguousarray(np.concatenate([np.asarray(a, np.float32) for a in parts], 1))
    return join(always), join(first), join(second)


CONSTS = shape_constants()


class Lane:

    def __init__(self, sem, chained):
        self.sem, self.chained, self.n, self.steps, self.known = sem, chained, 0, [], {}

    def now(self):
        return (self.sem, self.n)

    def wait(self, *needs):
        for need in needs:
            if need is None or need[1] <= 0:
                continue
            sem, value = need
            if self.known.get(id(sem), 0) < value:
                self.known[id(sem)] = value
                self.steps.append(lambda e, sem=sem, value=value: e.wait_ge(sem, value))

    def do(self, f, *needs, own=None):
        self.wait(*needs)
        if self.chained if own is None else own:
            self.wait(self.now())
        self.n += 1
        self.steps.append(lambda e: f(e).then_inc(self.sem, 1))
        return self.now()

    def quiet(self, f, *needs):
        self.wait(*needs)
        self.steps.append(f)

    def emit(self, e):
        for step in self.steps:
            step(e)


class Banks:

    def __init__(self, tensor):
        self.tensor, self.free, self.turn = tensor, [()] * 4, 0

    def take(self, n=1):
        if n == 2 and self.turn % 2:
            self.turn += 1
        at = self.turn % 4
        self.turn += n
        needs = [x for b in range(at, at + n) for x in self.free[b]]
        return at, self.tensor[:, at:at + n, :].rearrange("p b n -> p (b n)"), needs

    def release(self, at, n, *tokens):
        for b in range(at, at + n):
            self.free[b] = tokens


def build(nc, stream, cols, rows, consts0, consts1, consts2, x, mem, positions, small_w, cmp_w1, cmp_w2, peer_keys, p_t, out):
    ctx = ExitStack()
    with ctx:
        def sb(name, shape, dt=F32):
            return ctx.enter_context(nc.sbuf_tensor(name, shape, dt))

        def sem(name):
            return ctx.enter_context(nc.semaphore(name))

        raw = [sb(f"raw{i}", [P, UNIT]) for i in range(UNITS)]
        w_hi = [sb(f"w_hi{i}", [P, UNIT], F32R) for i in range(2)]
        w_lo = [sb(f"w_lo{i}", [P, UNIT], F32R) for i in range(2)]
        x_hi, x_lo = sb("x_hi", [P, KD, T], F32R), sb("x_lo", [P, KD, T], F32R)
        hid_hi, hid_lo = sb("hid_hi", [P, 2, T], F32R), sb("hid_lo", [P, 2, T], F32R)
        h = sb("h", [P, TT, D])
        xn = sb("xn", [P, TT, D])
        col = sb("col", [P, N_COLS])
        row = sb("row", [P, D])
        ident_iota = sb("ident_iota", [P, 2 * P])
        picks = sb("picks", [P, 3, T])
        ss = sb("ss", [P, 8])
        ident, iota = ident_iota[:, 0:P], ident_iota[:, P:2 * P]
        ps_chunk = [ctx.enter_context(nc.psum_tensor(f"ps_chunk{i}", [P, 1024], F32)) for i in range(2)]
        ps_misc = ctx.enter_context(nc.psum_tensor("ps_misc", [P, 4, 512], F32))
        banks = Banks(ps_misc)

        s_w = [sem(f"s_w{i}") for i in range(UNITS)]
        s_hi = sem("s_hi")
        s_lo = sem("s_lo")
        s_use = sem("s_use")
        s_ev = sem("s_ev")
        s_out = sem("s_out")
        pe = Lane(sem("s_pe"), False)
        dve = Lane(sem("s_dve"), True)
        act = Lane(sem("s_act"), True)
        pool = Lane(sem("s_pool"), True)
        sp = Lane(sem("s_sp"), False)
        work = (pe, dve, act, pool)

        def c(name, i=0, n=1):
            return col[:, COLS[name][0] + i:COLS[name][0] + i + n]

        def r(plan, name):
            at, n = plan[name]
            return row[:, at:at + n]

        memory_of = ExitStack()
        places = {}

        def phase(name, *tensors):
            memory_of.close()
            for key, shape, dt in tensors:
                places[key] = memory_of.enter_context(nc.sbuf_tensor(f"{name}_{key}", shape, dt))
            used[0] = 0

        used = [0]
        phase("mixers", ("arena", [P, P * T], F32))

        def cut(*shape):
            n = int(np.prod(shape))
            at = used[0]
            used[0] += n
            assert used[0] <= places["arena"].shape[1], used
            a = places["arena"][:, at:at + n]
            if len(shape) == 2:
                a = a.rearrange("p (a b) -> p a b", b=shape[1])
            if len(shape) == 3:
                a = a.rearrange("p (a b c) -> p a b c", b=shape[1], c=shape[2])
            return a

        chunk_at = [0]

        def fence():
            totals = [lane.now() for lane in work] + [(s_use, UNITS * chunk_at[0]), (s_ev, chunk_at[0])]
            for lane in work + (sp,):
                lane.wait(*totals)
            for b in range(4):
                banks.free[b] = ()

        def mm(out, lhsT, rhs, start=True, stop=True):
            return lambda e: e.matmul(out, lhsT, rhs, start=start, stop=stop, skip_group_check=True)

        rows_at = [0]

        def rows_from(base):
            moved, rows_at[0] = base != rows_at[0], base
            return pe.now() if moved else None

        sent = {}

        def load(name, dst, src, *needs):
            if name not in sent:
                sent[name] = [sem("s_load_" + name), 0]
            group = sent[name]
            group[1] += 16
            act.quiet(lambda e: e.dma_start(dst, src).then_inc(group[0], 16), *needs)
            return tuple(group)

        load("first", h[:, :, :], x.rearrange("(t p) n -> p t n", p=P))
        load("first", ident_iota[:, :], consts0)
        have_first = load("first", col[:, :], cols)
        have_rows = load("rows", row[:, :], rows[0:1, :].broadcast_to([P, D]))

        def feed(e):
            def put(q, u):
                src = stream[u, :, :] if isinstance(u, int) else stream[bass.ds(u, 1), :, :].rearrange("a p n -> p (a n)")
                e.dma_start(raw[q][:, :], src).then_inc(s_w[q], 16)

            for q in range(UNITS):
                put(q, q)
            with e.Fori(1, chunk_at[0]) as i:
                for q in range(UNITS):
                    e.wait_ge(s_lo, i * UNITS + (q + 1 - UNITS))
                    put(q, i * UNITS + q)

        sp.steps.append(feed)

        def over_chunks(lane, first, count, body):
            def run(e):
                n, end = first, first + count
                while n < end and (n % 2 or n == 0):
                    for _ in range(2 if n == 0 else 1):
                        if n < end:
                            body(e, n % 2, n, n // 2)
                            n += 1
                pairs = (end - n) // 2
                if pairs > 1:
                    with e.Fori(0, pairs) as i:
                        for slot in range(2):
                            body(e, slot, i * 2 + (n + slot), i + n // 2)
                    n += 2 * pairs
                while n < end:
                    body(e, n % 2, n, n // 2)
                    n += 1
            lane.steps.append(run)

        def split_hi(e, q, n):
            e.wait_ge(s_w[q], n * 16 + 16)
            if not isinstance(n, int) or UNITS * n + q >= 2:
                e.wait_ge(s_use, n * UNITS + (q - 1))
            e.activation(w_hi[q % 2][:, :], raw[q][:, :], ACT.Copy).then_inc(s_hi, 1)

        def split_lo(e, q, n):
            e.wait_ge(s_hi, n * UNITS + (q + 1))
            e.tensor_tensor(w_lo[q % 2][:, :], raw[q][:, :], w_hi[q % 2][:, :].bitcast(F32),
                            ALU.subtract).then_inc(s_lo, 1)

        def split_chunks(first, count, act_hooks=(), dve_hooks=()):
            for lane, split, hooks in ((act, split_hi, act_hooks), (dve, split_lo, dve_hooks)):
                def body(e, n, slot, splits, hooked, split=split, hooks=hooks):
                    for part in range(2):
                        if splits:
                            for q in (2 * part, 2 * part + 1):
                                split(e, q, n)
                        if hooked and part < len(hooks) and hooks[part]:
                            hooks[part](e, slot, n - 1)

                def run(e, body=body):
                    body(e, first, 0, True, False)
                    n = first + 1
                    pairs = (count - 1) // 2
                    if pairs > 2:
                        for _ in range(2):
                            body(e, n, (n - 1) % 2, True, True)
                            n += 1
                        with e.Fori(0, pairs - 1) as i:
                            for s in range(2):
                                body(e, i * 2 + (n + s), (n + s - 1) % 2, True, True)
                        n += 2 * (pairs - 1)
                    while n < first + count:
                        body(e, n, (n - 1) % 2, True, True)
                        n += 1
                    body(e, first + count, (first + count - 1) % 2, False, True)
                lane.wait((s_ev, first))
                lane.steps.append(run)
            chunk_at[0] = first + count

        def product3(e, o, stationary, moving, start, stop):
            for i, (a, b) in enumerate(((0, 0), (1, 0), (0, 1))):
                last = e.matmul(o, stationary[a], moving[b], start=start and i == 0, stop=stop and i == 2,
                                skip_group_check=True)
            return last

        def room(e, n):
            if not isinstance(n, int) or n > 1:
                e.wait_ge(s_ev, n - 1)

        def multiply(name, token_major, *needs):
            first, count = STREAM[name]
            pe.wait(*needs)

            def body(e, slot, n, half):
                room(e, n)
                for q in range(UNITS):
                    e.wait_ge(s_lo, n * UNITS + (q + 1))
                    w = (w_hi[q % 2], w_lo[q % 2])
                    if token_major:
                        for t in range(TT):
                            for i in range(2):
                                k = 2 * q + i
                                last = product3(e, ps_chunk[slot][:, t * CW:(t + 1) * CW],
                                                [x[:, k, t * P:(t + 1) * P] for x in (x_hi, x_lo)],
                                                [a[:, i * CW:(i + 1) * CW] for a in w], k == 0, k == KD - 1)
                    else:
                        for k in range(KD):
                            last = product3(e, ps_chunk[slot][:, q * T:(q + 1) * T],
                                            [a[:, k * P:(k + 1) * P] for a in w],
                                            [x[:, k, :] for x in (x_hi, x_lo)], k == 0, k == KD - 1)
                    last.then_inc(s_use, 1)

            over_chunks(pe, first, count, body)
            return first, count

        def copy_hook(first, dst):
            def hook(e, slot, m):
                e.wait_ge(s_use, m * UNITS + UNITS)
                at = m - first
                e.activation(dst(at) if isinstance(at, int) else dst(bass.ds(at, 1)), ps_chunk[slot][:, :],
                             ACT.Copy).then_inc(s_ev, 1)
            return hook

        def chunk_rows(Z):
            return lambda at: Z[:, at, :] if isinstance(at, int) else Z[:, at, :].rearrange("p a n -> p (a n)")

        def rms_scale(src, *needs):
            for t in range(TT):
                act.do(lambda e, t=t: e.activation(xn[:, t, :], src[:, t, :], ACT.Square, accum_out=ss[:, t:t + 1]),
                       *needs)
            root = act.do(lambda e: e.activation(ss[:, 2:4], ss[:, 0:2], ACT.Sqrt, scale=1.0 / D, bias=c("eps")))
            dve.do(lambda e: e.reciprocal(ss[:, 4:6], ss[:, 2:4]), root)
            for t in range(TT):
                done = dve.do(lambda e, t=t: e.tensor_scalar(xn[:, t, :], src[:, t, :], ss[:, 4 + t:5 + t], None,
                                                             ALU.mult), *needs)
            return done

        def turn(srcs, needs, evac, rows_out=P, banks_n=1):
            at, ps, free = banks.take(banks_n)
            for i, s in enumerate(srcs):
                done = pe.do(lambda e, i=i, s=s: e.transpose(ps[0:rows_out, i * P:(i + 1) * P], s, ident),
                             *needs, *free)
            tokens = evac(ps[0:rows_out, 0:len(srcs) * P], done)
            banks.release(at, banks_n, *tokens)
            return tokens

        def into_x(src, k, gain, needs):
            for i in range(src.shape[1] // T):
                piece = src[:, i * T:(i + 1) * T]
                act.do(lambda e, i=i, piece=piece: e.activation(x_hi[:, k + i, :], piece, ACT.Copy, scale=gain(k + i)),
                       *needs, own=False)
            for i in range(src.shape[1] // T):
                piece = src[:, i * T:(i + 1) * T]
                v = dve.do(lambda e, i=i, piece=piece: e.scalar_tensor_tensor(
                    out=x_lo[:, k + i, :], in0=piece, scalar=gain(k + i), in1=x_hi[:, k + i, :].bitcast(F32),
                    op0=ALU.mult, op1=ALU.subtract), act.now(), own=False)
            return (v,)

        def feature_major(src, gain, needs, k0=0, tiles=KD):
            for b in range(tiles // 2):
                pieces = [src[:, t, k * P:(k + 1) * P] for k in (2 * b, 2 * b + 1) for t in range(TT)]
                tokens = turn(pieces, needs, lambda ps, done, b=b: into_x(ps, k0 + 2 * b, gain, [done]))
            return tokens

        def copy_evac(lane, dst):
            def evac(ps, done):
                if lane is act:
                    return (act.do(lambda e: e.activation(dst, ps, ACT.Copy), done),)
                return (dve.do(lambda e: e.tensor_copy(dst, ps), done),)
            return evac

        def softmax(products, heads, length, scale, add, mult, gate, weights, needs, stats):
            at, ps, free = banks.take(2)
            done = products(ps, list(needs) + list(free))
            s = ps[:, 0:heads * length].rearrange("p (h l) -> p h l", h=heads)
            if add is not None:
                read = dve.do(lambda e: e.scalar_tensor_tensor(
                    out=weights, in0=s, scalar=scale, in1=add.unsqueeze(1).broadcast_to([P, heads, length]),
                    op0=ALU.mult, op1=ALU.add), done)
            else:
                read = dve.do(lambda e: e.tensor_scalar(weights, s, scale, None, ALU.mult), done)
            banks.release(at, 2, read)
            top, den = stats[:, 0:heads], stats[:, heads:2 * heads]
            wide = lambda a: a.unsqueeze(2).broadcast_to([P, heads, length])
            dve.do(lambda e: e.tensor_reduce(top, weights, AX.X, ALU.max))
            v = dve.do(lambda e: e.tensor_tensor(weights, weights, wide(top), ALU.subtract))
            a = act.do(lambda e: e.activation(weights, weights, ACT.Exp), v)
            dve.wait(a)
            if mult is not None:
                dve.do(lambda e: e.tensor_tensor(weights, weights, mult.unsqueeze(1).broadcast_to([P, heads, length]),
                                                 ALU.mult))
            dve.do(lambda e: e.tensor_reduce(den, weights, AX.X, ALU.add))
            dve.do(lambda e: e.reciprocal(den, den))
            if gate is not None:
                dve.do(lambda e: e.tensor_tensor(den, den, gate, ALU.mult))
            return dve.do(lambda e: e.tensor_tensor(weights, weights, wide(den), ALU.mult))

        def add_projection(name, *needs):
            first, count = multiply(name, True, *needs)

            def hook(e, slot, m):
                e.wait_ge(s_use, m * UNITS + UNITS)
                at = (m - first) * CW
                e.tensor_tensor(h[:, :, at:at + CW], h[:, :, at:at + CW],
                                ps_chunk[slot][:, :].rearrange("p (t n) -> p t n", t=TT), ALU.add).then_inc(s_ev, 1)

            split_chunks(first, count, dve_hooks=(hook,))
            return (s_ev, first + count)

        Z = cut(8, 1024)
        k1 = cut(consts1.shape[1])
        have_k1 = load("k1", k1, consts1)
        masks = k1[:, 0:10 * P].rearrange("p (m n) -> p m n", m=10)
        strict, inclusive, head_ones = masks[:, 7, :], masks[:, 8, :], masks[:, 9, :]
        restart = k1[:, 10 * P:10 * P + D]
        sw_held = k1[:, 10 * P + D:10 * P + D + 512].rearrange("p (t n) -> p t n", t=TT)
        sw_add = k1[:, 10 * P + D + 512:10 * P + D + 1024].rearrange("p (t n) -> p t n", t=TT)
        head_pick = k1[:, 10 * P + D + 1024:10 * P + D + 1026]
        mixed = xn
        lora = cut(2 * T)
        have_lora = load("k1", lora, small_w)

        dve.wait(have_first)
        act.wait(have_first)
        pe.wait(have_first)
        scaled = rms_scale(h)
        turned = feature_major(xn, lambda k: c("norm_mix_g", k), [scaled])
        first, _ = multiply("w_in feature", False, *turned)
        multiply("w_in token", True)
        split_chunks(first, 8, act_hooks=(copy_hook(first, chunk_rows(Z)),))
        fence()
        act.wait(have_rows, have_lora)
        dve.wait(have_rows, have_lora)
        pe.wait(have_lora)

        zc = Z[:, 0:2, :].rearrange("p c (k t) -> p (c k) t", t=T)
        zq, zf = Z[:, 2, :], Z[:, 3, :]
        zb = Z[:, 4, :].rearrange("p (k t) -> p k t", t=T)
        zi, zg = (Z[:, n, :].rearrange("p (t n) -> p t n", t=TT) for n in (5, 6))
        zv = Z[:, 7, :].rearrange("p (t n) -> p t n", t=TT)

        base = used[0]

        def hgrn():
            K, LF, B, E = cut(D), cut(D), cut(D), cut(D)
            QL, KL, QE = cut(D), cut(D), cut(D)
            S = cut(8, P)
            KT = cut(TT, 512)
            state = cut(HG_H, P)
            EL = cut(16)
            O = cut(TT, 512)
            by_head = lambda a: a.rearrange("p (h t) -> p h t", h=HG_H)
            act.do(lambda e: e.activation(K, zf, ACT.Sigmoid, scale=-1.0))
            act.do(lambda e: e.activation(zq, zq, ACT.Silu))
            g = act.do(lambda e: e.activation(Z[:, 6, :], Z[:, 6, :], ACT.Silu))
            act.do(lambda e: e.activation(LF, zf, ACT.Abs))
            act.do(lambda e: e.activation(LF, LF, ACT.Exp, scale=-1.0))
            a = act.do(lambda e: e.activation(LF, LF, ACT.Ln, bias=c("one")))
            dve.do(lambda e: e.scalar_tensor_tensor(out=LF, in0=zf, scalar=0.0, in1=LF, op0=ALU.min,
                                                    op1=ALU.subtract), a)
            dve.do(lambda e: e.tensor_tensor_scan(B, restart, LF, 0.0, ALU.mult, ALU.add))
            dve.do(lambda e: e.memset(S, 0.0))
            for level in range(-1, LEVELS):
                if level < 0:
                    q_l, k_l, mask, v = zq, K, masks[:, 6, :], dve.now()
                else:
                    b = 2 << level
                    view = lambda a, b=b: a.rearrange("p (m b) -> p m b", b=b)
                    mid = view(B)[:, :, b // 2 - 1:b // 2].broadcast_to([P, D // b, b])
                    v = dve.do(lambda e, view=view, mid=mid: e.tensor_tensor(view(E), view(B), mid, ALU.subtract),
                               act.now())
                    act.do(lambda e: e.activation(E, E, ACT.Abs), v)
                    a = act.do(lambda e: e.activation(E, E, ACT.Exp, scale=-1.0))
                    dve.do(lambda e: e.tensor_tensor(QL, zq, E, ALU.mult), a, pe.now())
                    v = dve.do(lambda e: e.tensor_tensor(KL, K, E, ALU.mult))
                    q_l, k_l, mask = QL, KL, masks[:, level, :]
                at, ps, free = banks.take(2)
                for i in range(8):
                    lo = i * P
                    done = pe.do(mm(ps[:, lo:lo + P], k_l[:, lo:lo + P], q_l[:, lo:lo + P]), v, act.now(), *free)
                v = dve.do(lambda e, ps=ps, mask=mask: e.copy_predicated(
                    S, mask.bitcast(U32).unsqueeze(1).broadcast_to([P, 8, P]),
                    ps.rearrange("p (a b) -> p a b", b=P)), done)
                banks.release(at, 2, v)
            a = act.do(lambda e: e.activation(E, B, ACT.Exp), dve.now())
            dve.do(lambda e: e.tensor_tensor(QE, zq, E, ALU.mult), a)
            view = lambda a: a.rearrange("p (m b) -> p m b", b=HG_C)
            last = view(B)[:, :, HG_C - 1:HG_C]
            v = dve.do(lambda e: e.tensor_tensor(view(E), last.broadcast_to([P, 16, HG_C]), view(B), ALU.subtract))
            act.do(lambda e: e.activation(E, E, ACT.Exp), v)
            a = act.do(lambda e: e.activation(EL.unsqueeze(2), last, ACT.Exp))
            v = dve.do(lambda e: e.tensor_tensor(KL, K, E, ALU.mult), a, pe.now())
            for t in range(TT):
                turn([KL[:, hd * T + t * P:hd * T + (t + 1) * P] for hd in range(HG_H)], [v],
                     copy_evac(act, KT[:, t, :]))
            for t in range(TT):
                at, ps, free = banks.take()
                for hd in range(HG_H):
                    done = pe.do(mm(ps[:, hd * P:(hd + 1) * P], S[:, 2 * hd + t, :], zi[:, t, hd * P:(hd + 1) * P]),
                                 dve.now(), *free)
                a = act.do(lambda e, ps=ps, t=t: e.activation(O[:, t, :], ps, ACT.Copy), done)
                banks.release(at, 1, a)
            dve.do(lambda e: e.memset(state, 0.0))
            for n in range(T // HG_C):
                t, lo = n // 2, HG_C * (n % 2)
                if n:
                    at, ps, free = banks.take()
                    for hd in range(HG_H):
                        done = pe.do(mm(ps[lo:lo + HG_C, hd * P:(hd + 1) * P],
                                        QE[:, hd * T + n * HG_C:hd * T + (n + 1) * HG_C], state[:, hd, :]),
                                     dve.now(), *free)
                    v = dve.do(lambda e, ps=ps, t=t, lo=lo: e.tensor_tensor(
                        O[lo:lo + HG_C, t, :], O[lo:lo + HG_C, t, :], ps[lo:lo + HG_C, :], ALU.add), done, act.now())
                    banks.release(at, 1, v)
                if n < T // HG_C - 1:
                    at, ps, free = banks.take()
                    for hd in range(HG_H):
                        done = pe.do(mm(ps[:, hd * P:(hd + 1) * P], KT[lo:lo + HG_C, t, hd * P:(hd + 1) * P],
                                        zi[lo:lo + HG_C, t, hd * P:(hd + 1) * P]), act.now(), *free)
                    for hd in range(HG_H):
                        at_l = hd * 4 + n
                        v = dve.do(lambda e, ps=ps, hd=hd, at_l=at_l: e.scalar_tensor_tensor(
                            out=state[:, hd, :], in0=state[:, hd, :], scalar=EL[:, at_l:at_l + 1],
                            in1=ps[:, hd * P:(hd + 1) * P], op0=ALU.mult, op1=ALU.add), done)
                    banks.release(at, 1, v)
            Of = O.rearrange("p t n -> p (t n)")
            O8 = Of.rearrange("p (a b) -> p a b", b=P)
            dve.do(lambda e: e.tensor_tensor(E, Of, Of, ALU.mult))
            v = dve.do(lambda e: e.tensor_reduce(EL[:, 0:8], E.rearrange("p (a b) -> p a b", b=P), AX.X, ALU.add))
            a = act.do(lambda e: e.activation(EL[:, 8:16], EL[:, 0:8], ACT.Sqrt, scale=1.0 / P, bias=c("eps")), v)
            dve.do(lambda e: e.reciprocal(EL[:, 0:8], EL[:, 8:16]), a)
            dve.do(lambda e: e.tensor_tensor(O8, O8, EL[:, 0:8].unsqueeze(2).broadcast_to([P, 8, P]), ALU.mult))
            dve.do(lambda e: e.tensor_tensor(
                zg, zg, r(ROWS_1, "hgrn_gnorm_g").unsqueeze(1).broadcast_to([P, TT, 512]), ALU.mult), g)
            dve.do(lambda e: e.tensor_tensor(mixed[:, :, 0:512], O, zg, ALU.mult))

        def windows():
            W = cut(4, T)
            PT = cut(TT, 512)
            stats = cut(8)
            for t in range(TT):
                length = (t + 1) * P

                def products(ps, needs, t=t, length=length):
                    for hd in (0, 2, 1, 3):
                        j, lo = hd // 2, SW_D * (hd % 2)
                        done = pe.do(mm(ps[:, hd * length:(hd + 1) * length], zb[lo:lo + SW_D, j, t * P:(t + 1) * P],
                                        zb[lo:lo + SW_D, 2 + j, 0:length]), *needs, rows_from(lo))
                    return done

                w = W[:, :, 0:length]
                v = softmax(products, SW_H, length, SW_D ** -0.5, sw_add[:, t, 0:length], sw_held[:, t, 0:length],
                            None, w, [pe.now()], stats)
                for k in range(t + 1):
                    turn([w[:, hd, k * P:(k + 1) * P] for hd in range(SW_H)], [v], copy_evac(act, PT[:, k, :]))
                at, ps, free = banks.take()
                for hd in range(SW_H):
                    for k in range(t + 1):
                        done = pe.do(mm(ps[:, hd * SW_D:(hd + 1) * SW_D], PT[:, k, hd * P:(hd + 1) * P],
                                        zv[:, k, hd * SW_D:(hd + 1) * SW_D], k == 0, k == t), act.now(), *free)
                v = dve.do(lambda e, ps=ps, t=t: e.tensor_copy(mixed[:, t, 512:768], ps[:, 0:256]), done)
                banks.release(at, 1, v)

        def rwkv():
            CM = cut(8, T)
            two = lambda: cut(512)
            A, LW, B, KK, PX, AB, KB, R, K2, X1, X2, X3 = (two() for _ in range(12))
            VT, ABT, KBT, G, Y = (cut(TT, T) for _ in range(5))
            S0 = cut(2, RK_N)
            U, RH = cut(T), cut(T)
            EL, BS = cut(8), cut(8)
            MT, NT, RAT, RKT, MX, MXT, Y1, ML = (cut(8, P) for _ in range(8))
            flat = lambda a: a.rearrange("p a b -> p (a b)")
            place = lambda hd, t: (hd % 2) * 4 + (hd // 2) * 2 + t
            dve.do(lambda e: e.tensor_tensor(CM[:, :, 1:T], zc[:, :, 0:T - 1], zc[:, :, 1:T], ALU.subtract))
            dve.do(lambda e: e.tensor_scalar(CM[:, :, 0:1], zc[:, :, 0:1], -1.0, None, ALU.mult))
            for k in range(8):
                dve.do(lambda e, k=k: e.scalar_tensor_tensor(out=CM[:, k, :], in0=CM[:, k, :], scalar=c("rwkv_mu", k),
                                                             in1=zc[:, k, :], op0=ALU.mult, op1=ALU.add))
            cm_done = dve.now()
            rr, kk, vv = (CM[:, 2 * n:2 * n + 2, :] for n in range(3))
            rr, kk = flat(rr), flat(kk)
            th, sg = X1[:, 0:T], X1[:, T:2 * T]
            act.do(lambda e: e.activation(th[0:64, :], CM[0:64, 6, :], ACT.Tanh), cm_done)
            a = act.do(lambda e: e.activation(sg, CM[:, 7, :], ACT.Sigmoid))
            wa, g2 = lora[:, 0:256], lora[:, 256:512]
            at, ps, free = banks.take(2)
            for j in range(2):
                pe.do(mm(ps[:, j * T:(j + 1) * T], wa[0:64, j * P:(j + 1) * P], th[0:64, :]), a, *free)
            for j in range(2):
                done = pe.do(mm(ps[:, 512 + j * T:512 + (j + 1) * T], wa[64:128, j * P:(j + 1) * P], CM[64:128, 6, :]))
            for j in range(2):
                act.do(lambda e, j=j, ps=ps: e.activation(LW[:, j * T:(j + 1) * T], ps[:, j * T:(j + 1) * T], ACT.Sigmoid,
                                                   bias=c("rwkv_w0", j)), done)
                a = act.do(lambda e, j=j, ps=ps: e.activation(A[:, j * T:(j + 1) * T], ps[:, 512 + j * T:512 + (j + 1) * T],
                                                       ACT.Sigmoid, bias=c("rwkv_a0", j)))
            banks.release(at, 2, a)
            gate_at, gps, free = banks.take()
            for t in range(TT):
                gdone = pe.do(mm(gps[:, t * T:(t + 1) * T], sg[:, t * P:(t + 1) * P], g2), *free)
            g_tok = act.do(lambda e: e.activation(flat(G), gps, ACT.Copy), gdone)
            banks.release(gate_at, 1, g_tok)
            dve.do(lambda e: e.tensor_scalar(LW, LW, -RK_DECAY_SCALE, None, ALU.mult), a)
            dve.do(lambda e: e.tensor_tensor_scan(B, restart[:, 0:512], LW, 0.0, ALU.mult, ALU.add))
            for j in range(2):
                s = slice(j * T, (j + 1) * T)
                dve.do(lambda e, s=s, j=j: e.tensor_scalar(KK[:, s], kk[:, s], c("rwkv_k_k", j), None, ALU.mult))
            v = dve.do(lambda e: e.tensor_tensor(X2, KK, KK, ALU.mult))
            at, ps, free = banks.take()
            done = pe.do(mm(ps, head_ones, X2), v, *free)
            a = act.do(lambda e, ps=ps: e.activation(X2, ps, ACT.Sqrt), done)
            banks.release(at, 1, a)
            dve.do(lambda e: e.tensor_scalar(X2, X2, 1e-12, None, ALU.max), a)
            dve.do(lambda e: e.reciprocal(X2, X2))
            dve.do(lambda e: e.tensor_tensor(KK, KK, X2, ALU.mult))
            for j in range(2):
                s = slice(j * T, (j + 1) * T)
                dve.do(lambda e, s=s, j=j: e.tensor_scalar(K2[:, s], A[:, s], 1.0, c("rwkv_k_a", j), ALU.subtract,
                                                           ALU.mult))
            dve.do(lambda e: e.scalar_tensor_tensor(out=K2, in0=K2, scalar=1.0, in1=kk, op0=ALU.add, op1=ALU.mult))
            v = dve.do(lambda e: e.tensor_tensor(X2, B, LW, ALU.subtract))
            act.do(lambda e: e.activation(X2, X2, ACT.Exp), v)
            act.do(lambda e: e.activation(X3, B, ACT.Exp))
            last = B.rearrange("p (m b) -> p m b", b=RK_C)[:, :, RK_C - 1:RK_C]
            act.do(lambda e: e.activation(EL.unsqueeze(2), last, ACT.Exp))
            a = act.do(lambda e: e.activation(X1, B, ACT.Exp, scale=-1.0), gdone)
            dve.do(lambda e: e.tensor_tensor(PX, KK, X2, ALU.mult), a)
            dve.do(lambda e: e.tensor_tensor(R, rr, X3, ALU.mult))
            dve.do(lambda e: e.tensor_tensor(KB, K2, X1, ALU.mult))
            dve.do(lambda e: e.tensor_tensor(AB, KK, A, ALU.mult))
            v = dve.do(lambda e: e.tensor_tensor(AB, AB, X1, ALU.mult))
            for src, dst in ((flat(vv), VT), (AB, ABT), (KB, KBT)):
                turn([src[:, j * T + t * P:j * T + (t + 1) * P] for t in range(TT) for j in range(2)], [v],
                     copy_evac(act, flat(dst)))
            turned = act.now()
            for j in range(2):
                s = slice(j * T, (j + 1) * T)
                dve.do(lambda e, s=s, j=j: e.scalar_tensor_tensor(out=X2[:, s], in0=rr[:, s], scalar=c("rwkv_r_k", j),
                                                                  in1=K2[:, s], op0=ALU.mult, op1=ALU.mult))
            v = dve.now()
            at, ps, free = banks.take()
            for t in range(TT):
                for j in range(2):
                    lo = t * 4 + 2 * j
                    done = pe.do(mm(ps[:, lo:lo + 2], X2[:, j * T + t * P:j * T + (t + 1) * P], head_pick), v, *free)
            v = dve.do(lambda e, ps=ps: e.tensor_copy(BS, ps[:, 0:8]), done)
            banks.release(at, 1, v)
            for dst, left, right, mask in ((MT, AB, PX, strict), (NT, KB, PX, strict), (RAT, AB, R, inclusive),
                                           (RKT, KB, R, inclusive)):
                at, ps, free = banks.take(2)
                for hd in range(RK_H):
                    j, lo = hd // 2, RK_N * (hd % 2)
                    for t in range(TT):
                        s = slice(j * T + t * P, j * T + (t + 1) * P)
                        i = place(hd, t)
                        done = pe.do(mm(ps[:, i * P:(i + 1) * P], left[lo:lo + RK_N, s], right[lo:lo + RK_N, s]), *free)
                v = dve.do(lambda e, ps=ps, dst=dst, mask=mask: e.tensor_tensor(
                    dst, ps.rearrange("p (a b) -> p a b", b=P), mask.unsqueeze(1).broadcast_to([P, 8, P]), ALU.mult),
                    done)
                banks.release(at, 2, v)
            eye8 = ident.unsqueeze(1).broadcast_to([P, 8, P])
            dve.do(lambda e: e.tensor_copy(MX, eye8))
            dve.do(lambda e: e.tensor_copy(MXT, eye8))
            for level in range(LEVELS):
                v = dve.do(lambda e, level=level: e.tensor_tensor(
                    ML, MT, masks[:, level, :].unsqueeze(1).broadcast_to([P, 8, P]), ALU.mult), pe.now())
                at, ps, free = banks.take(2)
                for i in range(8):
                    done = pe.do(mm(ps[:, i * P:(i + 1) * P], ML[:, i, :], MX[:, i, :]), v, *free)
                a = act.do(lambda e, ps=ps: e.activation(flat(Y1), ps, ACT.Copy), done)
                banks.release(at, 2, a)
                for dst, left, right in ((MX, MXT, Y1), (MXT, Y1, MXT)):
                    at, ps, free = banks.take(2)
                    for i in range(8):
                        done = pe.do(mm(ps[:, i * P:(i + 1) * P], left[:, i, :], right[:, i, :]), a, *free)
                    dst_done = (at, ps, dst, done)
                    if dst is MX:
                        first_half = dst_done
                for at, ps, dst, done in (first_half, dst_done):
                    v = dve.do(lambda e, ps=ps, dst=dst: e.tensor_tensor(flat(dst), flat(dst), ps, ALU.subtract),
                               dst_done[3])
                    banks.release(at, 2, v)
            dve.do(lambda e: e.memset(S0, 0.0))
            for n in range(T // RK_C):
                t, lo = n // 2, RK_C * (n % 2)
                tok = slice(lo, lo + RK_C)
                heads = [(hd, hd // 2, RK_N * (hd % 2)) for hd in (0, 2, 1, 3)]
                col_of = lambda j, n=n: slice(j * T + n * RK_C, j * T + (n + 1) * RK_C)
                vs = lambda hd: slice(hd * RK_N, (hd + 1) * RK_N)
                at, ps, free = banks.take()
                ready = dve.now()
                for hd, j, kb in heads:
                    done = pe.do(mm(ps[tok, vs(hd)], PX[kb:kb + RK_N, col_of(j)], S0[kb:kb + RK_N, j, :], hd == 0, False),
                                 ready, *free, rows_from(kb))
                for hd, j, kb in heads:
                    done = pe.do(mm(ps[tok, vs(hd)], NT[tok, place(hd, t), tok], VT[tok, t, vs(hd)], False, True), done,
                                 rows_from(lo))
                v = dve.do(lambda e, ps=ps, tok=tok: e.tensor_scalar(RH[tok, :], ps[tok, 0:T], -1.0, None, ALU.mult),
                           done)
                banks.release(at, 1, v)
                at, ps, free = banks.take()
                for hd, j, kb in heads:
                    done = pe.do(mm(ps[tok, vs(hd)], MXT[tok, place(hd, t), tok], RH[tok, vs(hd)]), v, *free, rows_from(lo))
                v = dve.do(lambda e, ps=ps, tok=tok: e.tensor_copy(U[tok, :], ps[tok, 0:T]), done)
                banks.release(at, 1, v)
                at, ps, free = banks.take()
                for hd, j, kb in heads:
                    done = pe.do(mm(ps[tok, vs(hd)], R[kb:kb + RK_N, col_of(j)], S0[kb:kb + RK_N, j, :], hd == 0, False),
                                 *free, rows_from(kb))
                for hd, j, kb in heads:
                    pe.do(mm(ps[tok, vs(hd)], RAT[tok, place(hd, t), tok], U[tok, vs(hd)], False, False), done, v, rows_from(lo))
                    ydone = pe.do(mm(ps[tok, vs(hd)], RKT[tok, place(hd, t), tok], VT[tok, t, vs(hd)], False, True))
                a = act.do(lambda e, ps=ps, tok=tok, t=t: e.activation(Y[tok, t, :], ps[tok, 0:T], ACT.Copy), ydone)
                banks.release(at, 1, a)
                if n < T // RK_C - 1:
                    at, ps, free = banks.take()
                    for hd, j, kb in heads:
                        o = ps[kb:kb + RK_N, j * RK_N:(j + 1) * RK_N]
                        pe.do(mm(o, ABT[tok, t, vs(hd)], U[tok, vs(hd)], True, False), *free)
                        done = pe.do(mm(o, KBT[tok, t, vs(hd)], VT[tok, t, vs(hd)], False, True))
                    dve.do(lambda e, ps=ps: e.tensor_tensor(flat(S0), flat(S0), ps[:, 0:P], ALU.add), done)
                    e_last = EL.rearrange("p (j n) -> p j n", j=2)[:, :, n:n + 1].broadcast_to([P, 2, RK_N])
                    v = dve.do(lambda e, e_last=e_last: e.tensor_tensor(S0, S0, e_last, ALU.mult))
                    banks.release(at, 1, v)
            Y8 = flat(Y).rearrange("p (a b) -> p a b", b=RK_N)
            wide = lambda a: a.unsqueeze(2).broadcast_to([P, 8, RK_N])
            m, sq = EL, X1.rearrange("p (a b) -> p a b", b=RK_N)
            dve.do(lambda e: e.tensor_reduce(m, Y8, AX.X, ALU.add), act.now())
            dve.do(lambda e: e.tensor_scalar(m, m, 1.0 / RK_N, None, ALU.mult))
            dve.do(lambda e: e.tensor_tensor(Y8, Y8, wide(m), ALU.subtract))
            dve.do(lambda e: e.tensor_tensor(sq, Y8, Y8, ALU.mult))
            v = dve.do(lambda e: e.tensor_reduce(m, sq, AX.X, ALU.add))
            a = act.do(lambda e: e.activation(m, m, ACT.Sqrt, scale=1.0 / RK_N, bias=c("gn_eps")), v)
            dve.do(lambda e: e.reciprocal(m, m), a)
            dve.do(lambda e: e.tensor_tensor(Y8, Y8, wide(m), ALU.mult))
            across = lambda name: r(ROWS_1, name).unsqueeze(1).broadcast_to([P, TT, T])
            dve.do(lambda e: e.tensor_tensor(Y, Y, across("rwkv_ln_w"), ALU.mult))
            dve.do(lambda e: e.tensor_tensor(Y, Y, across("rwkv_ln_b"), ALU.add))
            dve.do(lambda e: e.tensor_tensor(sq, flat(VT).rearrange("p (a b) -> p a b", b=RK_N), wide(BS), ALU.mult),
                   turned)
            dve.do(lambda e: e.tensor_tensor(Y8, Y8, sq, ALU.add))
            dve.do(lambda e: e.tensor_tensor(mixed[:, :, 768:1024], Y, G, ALU.mult), g_tok)

        hgrn()
        fence()
        used[0] = base
        windows()
        fence()
        used[0] = base
        rwkv()
        fence()

        plain = lambda k: c("one")

        sp_out = [0]

        t = feature_major(mixed, plain, [dve.now()])
        summed = add_projection("w_out", *t)
        fence()

        def ffn():
            phase("ffn", ("GT_hi", [P, NF, T], F32R), ("GT_lo", [P, NF, T], F32R), ("arena", [P, 8192], F32))
            GT_hi, GT_lo = places["GT_hi"], places["GT_lo"]
            UC = cut(2, 4, T)
            GV = cut(2, 512)
            scaled = rms_scale(h)
            t = feature_major(xn, lambda k: c("norm_ffn_g", k), [scaled])
            first, count = multiply("ffn_up", False, *t)
            tap0 = COLS["ffn_conv"][0]
            s_tap, s_sum, s_gv, s_gt = (sem(n) for n in ("s_tap", "s_sum", "s_gv", "s_gt"))

            def newest_tap(e, slot, m):
                i = m - first
                e.wait_ge(s_use, m * UNITS + UNITS)
                if not isinstance(i, int) or i > 1:
                    e.wait_ge(s_gv, i - 1)
                for piece in range(4):
                    at = i * 16 + (tap0 + 4 * piece)
                    last = e.activation(UC[:, slot, piece, :], ps_chunk[slot][:, piece * T:(piece + 1) * T],
                                        ACT.Identity, scale=col[:, bass.ds(at + 2, 1)], bias=col[:, bass.ds(at + 3, 1)])
                    if piece % 2:
                        last.then_inc(s_tap, 1)

            def older_taps(e, slot, m):
                i = m - first
                for lag in (1, 2):
                    for piece in range(4):
                        at = i * 16 + (tap0 + 4 * piece)
                        if lag == 1 and piece % 2 == 0:
                            e.wait_ge(s_tap, i * 2 + (piece // 2 + 1))
                        if lag == 2:
                            e.wait_ge(s_sum, i * 8 + (piece + 1))
                        o = UC[:, slot, piece, lag:T]
                        e.scalar_tensor_tensor(out=o, in0=ps_chunk[slot][:, piece * T:(piece + 1) * T - lag],
                                               scalar=col[:, bass.ds(at + (2 - lag), 1)], in1=o, op0=ALU.mult,
                                               op1=ALU.add).then_inc(s_sum, 1)
                e.wait_ge(s_sum, i * 8 + 8)
                e.sem_inc(s_ev, 1)

            def gate_silu(e, slot, m):
                i = m - first
                e.wait_ge(s_sum, i * 8 + 8)
                gates = UC[:, slot, 0:2, :]
                e.activation(gates, gates, ACT.Silu).then_inc(s_tap2, 1)
                e.wait_ge(s_gv, i + 1)
                e.activation(GT_hi[:, bass.ds(i * 2, 2), :], GV[:, slot, :].rearrange("p (a t) -> p a t", a=2),
                             ACT.Copy).then_inc(s_gt, 1)

            s_tap2 = sem("s_silu")

            def gated(e, slot, m):
                i = m - first
                e.wait_ge(s_tap2, i + 1)
                gv = GV[:, slot, :].rearrange("p (a t) -> p a t", a=2)
                e.tensor_tensor(gv, UC[:, slot, 0:2, :], UC[:, slot, 2:4, :], ALU.mult).then_inc(s_gv, 1)
                e.wait_ge(s_gt, i + 1)
                e.tensor_tensor(GT_lo[:, bass.ds(i * 2, 2), :], gv, GT_hi[:, bass.ds(i * 2, 2), :].bitcast(F32),
                                ALU.subtract).then_inc(s_gl, 1)

            s_gl = sem("s_gl")
            split_chunks(first, count, act_hooks=(newest_tap, gate_silu), dve_hooks=(older_taps, gated))
            ffn_down(GT_hi, GT_lo, (s_gl, count))

        def ffn_down(GT_hi, GT_lo, ready):
            first, count = STREAM["ffn_down, ple_proj"]
            PL = cut(2 * T)
            got = load("p", PL, p_t)
            act.wait(got)
            dve.wait(got)
            for lane in (act, dve):
                lane.wait((s_use, UNITS * first))
            into_p = into_x(PL, 0, plain, [])
            split_chunks(first, count)
            pe.wait(ready, *[x for b in range(4) for x in banks.free[b]])

            def rows_of(e, u, x, k, begin, end):
                e.wait_ge(s_lo, UNITS * first + u + 1)
                for t in range(TT):
                    for half in range(2):
                        last = product3(e, ps_misc[:, 2 * t + half, :], [a[:, k, t * P:(t + 1) * P] for a in x],
                                        [w[u % 2][:, half * CW:(half + 1) * CW] for w in (w_hi, w_lo)], begin, end)
                last.then_inc(s_use, 1)

            def down(e):
                for k in range(NF):
                    rows_of(e, k, (GT_hi, GT_lo), k, k == 0, k == NF - 1)

            def proj(e):
                for k in range(2):
                    rows_of(e, NF + k, (x_hi, x_lo), k, k == 0, k == 1)

            pe.steps.append(down)
            dve.wait((s_use, UNITS * first + NF))
            sums = ps_misc[:, :, :].rearrange("p b n -> p (b n)")
            hf = h[:, :, :].rearrange("p t n -> p (t n)")
            v = dve.do(lambda e: e.tensor_tensor(hf, hf, sums, ALU.add))
            pe.wait(v, *into_p)
            pe.steps.append(proj)
            act.wait((s_use, UNITS * (first + count)))
            places["ple"] = cut(2 * D)
            a = act.do(lambda e: e.activation(places["ple"], sums, ACT.Copy))
            act.quiet(lambda e: e.sem_inc(s_ev, count), a)
            fence()
        ffn()
        def ple_and_norm():
            ple = places["ple"]
            gate = cut(TT, D)
            have_gain = load("gain", row[:, :], rows[1:2, :].broadcast_to([P, D]))
            scaled = rms_scale(h)
            t = feature_major(xn, lambda k: c("norm_ple_g", k), [scaled])
            first, count = multiply("ple_gate", True, *t)

            def hook(e, slot, m):
                e.wait_ge(s_use, m * UNITS + UNITS)
                at = (m - first) * CW
                e.activation(gate[:, :, at:at + CW], ps_chunk[slot][:, :].rearrange("p (t n) -> p t n", t=TT),
                             ACT.Sigmoid).then_inc(s_ev, 1)

            split_chunks(first, count, act_hooks=(hook,))
            gf = gate.rearrange("p t n -> p (t n)")
            hf = h[:, :, :].rearrange("p t n -> p (t n)")
            dve.do(lambda e: e.tensor_tensor(gf, gf, ple, ALU.mult), (s_ev, first + count))
            v = dve.do(lambda e: e.tensor_tensor(hf, hf, gf, ALU.add))
            rms_scale(h, v)
            dve.do(lambda e: e.tensor_tensor(h[:, :, :], xn[:, :, :], row[:, :].unsqueeze(1)
                                             .broadcast_to([P, TT, D]), ALU.mult), have_gain)
            fence()
        ple_and_norm()
        def mixers_2():
            phase("mixers_2", ("arena", [P, P * T], F32))
            Z2 = cut(5, 1024)
            cmpw1, cmpw2 = cut(2, 16, P), cut(2 * NSA_D)
            load("second", cmpw1.rearrange("p a b c -> p (a b c)"), cmp_w1)
            load("second", cmpw2, cmp_w2)
            k2 = cut(consts2.shape[1])
            pos_raw = cut(TT)
            load("second", k2, consts2)
            load("second", pos_raw.bitcast(I32), positions)
            have = load("second", row[:, :], rows[2:3, :].broadcast_to([P, D]))
            act.wait(have)
            pe.wait(have)
            dve.wait(have)
            causal = k2[:, 0:512].rearrange("p (t n) -> p t n", t=TT)
            seen = k2[:, 512:544].rearrange("p (t n) -> p t n", t=TT)
            seen_add = k2[:, 544:576].rearrange("p (t n) -> p t n", t=TT)
            inv = k2[:, 576:584]
            scaled = rms_scale(h)
            t = feature_major(xn, lambda k: c("mix_norm_g_2", k), [scaled])
            first, _ = multiply("w_in_2 feature", False, *t)
            multiply("w_in_2 token", True)
            split_chunks(first, 5, act_hooks=(copy_hook(first, chunk_rows(Z2)),))
            got = [(s_ev, first + 5)] * 5
            convolved = conv_module(Z2, got)
            nsa(Z2, got, causal, seen, seen_add, inv, pos_raw, cmpw1, cmpw2)
            conv_norm(convolved)

        def conv_module(Z2, got):
            pad = CONV_K - 1
            U = cut(CONV_T, T + pad)
            Y = cut(CONV_T, T)
            tiles = lambda n: Z2[:, n, :].rearrange("p (k t) -> p k t", t=T)
            a = act.do(lambda e: e.activation(Z2[:, 1, :], Z2[:, 1, :], ACT.Sigmoid), got[1])
            dve.do(lambda e: e.memset(U[:, :, 0:pad], 0.0))
            dve.do(lambda e: e.tensor_tensor(U[:, :, pad:pad + T], tiles(0), tiles(1), ALU.mult), a, got[0])
            tap0 = COLS["conv_dw_w_2"][0]
            for k in range(CONV_T):
                dve.do(lambda e, k=k: e.tensor_scalar(Y[:, k, :], U[:, k, 0:T], col[:, tap0 + k:tap0 + k + 1],
                                                      c("conv_dw_b_2", k), ALU.mult, ALU.add))
            before = dve.n - CONV_T

            def taps(e):
                with e.Fori(1, CONV_K) as j:
                    for k in range(CONV_T):
                        e.wait_ge(dve.sem, j * CONV_T + (before - CONV_T + k + 1))
                        e.scalar_tensor_tensor(out=Y[:, k, :], in0=U[:, k, bass.ds(j, T)],
                                               scalar=col[:, bass.ds(j * CONV_T + (tap0 + k), 1)], in1=Y[:, k, :],
                                               op0=ALU.mult, op1=ALU.add).then_inc(dve.sem, 1)

            dve.steps.append(taps)
            dve.n += CONV_T * (CONV_K - 1)
            return Y, dve.now()

        def conv_norm(convolved):
            Y, ready = convolved
            YT, SQ = (xn[:, i, :].rearrange("p (t n) -> p t n", t=TT) for i in range(2))
            st = cut(8)
            for t in range(TT):
                turn([Y[:, k, t * P:(t + 1) * P] for k in range(CONV_T)], [ready], copy_evac(act, YT[:, t, :]))
            m, q = st[:, 0:2], st[:, 2:4]
            wide = lambda a: a.unsqueeze(2).broadcast_to([P, TT, 512])
            dve.do(lambda e: e.tensor_reduce(m, YT, AX.X, ALU.add), act.now())
            dve.do(lambda e: e.tensor_scalar(m, m, 1.0 / 512, None, ALU.mult))
            dve.do(lambda e: e.tensor_tensor(YT, YT, wide(m), ALU.subtract))
            dve.do(lambda e: e.tensor_tensor(SQ, YT, YT, ALU.mult))
            v = dve.do(lambda e: e.tensor_reduce(q, SQ, AX.X, ALU.add))
            a = act.do(lambda e: e.activation(q, q, ACT.Sqrt, scale=1.0 / 512, bias=c("eps")), v)
            dve.do(lambda e: e.reciprocal(q, q), a)
            v = dve.do(lambda e: e.tensor_tensor(YT, YT, wide(q), ALU.mult))
            SF = SQ.rearrange("p t n -> p (t n)")
            for b in range(2):
                def evac(ps, done, b=b):
                    for i in range(2):
                        k = 2 * b + i
                        last = act.do(lambda e, k=k, i=i: e.activation(
                            SF[:, k * T:(k + 1) * T], ps[:, i * T:(i + 1) * T], ACT.Silu, scale=c("conv_ln_g_2", k),
                            bias=c("conv_ln_b_2", k)), done, own=False)
                    return (last,)
                turn([YT[:, t, k * P:(k + 1) * P] for k in (2 * b, 2 * b + 1) for t in range(TT)], [v], evac)
            into_x(SF, 0, plain, [act.now()])

        def nsa(Z2, got, causal, seen, seen_add, inv, pos_raw, cmpw1, cmpw2):
            zq = Z2[:, 2, :].rearrange("p (t h d) -> p t h d", t=TT, h=NSA_H)
            zkv = Z2[:, 3, :].rearrange("p (t n) -> p t n", t=TT)
            zw = Z2[:, 4, :].rearrange("p (t n) -> p t n", t=TT)
            rope_at = cut(TT)
            angle, CS, N1 = cut(TT, 8), cut(2, TT, 8), cut(TT, 8)
            QR = cut(1024)
            QU, QT = cut(NSA_H, T), cut(NSA_H, T)
            KST, KWT = cut(NSA_G, T), cut(NSA_G, T)
            GA = cut(TT, 24)
            W = [cut(4, T) for _ in range(2)]
            stats = [cut(16) for _ in range(2)]
            PT = cut(4, NSA_H * P)
            PC, PCT = cut(NSA_H, P), cut(NSA_H * P)
            VC = cut(NSA_G, NSA_D)
            NS = cut(TT, 512)
            R4 = cut(4, 128)
            for n in (2, 3, 4):
                dve.wait(got[n])
            dve.do(lambda e: e.tensor_copy(rope_at, pos_raw.bitcast(I32)))
            dve.do(lambda e: e.tensor_tensor(angle, rope_at.unsqueeze(2).broadcast_to([P, TT, 8]),
                                             inv.unsqueeze(1).broadcast_to([P, TT, 8]), ALU.mult))
            two_pi, high = 2 * np.pi, 6.28125
            magic = 1.5 * 2.0 ** 23
            for i, quarter in ((0, 0.25), (1, 0.0)):
                dve.do(lambda e, quarter=quarter: e.tensor_scalar(N1, angle, 1 / two_pi, quarter, ALU.mult, ALU.add))
                dve.do(lambda e: e.tensor_scalar(N1, N1, magic, None, ALU.add))
                dve.do(lambda e: e.tensor_scalar(N1, N1, -magic, None, ALU.add))
                dve.do(lambda e, i=i: e.scalar_tensor_tensor(out=CS[:, i, :, :], in0=N1, scalar=-high, in1=angle,
                                                             op0=ALU.mult, op1=ALU.add))
                dve.do(lambda e, i=i: e.scalar_tensor_tensor(out=CS[:, i, :, :], in0=N1, scalar=high - two_pi,
                                                             in1=CS[:, i, :, :], op0=ALU.mult, op1=ALU.add))
                dve.do(lambda e, i=i, quarter=quarter: e.tensor_scalar(CS[:, i, :, :], CS[:, i, :, :],
                                                                       quarter * two_pi, None, ALU.add))
            flat_cs = CS.rearrange("p i t d -> p (i t d)")
            v = dve.do(lambda e: e.tensor_scalar(flat_cs, flat_cs, 3.1415925, -3.1415925, ALU.min, ALU.max))
            cs_ready = act.do(lambda e: e.activation(flat_cs, flat_cs, ACT.Sin), v)
            gates_ready = act.do(lambda e: e.activation(GA, zw[:, :, 256:280], ACT.Sigmoid))

            def heads_turned(src, count, dst, needs):
                for hd in range(0, count, 2):
                    turn([src(hd + i, t) for i in range(2) for t in range(TT)], needs,
                         copy_evac(act, dst[0:64, hd:hd + 2, :].rearrange("p h t -> p (h t)")), rows_out=64)

            heads_turned(lambda hd, t: zq[:, t, hd, :], NSA_H, QU, [got[2]])

            def rope(x, count):
                r4 = [R4[:, i, 0:TT * count * 8].rearrange("p (t h d) -> p t h d", t=TT, h=count) for i in range(4)]
                x1, x2 = x[:, :, :, 0:8], x[:, :, :, 8:16]
                cos, sin = (CS[:, i, :, :].unsqueeze(2).broadcast_to([P, TT, count, 8]) for i in range(2))
                dve.wait(cs_ready)
                for o, a, b in ((r4[0], x1, cos), (r4[1], x2, sin), (r4[2], x2, cos), (r4[3], x1, sin)):
                    dve.do(lambda e, o=o, a=a, b=b: e.tensor_tensor(o, a, b, ALU.mult))
                dve.do(lambda e: e.tensor_tensor(x1, r4[0], r4[1], ALU.subtract))
                return dve.do(lambda e: e.tensor_tensor(x2, r4[2], r4[3], ALU.add))

            dve.do(lambda e: e.tensor_copy(QR, Z2[:, 2, :]))
            qr = QR.rearrange("p (t h d) -> p t h d", t=TT, h=NSA_H)
            group = lambda z, at: z[:, :, at:at + 128].rearrange("p t (g d) -> p t g d", g=NSA_G)
            v = rope(qr, NSA_H)
            heads_turned(lambda hd, t: qr[:, t, hd, :], NSA_H, QT, [v])
            ks, kw = group(zkv, 256), group(zw, 0)
            v = rope(ks, NSA_G)
            heads_turned(lambda g, t: ks[:, t, g, :], NSA_G, KST, [v])
            v = rope(kw, NSA_G)
            heads_turned(lambda g, t: kw[:, t, g, :], NSA_G, KWT, [v])

            KD2 = cut(TT, 4, 128)
            XK = cut(4, T)
            X = cut(2, 16, 30)
            HD, KCT = cut(60), cut(30)
            for copy in range(2):
                v = dve.do(lambda e, copy=copy: e.tensor_copy(
                    KD2[:, :, :, copy * 64:copy * 64 + 64], zkv[:, :, 0:256].rearrange("p t (m d) -> p t m d", d=64)))
            dve.do(lambda e: e.memset(VC, 0.0))
            dve.do(lambda e: e.memset(PC, 0.0))
            for m in (0, 2):
                def evac(ps, done, m=m):
                    ps = ps.rearrange("p (m t) -> p m t", t=T)
                    act.do(lambda e: e.activation(XK[0:64, m:m + 2, :], ps[0:64, :, :], ACT.Copy), done)
                    return (act.do(lambda e: e.activation(XK[64:128, m:m + 2, 0:T - 1], ps[64:128, :, 1:T], ACT.Copy)),)
                turn([KD2[:, t, i, :] for i in (m, m + 1) for t in range(TT)], [v], evac)
            for kv in range(2):
                for mh in range(2):
                    x_in = XK[:, 2 * kv:2 * kv + 2, 16 * mh:16 * mh + 240].rearrange(
                        "p g (c m two) -> p m g c two", c=N_CMP, two=2)[:, :, :, :, 0]
                    pos = c("cmp_pos_2", kv * 16 + mh * 8, 8).unsqueeze(2).unsqueeze(3).broadcast_to([P, 8, 2, N_CMP])
                    x_out = X[:, kv, mh * 8:mh * 8 + 8, :].rearrange("p m (g c) -> p m g c", g=2)
                    v = dve.do(lambda e, x_in=x_in, pos=pos, x_out=x_out: e.tensor_tensor(x_out, x_in, pos, ALU.add),
                               act.now())
            at, ps, free = banks.take()
            for kv in range(2):
                for m in range(16):
                    done = pe.do(mm(ps[:, kv * 30:kv * 30 + 30], cmpw1[:, kv, m, :], X[:, kv, m, :], m == 0, m == 15),
                                 v, *free)
            for kv in range(2):
                a = act.do(lambda e, kv=kv, ps=ps: e.activation(
                    HD[:, kv * 30:kv * 30 + 30], ps[:, kv * 30:kv * 30 + 30], ACT.Gelu_apprx_tanh,
                    bias=c("cmp_b1_2", kv)), done)
            banks.release(at, 1, a)
            at, ps, free = banks.take()
            pe.do(mm(ps[0:64, 0:30], cmpw2[:, 0:64], HD[:, 0:30]), a, *free)
            for g in range(NSA_G):
                done = pe.do(mm(ps[0:N_CMP, 64 + g * 64:128 + g * 64], HD[:, 30 + g * N_CMP:30 + (g + 1) * N_CMP],
                                cmpw2[:, 64:128]))
            dve.do(lambda e, ps=ps: e.tensor_scalar(KCT[0:64, :], ps[0:64, 0:30], c("cmp_b2_2")[0:64, :], None,
                                                    ALU.add), done)
            v = dve.do(lambda e, ps=ps: e.tensor_tensor(
                VC[0:N_CMP, :, :], ps[0:N_CMP, 64:192].rearrange("p (g d) -> p g d", g=NSA_G),
                row[0:N_CMP, 0:64].unsqueeze(1).broadcast_to([N_CMP, NSA_G, NSA_D]), ALU.add))
            banks.release(at, 1, v)

            scale = NSA_D ** -0.5
            gate = lambda t, b, lo, hi: GA[:, t, :].rearrange("p (h b) -> p h b", b=3)[:, lo:hi, b]
            dve.wait(gates_ready)
            turn_w = 0
            for t in range(TT):
                def products(ps, needs, t=t):
                    for hd in range(NSA_H):
                        done = pe.do(mm(ps[:, hd * N_CMP:(hd + 1) * N_CMP], QU[0:64, hd, t * P:(t + 1) * P],
                                        KCT[0:64, (hd // 4) * N_CMP:(hd // 4 + 1) * N_CMP]), *needs)
                    return done
                pc = PC[:, :, 0:N_CMP]
                softmax(products, NSA_H, N_CMP, scale, seen_add[:, t, 0:N_CMP], None, gate(t, 0, 0, 8), pc,
                        [v, act.now()], stats[0])
                v = dve.do(lambda e, t=t, pc=pc: e.tensor_tensor(
                    pc, pc, seen[:, t, 0:N_CMP].unsqueeze(1).broadcast_to([P, NSA_H, N_CMP]), ALU.mult))
                for half in range(2):
                    turn([PC[:, 4 * half + i, :] for i in range(4)], [v],
                         copy_evac(act, PCT[:, half * 512:(half + 1) * 512]))
                length = (t + 1) * P
                for b, keys in ((0, KST), (1, KWT)):
                    for g in range(NSA_G):
                        def products(ps, needs, t=t, keys=keys, g=g, length=length):
                            for i in range(4):
                                done = pe.do(mm(ps[:, i * length:(i + 1) * length],
                                                QT[0:64, 4 * g + i, t * P:(t + 1) * P], keys[0:64, g, 0:length]),
                                             *needs)
                            return done
                        w = W[turn_w % 2][:, :, 0:length]
                        v = softmax(products, 4, length, scale, causal[:, t, 0:length], None,
                                    gate(t, 1 + b, 4 * g, 4 * g + 4), w, [act.now()], stats[turn_w % 2])
                        turn_w += 1
                        for k in range(t + 1):
                            turn([w[:, i, k * P:(k + 1) * P] for i in range(4)], [v],
                                 copy_evac(act, PT[:, 2 * b + k, g * 512:(g + 1) * 512]))
                at, ps, free = banks.take()
                for hd in range(NSA_H):
                    g = hd // 4
                    s = slice(hd * P, (hd + 1) * P)
                    o = ps[:, hd * 64:(hd + 1) * 64]
                    terms = [(PCT[:, s], VC[:, g, :])]
                    for k in range(t + 1):
                        terms.append((PT[:, k, s], zkv[:, k, 384 + g * 64:448 + g * 64]))
                        terms.append((PT[:, 2 + k, s], zw[:, k, 128 + g * 64:192 + g * 64]))
                    for i, (a, b) in enumerate(terms):
                        done = pe.do(mm(o, a, b, i == 0, i == len(terms) - 1), act.now(), *free)
                v = dve.do(lambda e, ps=ps, t=t: e.tensor_copy(NS[:, t, :], ps), done)
                banks.release(at, 1, v)
            feature_major(NS, plain, [v], k0=4, tiles=4)

        def memory():
            used[0] = 0
            M = cut(TT, D)
            QM, KM, VM = cut(8, T), cut(8, T), cut(TT, D)
            W = cut(MEM_H, T)
            PT = cut(TT, MEM_H * P)
            OM = cut(TT, D)
            stats = cut(8)
            have = load("memory", M, mem.rearrange("(t p) n -> p t n", p=P))
            act.wait(have)
            dve.wait(have)
            scaled = rms_scale(M)
            t = feature_major(xn, lambda k: c("mem_kv_norm_g_2", k), [scaled])
            k_first, _ = multiply("mem_k", False, *t)
            v_first, _ = multiply("mem_v", True)
            four = lambda dst: lambda at: dst[:, 4 * at:4 * at + 4, :].rearrange("p k t -> p (k t)")
            halves = lambda dst: lambda at: dst[:, :, at * CW:(at + 1) * CW].rearrange("p t n -> p (t n)")

            def v_hook(e, slot, m):
                e.wait_ge(s_use, m * UNITS + UNITS)
                at = (m - v_first) * CW
                e.activation(VM[:, :, at:at + CW], ps_chunk[slot][:, :].rearrange("p (t n) -> p t n", t=TT),
                             ACT.Copy).then_inc(s_ev, 1)

            split_chunks(k_first, 2, act_hooks=(copy_hook(k_first, four(KM)),))
            split_chunks(v_first, 2, act_hooks=(v_hook,))
            for lane in (act, dve):
                lane.wait((s_use, UNITS * (v_first + 2)))
            scaled = rms_scale(h)
            t = feature_major(xn, lambda k: c("mem_q_norm_g_2", k), [scaled])
            q_first, _ = multiply("mem_q", False, *t)
            split_chunks(q_first, 2, act_hooks=(copy_hook(q_first, four(QM)),))
            ready = (s_ev, q_first + 2)
            for t in range(TT):
                def products(ps, needs, t=t):
                    for hd in range(MEM_H):
                        for k in range(2):
                            done = pe.do(mm(ps[:, hd * T:(hd + 1) * T], QM[:, 2 * hd + k, t * P:(t + 1) * P],
                                            KM[:, 2 * hd + k, :], k == 0, k == 1), *needs)
                    return done
                v = softmax(products, MEM_H, T, 256 ** -0.5, None, None, None, W, [ready], stats)
                for k in range(TT):
                    turn([W[:, hd, k * P:(k + 1) * P] for hd in range(MEM_H)], [v], copy_evac(act, PT[:, k, :]))
                at, ps, free = banks.take(2)
                for hd in range(MEM_H):
                    for k in range(TT):
                        done = pe.do(mm(ps[:, hd * T:(hd + 1) * T], PT[:, k, hd * P:(hd + 1) * P],
                                        VM[:, k, hd * T:(hd + 1) * T], k == 0, k == 1), act.now(), *free)
                v = dve.do(lambda e, ps=ps, t=t: e.tensor_copy(OM[:, t, :], ps), done)
                banks.release(at, 2, v)
            t = feature_major(OM, plain, [v])
            add_projection("mem_o", *t)

        def peer_select():
            used[0] = 0
            QP = cut(16, T)
            SC, SR = cut(32, P), cut(32, P)
            V16 = cut(32, 16)
            I16 = cut(32, 16)
            IU = cut(32, 16)
            C, CR = cut(16, T), cut(16, T)
            B16, PU = cut(16, 16), cut(16, 16)
            EQ = cut(2048)
            AB = cut(2, T)
            PK = cut(3, T)
            st = cut(32)
            keys = cut(2048)
            have_keys = load("keys", keys, peer_keys)
            scaled = rms_scale(h)
            t = feature_major(xn, lambda k: c("peer_norm_g_2", k), [scaled])
            first, count = multiply("peer_q", False, *t)
            split_chunks(first, count, act_hooks=(copy_hook(first, chunk_rows(
                QP.rearrange("p (c k) t -> p c (k t)", k=4))),))
            pe.wait(have_keys)
            for t in range(TT):
                for b in range(4):
                    at, ps, free = banks.take()
                    for i in range(4):
                        hp = 4 * b + i
                        done = pe.do(mm(ps[:, i * P:(i + 1) * P], QP[:, hp, t * P:(t + 1) * P],
                                        keys[:, hp * P:(hp + 1) * P]), (s_ev, first + count), *free)
                    lo = 16 * t + 4 * b
                    a = act.do(lambda e, ps=ps, lo=lo: e.activation(
                        SC[:, lo:lo + 4, :].rearrange("p a b -> p (a b)"), ps, ACT.Copy), done)
                    banks.release(at, 1, a)

            def top16(src, rest, count, values, indices):
                iu = indices.bitcast(U32)
                passes = (
                    lambda e, i: e.max(values[:, i, 0:8], src[:, i, :]),
                    lambda e, i: e.match_replace(out=rest[:, i, :], in_to_replace=values[:, i, 0:8],
                                                 in_values=src[:, i, :], imm_value=-3e38),
                    lambda e, i: e.max(values[:, i, 8:16], rest[:, i, :]),
                    lambda e, i: e.max_index(iu[:, i, 0:8], values[:, i, 0:8], src[:, i, :]),
                    lambda e, i: e.max_index(iu[:, i, 8:16], values[:, i, 8:16], rest[:, i, :]))
                for step in passes:
                    before = dve.now()
                    for i in range(count):
                        dve.do(lambda e, step=step, i=i: step(e, i), before, own=False)

            dve.wait(a)
            top16(SC, SR, 32, V16, IU)
            dve.do(lambda e: e.tensor_copy(I16, IU.bitcast(U32)))
            v4 = V16.rearrange("p (t h s) k -> p t h s k", t=TT, s=2) if False else V16
            wide = [P, PEER_H, 16, 16]
            half = lambda a, t, s: a[:, 16 * t:16 * t + 16, :].rearrange("p (h s) k -> p h s k", s=2)[:, :, s, :]
            for t in range(TT):
                dve.do(lambda e, t=t: e.tensor_tensor(
                    C[:, 8 * t:8 * t + 8, :].rearrange("p h (a b) -> p h a b", a=16),
                    half(V16, t, 0).unsqueeze(3).broadcast_to(wide), half(V16, t, 1).unsqueeze(2).broadcast_to(wide),
                    ALU.add))
            top16(C, CR, 16, B16, PU)
            pos = PU.rearrange("p a b -> p (a b)").bitcast(U32)
            ab_u = CR[:, 0:2, :].bitcast(U32)
            dve.do(lambda e: e.tensor_scalar(ab_u[:, 0, :], pos, 4, None, ALU.logical_shift_right))
            dve.do(lambda e: e.tensor_scalar(ab_u[:, 1, :], pos, 15, None, ALU.bitwise_and))
            dve.do(lambda e: e.tensor_copy(AB, ab_u))
            eq = EQ.rearrange("p (h k j) -> p h k j", h=PEER_H, k=16)
            for s in range(2):
                for t in range(TT):
                    which = AB[:, s, t * P:(t + 1) * P].rearrange("p (h k) -> p h k", h=PEER_H)
                    dve.do(lambda e, which=which: e.tensor_tensor(
                        eq, iota[:, 0:16].unsqueeze(1).unsqueeze(1).broadcast_to(wide),
                        which.unsqueeze(3).broadcast_to(wide), ALU.is_equal))
                    dve.do(lambda e, t=t, s=s: e.tensor_tensor(
                        eq, eq, half(I16, t, s).unsqueeze(2).broadcast_to(wide), ALU.mult))
                    dve.do(lambda e, t=t, s=s: e.tensor_reduce(
                        PK[:, s, t * P:(t + 1) * P], EQ.rearrange("p (r j) -> p r j", j=16), AX.X, ALU.add))
            rows16 = PK[:, 2, :].rearrange("p (r k) -> p r k", k=16)
            v = dve.do(lambda e: e.tensor_tensor(rows16, B16, B16[:, :, 0:1].broadcast_to([P, 16, 16]), ALU.subtract))
            a = act.do(lambda e: e.activation(PK[:, 2, :], PK[:, 2, :], ACT.Exp), v)
            dve.do(lambda e: e.tensor_reduce(st[:, 0:16], rows16, AX.X, ALU.add), a)
            dve.do(lambda e: e.reciprocal(st[:, 0:16], st[:, 0:16]))
            v = dve.do(lambda e: e.tensor_tensor(rows16, rows16, st[:, 0:16].unsqueeze(2).broadcast_to([P, 16, 16]),
                                                 ALU.mult))
            for what in ((0, 1), (2,)):
                turn([PK[:, i, t * P:(t + 1) * P] for i in what for t in range(TT)], [v],
                     copy_evac(act, picks[:, what[0]:what[-1] + 1, :].rearrange("p a t -> p (a t)")))

        def peer_gates():
            G = places["arena"][:, :].rearrange("p (s n) -> p s n", n=4 * P)
            cols_hot = [xn[:, 0, 512 * s:512 * s + 512].rearrange("p (a b) -> p a b", b=P) for s in range(2)]
            rows_hot = [xn[:, 1, 512 * s:512 * s + 512].rearrange("p (a b) -> p a b", b=P) for s in range(2)]
            s_rows, s_cols, s_made, s_kept = (sem(n) for n in ("s_rows", "s_cols", "s_made", "s_kept"))
            groups = T // 4
            wide = [P, 4, P]

            def loop(e, body):
                for g in range(4):
                    body(e, g, g)
                with e.Fori(1, groups // 4) as i:
                    for g in range(4):
                        body(e, i * 4 + g, g)

            def after(e, s, n, back):
                if not isinstance(n, int) or n >= back:
                    e.wait_ge(s, n - (back - 1))

            def hot_body(e, n, g):
                after(e, s_made, n, 2)
                r = picks[:, 0, bass.ds(n * 4, 4)] if not isinstance(n, int) else picks[:, 0, 4 * n:4 * n + 4]
                e.tensor_tensor(rows_hot[g % 2], iota.unsqueeze(1).broadcast_to(wide),
                                r.unsqueeze(2).broadcast_to(wide), ALU.is_equal).then_inc(s_rows, 1)

                for i in range(4):
                    at = n * 4 + i
                    pick = (lambda q: picks[:, q, at:at + 1]) if isinstance(at, int) else (
                        lambda q: picks[:, q, bass.ds(at, 1)])
                    last = e.tensor_scalar(cols_hot[g % 2][:, i, :], iota, pick(1), pick(2), ALU.is_equal, ALU.mult)
                last.then_inc(s_cols, 1)

            def made_body(e, n, g):
                e.wait_ge(s_rows, n + 1)
                e.wait_ge(s_cols, n + 1)
                after(e, s_kept, n, 4)
                for i in range(4):
                    last = e.matmul(ps_misc[:, g, i * P:(i + 1) * P], cols_hot[g % 2][:, i, :],
                                    rows_hot[g % 2][:, i, :], start=True, stop=True)
                last.then_inc(s_made, 1)

            def kept_body(e, n, g):
                e.wait_ge(s_made, n + 1)
                o = G[:, n, :] if isinstance(n, int) else G[:, bass.ds(n, 1), :].rearrange("p a n -> p (a n)")
                e.activation(o, ps_misc[:, g, :], ACT.Copy).then_inc(s_kept, 1)

            dve.steps.append(lambda e: loop(e, hot_body))
            pe.steps.append(lambda e: loop(e, made_body))
            act.steps.append(lambda e: loop(e, kept_body))
            for lane in work:
                lane.wait((s_kept, groups))

        def peer_experts():
            first, count = STREAM["peer"]
            chunk_at[0] = first + count
            u0 = UNITS * first
            G = places["arena"][:, :].rearrange("p (t i) -> p t i", i=P)
            gel = [xn[:, 0, s * T:(s + 1) * T] for s in range(2)]
            own = [xn[:, 1, s * T:(s + 1) * T] for s in range(2)]
            s_gel, s_own, s_hid = sem("s_gel"), sem("s_own"), sem("s_hid")

            def u_unit(e, b, i):
                e.wait_ge(s_lo, i * 2 + (u0 + 1))
                if not isinstance(i, int) or i > 1:
                    e.wait_ge(s_gel, i - 1)
                for k in range(KD):
                    last = product3(e, ps_chunk[b][:, 0:T], [w[0][:, k * P:(k + 1) * P] for w in (w_hi, w_lo)],
                                    [x[:, k, :] for x in (x_hi, x_lo)], k == 0, k == KD - 1)
                last.then_inc(s_use, 1)

            def v_unit(e, b, i, begin=False, end=False):
                e.wait_ge(s_lo, i * 2 + (u0 + 4))
                e.wait_ge(s_hid, i + 1)
                for t in range(TT):
                    for half in range(2):
                        last = product3(e, ps_misc[:, 2 * t + half, :],
                                        [x[:, b, t * P:(t + 1) * P] for x in (hid_hi, hid_lo)],
                                        [w[1][:, half * CW:(half + 1) * CW] for w in (w_hi, w_lo)], begin, end)
                last.then_inc(s_use, 1)

            def unused(e, u):
                e.wait_ge(s_lo, u + 1)
                e.wait_ge(s_use, u)
                e.sem_inc(s_use, 1)

            def gelu(e, b, i):
                e.wait_ge(s_use, i * 2 + (u0 + 1))
                if not isinstance(i, int) or i > 1:
                    e.wait_ge(s_own, i - 1)
                e.activation(gel[b], ps_chunk[b][:, 0:T], ACT.Gelu_apprx_tanh).then_inc(s_gel, 1)

            def gate_row(e, b, i):
                e.wait_ge(s_gel, i + 1)
                g = G[:, :, i] if isinstance(i, int) else G[:, :, bass.ds(i, 1)].rearrange("p t a -> p (t a)")
                e.tensor_tensor(own[b], gel[b], g, ALU.mult).then_inc(s_own, 1)
                e.wait_ge(s_own, i + 1)
                e.tensor_copy(hid_hi[:, b, :], own[b]).then_inc(s_hih, 1)
                e.wait_ge(s_hih, i + 1)
                e.tensor_tensor(hid_lo[:, b, :], own[b], hid_hi[:, b, :].bitcast(F32), ALU.subtract).then_inc(s_hid, 1)

            s_hih = sem("s_hih")

            def tensor_rows(e):
                u_unit(e, 0, 0)
                unused(e, u0 + 1)
                u_unit(e, 1, 1)
                v_unit(e, 0, 0, begin=True)
                with e.Fori(1, P // 2) as m:
                    for b in range(2):
                        u_unit(e, b, m * 2 + b)
                        v_unit(e, 1 - b, m * 2 + (b - 1))
                unused(e, u0 + 2 * P)
                v_unit(e, 1, P - 1, end=True)
                unused(e, u0 + 2 * P + 2)
                unused(e, u0 + 2 * P + 3)

            def rows(split, work_on_row):
                def run(e):
                    def pair(m):
                        for b in range(2):
                            for q in (2 * b, 2 * b + 1):
                                split(e, q, m + first)
                            work_on_row(e, b, m * 2 + b)
                    pair(0)
                    with e.Fori(1, P // 2) as m:
                        pair(m)
                    for q in range(UNITS):
                        split(e, q, first + P // 2)
                return run

            pe.steps.append(tensor_rows)
            act.steps.append(rows(split_hi, gelu))
            dve.steps.append(rows(split_lo, gate_row))
            dve.wait((s_use, u0 + UNITS * count))
            hf = h[:, :, :].rearrange("p t n -> p (t n)")
            summed = dve.do(lambda e: e.tensor_tensor(hf, hf, ps_misc[:, :, :].rearrange("p b n -> p (b n)"), ALU.add))
            act.wait(summed)

        def finish():
            have_gain = load("gain_2", row[:, :], rows[3:4, :].broadcast_to([P, D]))
            rms_scale(h)
            v = dve.do(lambda e: e.tensor_tensor(xn[:, :, :], xn[:, :, :], row[:, :].unsqueeze(1)
                                                 .broadcast_to([P, TT, D]), ALU.mult), have_gain)
            sp_out[0] += 16
            act.quiet(lambda e: e.dma_start(out.rearrange("(t p) n -> p t n", p=P), xn[:, :, :]).then_inc(s_out, 16), v)

        fence()
        mixers_2()
        add_projection("w_out_2", act.now(), dve.now())
        fence()
        memory()
        fence()
        peer_select()
        fence()
        peer_gates()
        peer_experts()
        finish()
        act.wait((s_out, sp_out[0]))

        memory_of.close()
        with nc.Block() as block:
            @block.sync
            def _(e):
                sp.emit(e)

            @block.tensor
            def _(e):
                pe.emit(e)

            @block.vector
            def _(e):
                dve.emit(e)

            @block.scalar
            def _(e):
                act.emit(e)

            @block.gpsimd
            def _(e):
                pool.emit(e)




def feature_units(w):
    return w.reshape(KD, P, -1, P).transpose(2, 1, 0, 3).reshape(-1, P, UNIT)


def token_units(w):
    n = -(-w.shape[1] // CW)
    full = np.zeros((D, n * CW), w.dtype)
    full[:, :w.shape[1]] = w
    return full.reshape(UNITS, 2, P, n, CW).transpose(3, 0, 2, 1, 4).reshape(-1, P, UNIT)


def lay_out(a):
    w = a["w_in"][0]
    aq, af, ai, ag = (w[:, 512 * n:512 * (n + 1)] for n in range(4))
    bq, bk, bv, cc = w[:, 2048:2304], w[:, 2304:2560], w[:, 2560:2816], w[:, 2816:]
    parts = {}
    parts["w_in feature"] = feature_units(np.concatenate([cc, aq, af, bq, bk], 1))
    parts["w_in token"] = token_units(np.concatenate([ai, ag, bv], 1))
    parts["w_out"] = token_units(a["w_out"][0])
    up = a["ffn_up"][0].reshape(D, 2, NF // 2, 2 * P).transpose(0, 2, 1, 3).reshape(D, 2 * D_FF)
    parts["ffn_up"] = feature_units(up)
    parts["ffn_down, ple_proj"] = np.concatenate([a["ffn_down"][0], a["ple_proj"][0]], 0).reshape(-1, P, D)
    parts["ple_gate"] = token_units(a["ple_gate"][0])
    w = a["w_in_2"][0]
    parts["w_in_2 feature"] = feature_units(w[:, :2 * CW])
    parts["w_in_2 token"] = token_units(w[:, 2 * CW:])
    parts["w_out_2"] = token_units(a["w_out_2"][0])
    for n, units in (("q", feature_units), ("k", feature_units), ("v", token_units), ("o", token_units)):
        parts["mem_" + n] = units(a["w_mem_%s_2" % n][0])
    parts["peer_q"] = feature_units(a["peer_w_q_2"][0])
    stream = np.zeros((UNITS * N_CHUNKS, P, UNIT), np.float32)
    for name, (first, count) in STREAM.items():
        if name != "peer":
            assert parts[name].shape[0] == UNITS * count, (name, parts[name].shape, count)
            stream[UNITS * first:UNITS * (first + count)] = parts[name]
    peer = stream[UNITS * STREAM["peer"][0]:]
    peer[0:2 * P:2] = a["peer_u_2"][0].reshape(P, P, KD, P).transpose(0, 3, 2, 1).reshape(P, P, UNIT)
    peer[3:2 * P + 3:2] = a["peer_v_2"][0].reshape(P, P, D)

    cols = np.zeros((P, N_COLS), np.float32)

    def put(name, value):
        at, n = COLS[name]
        cols[:, at:at + n] = value

    tiles = lambda v: v.reshape(-1, P).T
    for name, (at, n) in COLS.items():
        if name in a and name not in ("conv_dw_w_2", "cmp_b1_2", "cmp_b2_2", "cmp_pos_2"):
            put(name, tiles(a[name]))
    taps = np.concatenate([a["ffn_conv_w"][0], a["ffn_conv_b"]], 0)
    put("ffn_conv", taps.reshape(4, 2, NF // 2, 2, P).transpose(4, 2, 1, 3, 0).reshape(P, -1))
    put("conv_dw_w_2", a["conv_dw_w_2"][0].reshape(CONV_K, CONV_T, P).transpose(2, 0, 1).reshape(P, -1))
    put("cmp_b1_2", a["cmp_b1_2"][0].T)
    put("cmp_b2_2", np.concatenate([a["cmp_b2_2"][0, 0], np.zeros(64, np.float32)])[:, None])
    put("cmp_pos_2", a["cmp_pos_2"][0].reshape(2, CMP_B // 2, P).transpose(2, 0, 1).reshape(P, 32))
    put("eps", EPS)
    put("gn_eps", RK_GN_EPS)
    put("one", 1.0)
    rows = np.zeros((4, D), np.float32)
    for name, (at, n) in ROWS_1.items():
        rows[0, at:at + n] = a[name].reshape(-1)
    rows[1] = a["final_norm_g"]
    rows[2, 0:64] = a["cmp_b2_2"][0, 1]
    rows[3] = a["final_norm_g_2"]
    w1 = a["cmp_w1_2"][0].reshape(2, CMP_B // 2, P, P).transpose(2, 0, 1, 3).reshape(P, -1)
    keys = a["peer_sub_keys_2"][0].reshape(16, P, P).transpose(2, 0, 1).reshape(P, 16 * P)
    p_t = a["p"][0, 0].T.reshape(2, P, T).transpose(1, 0, 2).reshape(P, 2 * T)
    small = np.zeros((P, 512), np.float32)
    small[:64, :256], small[64:, :256], small[:, 256:] = a["rwkv_w2"][0], a["rwkv_a2"][0], a["rwkv_g2"][0]
    return {"stream": stream, "cols": cols, "rows": rows, "consts0": CONSTS[0], "consts1": CONSTS[1],
            "consts2": CONSTS[2], "x": a["x"][0], "mem": a["mem_2"][0],
            "positions": np.ascontiguousarray(a["positions_2"].reshape(TT, P).T),
            "small_w": small, "cmp_w1": np.ascontiguousarray(w1), "peer_keys": np.ascontiguousarray(keys),
            "p_t": np.ascontiguousarray(p_t), "cmp_w2": np.ascontiguousarray(a["cmp_w2_2"][0].transpose(1, 0, 2).reshape(P, 128))}


def kernel(**inputs):
    import concourse.bacc as bacc
    from concourse.bass_utils import run_bass_kernel_spmd

    arrays = lay_out({name: np.asarray(value) for name, value in inputs.items()})
    nc = bacc.Bacc("TRN2", target_bir_lowering=False, num_devices=1)
    aps = {name: nc.dram_tensor("in_" + name, a.shape, mybir.dt.from_np(a.dtype), kind="ExternalInput").ap()
           for name, a in arrays.items()}
    out = nc.dram_tensor("out", (T, D), F32, kind="ExternalOutput").ap()
    build(nc, out=out, **aps)
    result = run_bass_kernel_spmd(nc, [{"in_" + name: a for name, a in arrays.items()}], core_ids=[0])
    return result.results[0]["out"].reshape(1, T, D)
```

```python
import concourse.bass as bass
import numpy as np
from concourse import mybir
from contextlib import ExitStack

F32 = mybir.dt.float32
F32R = mybir.dt.float32r
I32 = mybir.dt.int32
U32 = mybir.dt.uint32
ALU = mybir.AluOpType
ACT = mybir.ActivationFunctionType
AX = mybir.AxisListType

P = 128
T = 256
TT = T // P
D = 1024
KD = D // P
CW = 512
UNIT = 1024
UNITS = 4
EPS = 1e-6
NEG = -1e30
HG_H, HG_K, HG_C = 4, 128, 64
RK_H, RK_N, RK_C = 4, 64, 64
RK_GN_EPS = 64e-5
RK_DECAY_SCALE = float(np.exp(-0.5))
SW_H, SW_D = 4, 64
SW_PATTERNS = ((128, 1), (512, 4), (2048, 16))
D_FF = 2816
NF = D_FF // P
CONV_K, CONV_T = 31, 4
NSA_H, NSA_G, NSA_D = 8, 2, 64
CMP_B, CMP_S = 32, 16
N_CMP = (T - CMP_B) // CMP_S + 1
ROPE_HALF = 8
ROPE_THETA = 500000.0
MEM_H = 4
PEER_H, PEER_K, PEER_TOP = 8, 128, 16
N_RET = PEER_H * PEER_TOP
LEVELS = 6
EARLY_SELECT, EARLY_GATES = 28, 16
EARLY = EARLY_SELECT + EARLY_GATES

STREAM = {}
_at = 0
for _name, _count in (("w_in feature", 5), ("w_in token", 3), ("w_out", 2), ("ffn_up", 11), ("ffn_down, ple_proj", 6),
                      ("ple_gate", 2), ("w_in_2 feature", 2), ("w_in_2 token", 3), ("w_out_2", 2), ("mem_k", 2),
                      ("mem_v", 2), ("mem_q", 2), ("mem_o", 2), ("peer_q", 4), ("peer early u", EARLY // 4),
                      ("peer early v", EARLY // 4), ("peer", (P - EARLY) // 2 + 1)):
    STREAM[_name] = (_at, _count)
    _at += _count
N_CHUNKS = _at


def columns_plan():
    plan, at = {}, 0
    for name, n in (("norm_mix_g", 8), ("norm_ffn_g", 8), ("norm_ple_g", 8), ("rwkv_mu", 8), ("rwkv_w0", 2),
                    ("rwkv_a0", 2), ("rwkv_k_k", 2), ("rwkv_k_a", 2), ("rwkv_r_k", 2),
                    ("ffn_conv", 4 * 2 * NF), ("mix_norm_g_2", 8), ("conv_dw_w_2", CONV_K * CONV_T),
                    ("conv_dw_b_2", CONV_T), ("conv_ln_g_2", CONV_T), ("conv_ln_b_2", CONV_T), ("cmp_b1_2", 2),
                    ("cmp_b2_2", 1), ("cmp_pos_2", 32), ("mem_q_norm_g_2", 8), ("mem_kv_norm_g_2", 8),
                    ("peer_norm_g_2", 8), ("eps", 1), ("gn_eps", 1), ("one", 1)):
        plan[name] = (at, n)
        at += n
    return plan, at


COLS, N_COLS = columns_plan()
ROWS_1 = {"hgrn_gnorm_g": (0, 512), "rwkv_ln_w": (512, 256), "rwkv_ln_b": (768, 256)}


def shape_constants():
    i = np.arange(P)
    token = np.arange(T)
    always = [np.eye(P), np.broadcast_to(i, (P, P))]
    first = []
    for level in range(LEVELS):
        b = 2 << level
        left, right = i % b < b // 2, i % b >= b // 2
        first.append((i[:, None] // b == i[None] // b) & left[:, None] & right[None])
    first.append(np.eye(P))
    same = i[:, None] // RK_C == i[None] // RK_C
    first.append(same & (i[:, None] < i[None]))
    first.append(same & (i[:, None] <= i[None]))
    first.append(i[:, None] // RK_N == i[None] // RK_N)
    first.append(np.broadcast_to(np.arange(D) % HG_C != 0, (P, D)))
    q, k = token[:, None], token[None]
    held = np.zeros((T, T))
    for window, dil in SW_PATTERNS:
        held += (k <= q) & ((q - k) % dil == 0) & ((q - k) // dil <= window // dil)
    rows = lambda a: a.reshape(TT, P, -1).transpose(1, 0, 2).reshape(P, -1)
    first += [rows(held), rows(np.where(held > 0, 0.0, NEG))]
    first.append(np.stack([i < RK_N, i >= RK_N], 1))
    c = np.arange(16)
    seen = (c[None] * CMP_S + CMP_B - 1 <= token[:, None]) & (c[None] < N_CMP)
    second = [rows(np.where(k <= q, 0.0, NEG)), rows(seen * 1.0), rows(np.where(seen, 0.0, NEG))]
    inv = np.float32(ROPE_THETA) ** -(np.arange(ROPE_HALF, dtype=np.float32) * 2.0 / (2 * ROPE_HALF))
    second.append(np.broadcast_to(inv, (P, ROPE_HALF)))
    join = lambda parts: np.ascontiguousarray(np.concatenate([np.asarray(a, np.float32) for a in parts], 1))
    return join(always), join(first), join(second)


CONSTS = shape_constants()


class Lane:

    def __init__(self, sem, chained):
        self.sem, self.chained, self.n, self.steps, self.known = sem, chained, 0, [], {}
        self.strand, self.last = "main", {"main": 0}

    def now(self):
        return (self.sem, self.last[self.strand])

    def wait(self, *needs):
        for need in needs:
            if need is None or need[1] <= 0:
                continue
            sem, value = need
            if self.known.get(id(sem), 0) < value:
                self.known[id(sem)] = value
                self.steps.append(lambda e, sem=sem, value=value: e.wait_ge(sem, value))

    def do(self, f, *needs, own=None):
        self.wait(*needs)
        if self.chained if own is None else own:
            self.wait(self.now())
        self.n += 1
        self.last[self.strand] = self.n
        self.steps.append(lambda e: f(e).then_inc(self.sem, 1))
        return self.now()

    def quiet(self, f, *needs):
        self.wait(*needs)
        self.steps.append(f)

    def emit(self, e):
        for step in self.steps:
            step(e)


class Banks:

    def __init__(self, pairs):
        self.pairs, self.free, self.strand = pairs, [()] * (2 * len(pairs)), "main"
        self.turn = {"main": 0}
        self.range = {"main": (4, 4)}

    def take(self, n=1):
        lo, count = self.range[self.strand]
        turn = self.turn[self.strand]
        if n == 2 and turn % 2:
            turn += 1
        at = lo + turn % count
        self.turn[self.strand] = turn + n
        needs = [x for b in range(at, at + n) for x in self.free[b]]
        return at, self.pairs[at // 2][:, at % 2 * 512:(at % 2 + n) * 512], needs

    def release(self, at, n, *tokens):
        for b in range(at, at + n):
            self.free[b] = tokens


def build(nc, stream, cols, rows, consts0, consts1, consts2, x, mem, positions, small_w, cmp_w1, cmp_w2, peer_keys, p_t, out):
    ctx = ExitStack()
    with ctx:
        def sb(name, shape, dt=F32):
            return ctx.enter_context(nc.sbuf_tensor(name, shape, dt))

        def sem(name):
            return ctx.enter_context(nc.semaphore(name))

        raw = [sb(f"raw{i}", [P, UNIT]) for i in range(UNITS)]
        w_hi = [sb(f"w_hi{i}", [P, UNIT], F32R) for i in range(2)]
        w_lo = [sb(f"w_lo{i}", [P, UNIT], F32R) for i in range(2)]
        x_hi, x_lo = sb("x_hi", [P, KD, T], F32R), sb("x_lo", [P, KD, T], F32R)
        hid_hi, hid_lo = sb("hid_hi", [P, 2, T], F32R), sb("hid_lo", [P, 2, T], F32R)
        h = sb("h", [P, TT, D])
        xn = sb("xn", [P, TT, D])
        col = sb("col", [P, N_COLS])
        row = sb("row", [P, D])
        ident_iota = sb("ident_iota", [P, 2 * P])
        picks = sb("picks", [P, 3, T])
        ss = sb("ss", [P, 8])
        ident, iota = ident_iota[:, 0:P], ident_iota[:, P:2 * P]
        ps_chunk = [ctx.enter_context(nc.psum_tensor(f"ps_chunk{i}", [P, 1024], F32)) for i in range(2)]
        ps_misc = ctx.enter_context(nc.psum_tensor("ps_misc", [P, 4, 512], F32))
        misc = ps_misc[:, :, :].rearrange("p b n -> p (b n)")
        banks = Banks([ps_chunk[0][:, :], ps_chunk[1][:, :], misc[:, 0:1024], misc[:, 1024:2048]])

        s_w = [sem(f"s_w{i}") for i in range(UNITS)]
        s_hi1, s_hi = sem("s_hi1"), sem("s_hi")
        s_lo1, s_lo = sem("s_lo1"), sem("s_lo")
        s_use1, s_use = sem("s_use1"), sem("s_use")
        s_ev = sem("s_ev")
        s_out = sem("s_out")
        pe = Lane(sem("s_pe"), False)
        dve = Lane(sem("s_dve"), True)
        act = Lane(sem("s_act"), True)
        pool = Lane(sem("s_pool"), True)
        sp = Lane(sem("s_sp"), False)
        work = (pe, dve, act, pool)

        def c(name, i=0, n=1):
            return col[:, COLS[name][0] + i:COLS[name][0] + i + n]

        def r(plan, name):
            at, n = plan[name]
            return row[:, at:at + n]

        memory_of = ExitStack()
        places = {}

        def phase(name, *tensors):
            memory_of.close()
            for key, shape, dt in tensors:
                places[key] = memory_of.enter_context(nc.sbuf_tensor(f"{name}_{key}", shape, dt))
            used[0] = 0

        used = [0]
        phase("mixers", ("arena", [P, P * T], F32))

        def cut(*shape):
            n = int(np.prod(shape))
            at = used[0]
            used[0] += n
            assert used[0] <= places["arena"].shape[1], used
            a = places["arena"][:, at:at + n]
            if len(shape) == 2:
                a = a.rearrange("p (a b) -> p a b", b=shape[1])
            if len(shape) == 3:
                a = a.rearrange("p (a b c) -> p a b c", b=shape[1], c=shape[2])
            return a

        chunk_at = [0]

        def fence():
            totals = [lane.now() for lane in work] + [(s_use, UNITS * chunk_at[0]), (s_ev, chunk_at[0])]
            for lane in work + (sp,):
                lane.wait(*totals)
            banks.free = [()] * 8

        def mm(out, lhsT, rhs, start=True, stop=True):
            return lambda e: e.matmul(out, lhsT, rhs, start=start, stop=stop, skip_group_check=True)

        def interleave(until=None, **strands):
            live = [name for name in strands if name not in through]
            for name in live:
                if name not in rows_at:
                    banks.range[name], banks.turn[name], rows_at[name] = strands[name][:2], 0, 0
                    for lane in work:
                        lane.last[name] = lane.n

            def switch(name):
                banks.strand = name
                for lane in work:
                    lane.strand = name

            while live and until not in through:
                for name in list(live):
                    switch(name)
                    for _ in range(strands[name][3]):
                        if name in live and next(strands[name][2], "end") == "end":
                            live.remove(name)
                            through.append(name)
            switch("main")
            for lane in work:
                lane.last["main"] = lane.n

        through = []

        rows_at = {"main": 0}

        def rows_from(base):
            moved, rows_at[banks.strand] = base != rows_at[banks.strand], base
            return pe.now() if moved else None

        sent = {}

        def load(name, dst, src, *needs):
            if name not in sent:
                sent[name] = [sem("s_load_" + name), 0]
            group = sent[name]
            group[1] += 16
            act.quiet(lambda e: e.dma_start(dst, src).then_inc(group[0], 16), *needs)
            return tuple(group)

        have_x = load("x", h[:, :, :], x.rearrange("(t p) n -> p t n", p=P))
        load("first", ident_iota[:, :], consts0)
        have_first = load("first", col[:, :], cols)

        def feed(e):
            def put(q, u):
                src = stream[u, :, :] if isinstance(u, int) else stream[bass.ds(u, 1), :, :].rearrange("a p n -> p (a n)")
                e.dma_start(raw[q][:, :], src).then_inc(s_w[q], 16)

            for q in range(UNITS):
                put(q, q)
            with e.Fori(1, chunk_at[0]) as i:
                for q in range(UNITS):
                    e.wait_ge(s_lo, i * UNITS + (q + 1 - UNITS))
                    put(q, i * UNITS + q)

        sp.wait(have_x)
        sp.steps.append(feed)

        def over_chunks(lane, first, count, body):
            def run(e):
                n, end = first, first + count
                while n < end and (n % 2 or n == 0):
                    for _ in range(2 if n == 0 else 1):
                        if n < end:
                            body(e, n % 2, n, n // 2)
                            n += 1
                pairs = (end - n) // 2
                if pairs > 1:
                    with e.Fori(0, pairs) as i:
                        for slot in range(2):
                            body(e, slot, i * 2 + (n + slot), i + n // 2)
                    n += 2 * pairs
                while n < end:
                    body(e, n % 2, n, n // 2)
                    n += 1
            lane.steps.append(run)

        def split_hi(e, q, n):
            e.wait_ge(s_w[q], n * 16 + 16)
            for part, used_up, made in ((0, s_use1, s_hi1), (1, s_use, s_hi)):
                if not isinstance(n, int) or UNITS * n + q >= 2:
                    e.wait_ge(used_up, n * UNITS + (q - 1))
                s = slice(part * CW, part * CW + CW)
                e.activation(w_hi[q % 2][:, s], raw[q][:, s], ACT.Copy).then_inc(made, 1)

        def split_lo(e, q, n):
            for part, high, made in ((0, s_hi1, s_lo1), (1, s_hi, s_lo)):
                e.wait_ge(high, n * UNITS + (q + 1))
                s = slice(part * CW, part * CW + CW)
                e.tensor_tensor(w_lo[q % 2][:, s], raw[q][:, s], w_hi[q % 2][:, s].bitcast(F32),
                                ALU.subtract).then_inc(made, 1)

        halves_of_unit = ((0, s_lo1, s_use1), (1, s_lo, s_use))

        def split_chunks(first, count, act_hooks=(), dve_hooks=()):
            for lane, split, hooks in ((act, split_hi, act_hooks), (dve, split_lo, dve_hooks)):
                def body(e, n, slot, splits, hooked, split=split, hooks=hooks):
                    for part in range(2):
                        if splits:
                            for q in (2 * part, 2 * part + 1):
                                split(e, q, n)
                        if hooked and part < len(hooks) and hooks[part]:
                            hooks[part](e, slot, n - 1)

                def run(e, body=body):
                    body(e, first, 0, True, False)
                    n = first + 1
                    pairs = (count - 1) // 2
                    if pairs > 2:
                        for _ in range(2):
                            body(e, n, (n - 1) % 2, True, True)
                            n += 1
                        with e.Fori(0, pairs - 1) as i:
                            for s in range(2):
                                body(e, i * 2 + (n + s), (n + s - 1) % 2, True, True)
                        n += 2 * (pairs - 1)
                    while n < first + count:
                        body(e, n, (n - 1) % 2, True, True)
                        n += 1
                    body(e, first + count, (first + count - 1) % 2, False, True)
                lane.wait((s_ev, first))
                lane.steps.append(run)
            chunk_at[0] = first + count

        def product3(e, o, stationary, moving, start, stop):
            for i, (a, b) in enumerate(((0, 0), (1, 0), (0, 1))):
                last = e.matmul(o, stationary[a], moving[b], start=start and i == 0, stop=stop and i == 2,
                                skip_group_check=True)
            return last

        def room(e, n):
            if not isinstance(n, int) or n > 1:
                e.wait_ge(s_ev, n - 1)

        def multiply(name, token_major, *needs):
            first, count = STREAM[name]
            pe.wait(*needs)

            def body(e, slot, n, half):
                room(e, n)
                for q in range(UNITS):
                    w = (w_hi[q % 2], w_lo[q % 2])
                    for part, made, used_up in halves_of_unit:
                        e.wait_ge(made, n * UNITS + (q + 1))
                        if token_major:
                            k = 2 * q + part
                            for t in range(TT):
                                last = product3(e, ps_chunk[slot][:, t * CW:(t + 1) * CW],
                                                [x[:, k, t * P:(t + 1) * P] for x in (x_hi, x_lo)],
                                                [a[:, part * CW:(part + 1) * CW] for a in w], k == 0, k == KD - 1)
                        else:
                            for k in range(4 * part, 4 * part + 4):
                                last = product3(e, ps_chunk[slot][:, q * T:(q + 1) * T],
                                                [a[:, k * P:(k + 1) * P] for a in w],
                                                [x[:, k, :] for x in (x_hi, x_lo)], k == 0, k == KD - 1)
                        last.then_inc(used_up, 1)

            over_chunks(pe, first, count, body)
            return first, count

        def copy_hook(first, dst):
            def hook(e, slot, m):
                e.wait_ge(s_use, m * UNITS + UNITS)
                at = m - first
                e.activation(dst(at) if isinstance(at, int) else dst(bass.ds(at, 1)), ps_chunk[slot][:, :],
                             ACT.Copy).then_inc(s_ev, 1)
            return hook

        def chunk_rows(Z):
            return lambda at: Z[:, at, :] if isinstance(at, int) else Z[:, at, :].rearrange("p a n -> p (a n)")

        def rms(src, *needs, tiles=(None, None)):
            for t in range(TT):
                act.do(lambda e, t=t: e.activation(xn[:, t, :], src[:, t, :], ACT.Square, accum_out=ss[:, t:t + 1]),
                       *needs, tiles[t], own=False)
            root = act.do(lambda e: e.activation(ss[:, 2:4], ss[:, 0:2], ACT.Sqrt, scale=1.0 / D, bias=c("eps")))
            return dve.do(lambda e: e.reciprocal(ss[:, 4:6], ss[:, 2:4]), root)

        def rms_scale(src, *needs, tiles=(None, None)):
            inverse = rms(src, *needs, tiles=tiles)
            v = dve.do(lambda e: e.tensor_scalar(xn[:, 0, :], src[:, 0, :], ss[:, 4:5], None, ALU.mult), tiles[0])
            a = act.do(lambda e: e.activation(xn[:, 1, :], src[:, 1, :], ACT.Copy, scale=ss[:, 5:6]), inverse)
            return [v, a]

        def rms_gain(src, dst, gain_ready, *needs):
            rms(src, *needs)
            return [dve.do(lambda e, t=t: e.scalar_tensor_tensor(
                out=dst[:, t, :], in0=src[:, t, :], scalar=ss[:, 4 + t:5 + t], in1=row[:, :], op0=ALU.mult,
                op1=ALU.mult), gain_ready) for t in range(TT)]

        def turn(srcs, needs, evac, rows_out=P, banks_n=1):
            at, ps, free = banks.take(banks_n)
            for i, s in enumerate(srcs):
                done = pe.do(lambda e, i=i, s=s: e.transpose(ps[0:rows_out, i * P:(i + 1) * P], s, ident),
                             *needs, *free)
            tokens = evac(ps[0:rows_out, 0:len(srcs) * P], done)
            banks.release(at, banks_n, *tokens)
            return tokens

        def into_x(src, k, gain, needs):
            for i in range(src.shape[1] // T):
                piece = src[:, i * T:(i + 1) * T]
                act.do(lambda e, i=i, piece=piece: e.activation(x_hi[:, k + i, :], piece, ACT.Copy, scale=gain(k + i)),
                       *needs, own=False)
            for i in range(src.shape[1] // T):
                piece = src[:, i * T:(i + 1) * T]
                v = dve.do(lambda e, i=i, piece=piece: e.scalar_tensor_tensor(
                    out=x_lo[:, k + i, :], in0=piece, scalar=gain(k + i), in1=x_hi[:, k + i, :].bitcast(F32),
                    op0=ALU.mult, op1=ALU.subtract), act.now(), own=False)
            return (v,)

        def feature_major(src, gain, needs, k0=0, tiles=KD):
            for b in range(tiles // 2):
                pieces = [src[:, t, k * P:(k + 1) * P] for k in (2 * b, 2 * b + 1) for t in range(TT)]
                tokens = turn(pieces, needs, lambda ps, done, b=b: into_x(ps, k0 + 2 * b, gain, [done]))
            return tokens

        def copy_evac(lane, dst):
            def evac(ps, done):
                if lane is act:
                    return (act.do(lambda e: e.activation(dst, ps, ACT.Copy), done),)
                return (dve.do(lambda e: e.tensor_copy(dst, ps), done),)
            return evac

        def softmax(products, heads, length, scale, add, mult, gate, weights, needs, stats):
            at, ps, free = banks.take(2)
            done = products(ps, list(needs) + list(free))
            yield
            s = ps[:, 0:heads * length].rearrange("p (h l) -> p h l", h=heads)
            if add is not None:
                read = dve.do(lambda e: e.scalar_tensor_tensor(
                    out=weights, in0=s, scalar=scale, in1=add.unsqueeze(1).broadcast_to([P, heads, length]),
                    op0=ALU.mult, op1=ALU.add), done)
            else:
                read = dve.do(lambda e: e.tensor_scalar(weights, s, scale, None, ALU.mult), done)
            banks.release(at, 2, read)
            top, den = stats[:, 0:heads], stats[:, heads:2 * heads]
            wide = lambda a: a.unsqueeze(2).broadcast_to([P, heads, length])
            v = dve.do(lambda e: e.tensor_reduce(top, weights, AX.X, ALU.max))
            if mult is None and length >= P:
                v = dve.do(lambda e: e.tensor_scalar(top, top, -1.0, None, ALU.mult))
                yield
                for hd in range(heads):
                    a = act.do(lambda e, hd=hd: e.activation(weights[:, hd, :], weights[:, hd, :], ACT.Exp,
                                                             bias=top[:, hd:hd + 1], accum_out=den[:, hd:hd + 1]),
                               v, own=False)
                yield
                dve.wait(a)
            else:
                v = dve.do(lambda e: e.tensor_tensor(weights, weights, wide(top), ALU.subtract))
                yield
                a = act.do(lambda e: e.activation(weights, weights, ACT.Exp), v)
                yield
                dve.wait(a)
                if mult is not None:
                    dve.do(lambda e: e.tensor_tensor(weights, weights,
                                                     mult.unsqueeze(1).broadcast_to([P, heads, length]), ALU.mult))
                dve.do(lambda e: e.tensor_reduce(den, weights, AX.X, ALU.add))
            dve.do(lambda e: e.reciprocal(den, den))
            if gate is not None:
                dve.do(lambda e: e.tensor_tensor(den, den, gate, ALU.mult))
            return dve.do(lambda e: e.tensor_tensor(weights, weights, wide(den), ALU.mult))

        def add_projection(name, *needs):
            first, count = multiply(name, True, *needs)

            def hook(e, slot, m):
                e.wait_ge(s_use, m * UNITS + UNITS)
                at = (m - first) * CW
                e.tensor_tensor(h[:, :, at:at + CW], h[:, :, at:at + CW],
                                ps_chunk[slot][:, :].rearrange("p (t n) -> p t n", t=TT), ALU.add).then_inc(s_ev, 1)

            split_chunks(first, count, dve_hooks=(hook,))
            return (s_ev, first + count)

        Z = cut(8, 1024)
        k1 = cut(consts1.shape[1])
        masks = k1[:, 0:10 * P].rearrange("p (m n) -> p m n", m=10)
        strict, inclusive, head_ones = masks[:, 7, :], masks[:, 8, :], masks[:, 9, :]
        restart = k1[:, 10 * P:10 * P + D]
        sw_held = k1[:, 10 * P + D:10 * P + D + 512].rearrange("p (t n) -> p t n", t=TT)
        sw_add = k1[:, 10 * P + D + 512:10 * P + D + 1024].rearrange("p (t n) -> p t n", t=TT)
        head_pick = k1[:, 10 * P + D + 1024:10 * P + D + 1026]
        mixed = xn
        lora = cut(2 * T)

        dve.wait(have_first)
        act.wait(have_first)
        pe.wait(have_first)
        act.wait(have_x)
        dve.wait(have_x)
        scaled = rms_scale(h)
        have_rows = load("rows", row[:, :], rows[0:1, :].broadcast_to([P, D]))
        load("k1", k1, consts1)
        have_lora = load("k1", lora, small_w)
        turned = feature_major(xn, lambda k: c("norm_mix_g", k), scaled)
        first, _ = multiply("w_in feature", False, *turned)
        multiply("w_in token", True)
        split_chunks(first, 8, act_hooks=(copy_hook(first, chunk_rows(Z)),))
        fence()
        act.wait(have_rows, have_lora)
        dve.wait(have_rows, have_lora)
        pe.wait(have_lora)

        zc = Z[:, 0:2, :].rearrange("p c (k t) -> p (c k) t", t=T)
        zq, zf = Z[:, 2, :], Z[:, 3, :]
        zb = Z[:, 4, :].rearrange("p (k t) -> p k t", t=T)
        zi, zg = (Z[:, n, :].rearrange("p (t n) -> p t n", t=TT) for n in (5, 6))
        zv = Z[:, 7, :].rearrange("p (t n) -> p t n", t=TT)

        base = used[0]

        def hgrn():
            K, LF, B, KL = cut(D), cut(D), cut(D), cut(D)
            S = cut(8, P)
            EL = cut(16)
            E, QL = zf, LF
            QE = QL
            KT, O = (a.rearrange("p (t n) -> p t n", t=TT) for a in (K, E))
            state = picks[:, 0:2, :].rearrange("p a (h n) -> p (a h) n", n=P)
            by_head = lambda a: a.rearrange("p (h t) -> p h t", h=HG_H)
            act.do(lambda e: e.activation(LF, zf, ACT.Abs))
            act.do(lambda e: e.activation(LF, LF, ACT.Exp, scale=-1.0))
            a = act.do(lambda e: e.activation(LF, LF, ACT.Ln, bias=c("one")))
            act.do(lambda e: e.activation(K, zf, ACT.Sigmoid, scale=-1.0))
            act.do(lambda e: e.activation(zq, zq, ACT.Silu))
            g = act.do(lambda e: e.activation(Z[:, 6, :], Z[:, 6, :], ACT.Silu))
            yield
            dve.do(lambda e: e.scalar_tensor_tensor(out=LF, in0=zf, scalar=0.0, in1=LF, op0=ALU.min,
                                                    op1=ALU.subtract), a)
            dve.do(lambda e: e.tensor_tensor_scan(B, restart, LF, 0.0, ALU.mult, ALU.add))
            dve.do(lambda e: e.memset(S, 0.0))
            for level in range(-1, LEVELS):
                if level < 0:
                    q_l, k_l, mask, v, w = zq, K, masks[:, 6, :], dve.now(), None
                else:
                    b = 2 << level
                    view = lambda a, b=b: a.rearrange("p (m b) -> p m b", b=b)
                    mid = view(B)[:, :, b // 2 - 1:b // 2].broadcast_to([P, D // b, b])
                    yield
                    v = dve.do(lambda e, view=view, mid=mid: e.tensor_tensor(view(E), view(B), mid, ALU.subtract),
                               act.now(), pool.now())
                    act.do(lambda e: e.activation(E, E, ACT.Abs), v)
                    yield
                    a = act.do(lambda e: e.activation(E, E, ACT.Exp, scale=-1.0))
                    w = pool.do(lambda e: e.tensor_tensor(QL, zq, E, ALU.mult), a, pe.now())
                    yield
                    v = dve.do(lambda e: e.tensor_tensor(KL, K, E, ALU.mult), a, pe.now())
                    q_l, k_l, mask = QL, KL, masks[:, level, :]
                yield
                at, ps, free = banks.take(2)
                for i in range(8):
                    lo = i * P
                    done = pe.do(mm(ps[:, lo:lo + P], k_l[:, lo:lo + P], q_l[:, lo:lo + P]), v, w, act.now(), *free)
                yield
                v = dve.do(lambda e, ps=ps, mask=mask: e.copy_predicated(
                    S, mask.bitcast(U32).unsqueeze(1).broadcast_to([P, 8, P]),
                    ps.rearrange("p (a b) -> p a b", b=P)), done)
                banks.release(at, 2, v)
            yield
            a = act.do(lambda e: e.activation(E, B, ACT.Exp), dve.now())
            dve.do(lambda e: e.tensor_tensor(QE, zq, E, ALU.mult), a, pe.now())
            view = lambda a: a.rearrange("p (m b) -> p m b", b=HG_C)
            last = view(B)[:, :, HG_C - 1:HG_C]
            yield
            v = dve.do(lambda e: e.tensor_tensor(view(E), last.broadcast_to([P, 16, HG_C]), view(B), ALU.subtract))
            act.do(lambda e: e.activation(E, E, ACT.Exp), v)
            yield
            a = act.do(lambda e: e.activation(EL.unsqueeze(2), last, ACT.Exp))
            yield
            v = dve.do(lambda e: e.tensor_tensor(KL, K, E, ALU.mult), a, pe.now())
            for t in range(TT):
                turn([KL[:, hd * T + t * P:hd * T + (t + 1) * P] for hd in range(HG_H)], [v],
                     copy_evac(act, KT[:, t, :]))
            for t in range(TT):
                yield
                at, ps, free = banks.take()
                for hd in range(HG_H):
                    done = pe.do(mm(ps[:, hd * P:(hd + 1) * P], S[:, 2 * hd + t, :], zi[:, t, hd * P:(hd + 1) * P]),
                                 dve.now(), *free)
                yield
                a = act.do(lambda e, ps=ps, t=t: e.activation(O[:, t, :], ps, ACT.Copy), done)
                banks.release(at, 1, a)
            dve.do(lambda e: e.memset(state, 0.0))
            for n in range(T // HG_C):
                t, lo = n // 2, HG_C * (n % 2)
                if n:
                    yield
                    at, ps, free = banks.take()
                    for hd in range(HG_H):
                        done = pe.do(mm(ps[lo:lo + HG_C, hd * P:(hd + 1) * P],
                                        QE[:, hd * T + n * HG_C:hd * T + (n + 1) * HG_C], state[:, hd, :]),
                                     dve.now(), *free)
                    yield
                    v = dve.do(lambda e, ps=ps, t=t, lo=lo: e.tensor_tensor(
                        O[lo:lo + HG_C, t, :], O[lo:lo + HG_C, t, :], ps[lo:lo + HG_C, :], ALU.add), done, act.now())
                    banks.release(at, 1, v)
                if n < T // HG_C - 1:
                    yield
                    at, ps, free = banks.take()
                    for hd in range(HG_H):
                        done = pe.do(mm(ps[:, hd * P:(hd + 1) * P], KT[lo:lo + HG_C, t, hd * P:(hd + 1) * P],
                                        zi[lo:lo + HG_C, t, hd * P:(hd + 1) * P]), act.now(), *free)
                    for hd in range(HG_H):
                        at_l = hd * 4 + n
                        yield
                        v = dve.do(lambda e, ps=ps, hd=hd, at_l=at_l: e.scalar_tensor_tensor(
                            out=state[:, hd, :], in0=state[:, hd, :], scalar=EL[:, at_l:at_l + 1],
                            in1=ps[:, hd * P:(hd + 1) * P], op0=ALU.mult, op1=ALU.add), done)
                    banks.release(at, 1, v)
            Of = O.rearrange("p t n -> p (t n)")
            O8 = Of.rearrange("p (a b) -> p a b", b=P)
            dve.do(lambda e: e.tensor_tensor(KL, Of, Of, ALU.mult), act.now(), pe.now())
            yield
            v = dve.do(lambda e: e.tensor_reduce(EL[:, 0:8], KL.rearrange("p (a b) -> p a b", b=P), AX.X, ALU.add))
            yield
            a = act.do(lambda e: e.activation(EL[:, 8:16], EL[:, 0:8], ACT.Sqrt, scale=1.0 / P, bias=c("eps")), v)
            dve.do(lambda e: e.reciprocal(EL[:, 0:8], EL[:, 8:16]), a)
            dve.do(lambda e: e.tensor_tensor(O8, O8, EL[:, 0:8].unsqueeze(2).broadcast_to([P, 8, P]), ALU.mult))
            dve.do(lambda e: e.tensor_tensor(
                zg, zg, r(ROWS_1, "hgrn_gnorm_g").unsqueeze(1).broadcast_to([P, TT, 512]), ALU.mult), g)
            dve.do(lambda e: e.tensor_tensor(mixed[:, :, 0:512], O, zg, ALU.mult))

        def windows():
            W = h[:, 0, :].rearrange("p (h n) -> p h n", n=T)
            PT = h[:, 1, :].rearrange("p (t n) -> p t n", t=TT)
            stats = ss
            for t in range(TT):
                length = (t + 1) * P

                def products(ps, needs, t=t, length=length):
                    for hd in (0, 2, 1, 3):
                        j, lo = hd // 2, SW_D * (hd % 2)
                        done = pe.do(mm(ps[:, hd * length:(hd + 1) * length], zb[lo:lo + SW_D, j, t * P:(t + 1) * P],
                                        zb[lo:lo + SW_D, 2 + j, 0:length]), *needs, rows_from(lo))
                    return done

                w = W[:, :, 0:length]
                v = yield from softmax(products, SW_H, length, SW_D ** -0.5, sw_add[:, t, 0:length], sw_held[:, t, 0:length],
                            None, w, [pe.now()], stats)
                for k in range(t + 1):
                    turn([w[:, hd, k * P:(k + 1) * P] for hd in range(SW_H)], [v], copy_evac(act, PT[:, k, :]))
                yield
                at, ps, free = banks.take()
                for hd in range(SW_H):
                    for k in range(t + 1):
                        done = pe.do(mm(ps[:, hd * SW_D:(hd + 1) * SW_D], PT[:, k, hd * P:(hd + 1) * P],
                                        zv[:, k, hd * SW_D:(hd + 1) * SW_D], k == 0, k == t), act.now(), *free)
                yield
                v = dve.do(lambda e, ps=ps, t=t: e.tensor_copy(mixed[:, t, 512:768], ps[:, 0:256]), done)
                banks.release(at, 1, v)

        def rwkv():
            two = lambda: cut(512)
            A, LW, B, KK, PX, AB, KB, R, K2, X1, X2, X3 = (two() for _ in range(12))
            G = cut(TT, T)
            S0 = cut(2, RK_N)
            U, RH = picks[:, 2, :], cut(T)
            EL, BS = cut(8), cut(8)
            MT, NT, RAT, RKT, Y1, ML = (cut(8, P) for _ in range(6))
            shift = cut(8, T)
            CM = zc
            MX, MXT = (shift[:, 4 * i:4 * i + 4, :].rearrange("p a (b n) -> p (a b) n", n=P) for i in range(2))
            VT, ABT, KBT, Y = (a.rearrange("p (t n) -> p t n", t=TT) for a in (LW, KK, A, X3))
            flat = lambda a: a.rearrange("p a b -> p (a b)")
            place = lambda hd, t: (hd % 2) * 4 + (hd // 2) * 2 + t
            dve.do(lambda e: e.tensor_tensor(shift[:, :, 1:T], zc[:, :, 0:T - 1], zc[:, :, 1:T], ALU.subtract))
            dve.do(lambda e: e.tensor_scalar(shift[:, :, 0:1], zc[:, :, 0:1], -1.0, None, ALU.mult))
            for k in (6, 7, 0, 1, 2, 3, 4, 5):
                if k == 0:
                    low_rank = dve.now()
                dve.do(lambda e, k=k: e.scalar_tensor_tensor(out=CM[:, k, :], in0=shift[:, k, :], scalar=c("rwkv_mu", k),
                                                             in1=zc[:, k, :], op0=ALU.mult, op1=ALU.add))
            rr, kk, vv = (CM[:, 2 * n:2 * n + 2, :] for n in range(3))
            rr, kk = flat(rr), flat(kk)
            th, sg = X1[:, 0:T], X1[:, T:2 * T]
            act.do(lambda e: e.activation(th[0:64, :], CM[0:64, 6, :], ACT.Tanh), low_rank)
            yield
            a = act.do(lambda e: e.activation(sg, CM[:, 7, :], ACT.Sigmoid))
            wa, g2 = lora[:, 0:256], lora[:, 256:512]
            yield
            at, ps, free = banks.take(2)
            for j in range(2):
                pe.do(mm(ps[:, j * T:(j + 1) * T], wa[0:64, j * P:(j + 1) * P], th[0:64, :]), a, *free)
            for j in range(2):
                done = pe.do(mm(ps[:, 512 + j * T:512 + (j + 1) * T], wa[64:128, j * P:(j + 1) * P], CM[64:128, 6, :]))
            for j in range(2):
                act.do(lambda e, j=j, ps=ps: e.activation(LW[:, j * T:(j + 1) * T], ps[:, j * T:(j + 1) * T], ACT.Sigmoid,
                                                   bias=c("rwkv_w0", j)), done)
                yield
                a = act.do(lambda e, j=j, ps=ps: e.activation(A[:, j * T:(j + 1) * T], ps[:, 512 + j * T:512 + (j + 1) * T],
                                                       ACT.Sigmoid, bias=c("rwkv_a0", j)))
            banks.release(at, 2, a)
            gate_at, gps, free = banks.take()
            for t in range(TT):
                gdone = pe.do(mm(gps[:, t * T:(t + 1) * T], sg[:, t * P:(t + 1) * P], g2), *free)
            g_tok = act.do(lambda e: e.activation(flat(G), gps, ACT.Copy), gdone)
            banks.release(gate_at, 1, g_tok)
            dve.do(lambda e: e.tensor_scalar(LW, LW, -RK_DECAY_SCALE, None, ALU.mult), a)
            dve.do(lambda e: e.tensor_tensor_scan(B, restart[:, 0:512], LW, 0.0, ALU.mult, ALU.add))
            for j in range(2):
                s = slice(j * T, (j + 1) * T)
                dve.do(lambda e, s=s, j=j: e.tensor_scalar(KK[:, s], kk[:, s], c("rwkv_k_k", j), None, ALU.mult))
            yield
            v = dve.do(lambda e: e.tensor_tensor(X2, KK, KK, ALU.mult))
            yield
            at, ps, free = banks.take()
            done = pe.do(mm(ps, head_ones, X2), v, *free)
            yield
            a = act.do(lambda e, ps=ps: e.activation(X2, ps, ACT.Sqrt), done)
            banks.release(at, 1, a)
            dve.do(lambda e: e.tensor_scalar(X2, X2, 1e-12, None, ALU.max), a)
            dve.do(lambda e: e.reciprocal(X2, X2))
            dve.do(lambda e: e.tensor_tensor(KK, KK, X2, ALU.mult))
            for j in range(2):
                s = slice(j * T, (j + 1) * T)
                dve.do(lambda e, s=s, j=j: e.tensor_scalar(K2[:, s], A[:, s], 1.0, c("rwkv_k_a", j), ALU.subtract,
                                                           ALU.mult))
            dve.do(lambda e: e.scalar_tensor_tensor(out=K2, in0=K2, scalar=1.0, in1=kk, op0=ALU.add, op1=ALU.mult))
            yield
            v = dve.do(lambda e: e.tensor_tensor(X2, B, LW, ALU.subtract))
            act.do(lambda e: e.activation(X2, X2, ACT.Exp), v)
            act.do(lambda e: e.activation(X3, B, ACT.Exp))
            last = B.rearrange("p (m b) -> p m b", b=RK_C)[:, :, RK_C - 1:RK_C]
            act.do(lambda e: e.activation(EL.unsqueeze(2), last, ACT.Exp))
            yield
            a = act.do(lambda e: e.activation(X1, B, ACT.Exp, scale=-1.0), gdone)
            dve.do(lambda e: e.tensor_tensor(PX, KK, X2, ALU.mult), a)
            dve.do(lambda e: e.tensor_tensor(R, rr, X3, ALU.mult))
            dve.do(lambda e: e.tensor_tensor(KB, K2, X1, ALU.mult))
            dve.do(lambda e: e.tensor_tensor(AB, KK, A, ALU.mult))
            yield
            v = dve.do(lambda e: e.tensor_tensor(AB, AB, X1, ALU.mult))
            for src, dst in ((flat(vv), VT), (AB, ABT), (KB, KBT)):
                turn([src[:, j * T + t * P:j * T + (t + 1) * P] for t in range(TT) for j in range(2)], [v],
                     copy_evac(act, flat(dst)))
            turned = act.now()
            for j in range(2):
                s = slice(j * T, (j + 1) * T)
                dve.do(lambda e, s=s, j=j: e.scalar_tensor_tensor(out=X2[:, s], in0=rr[:, s], scalar=c("rwkv_r_k", j),
                                                                  in1=K2[:, s], op0=ALU.mult, op1=ALU.mult))
            v = dve.now()
            yield
            at, ps, free = banks.take()
            for t in range(TT):
                for j in range(2):
                    lo = t * 4 + 2 * j
                    done = pe.do(mm(ps[:, lo:lo + 2], X2[:, j * T + t * P:j * T + (t + 1) * P], head_pick), v, *free)
            yield
            v = dve.do(lambda e, ps=ps: e.tensor_copy(BS, ps[:, 0:8]), done)
            banks.release(at, 1, v)
            for dst, left, right, mask in ((MT, AB, PX, strict), (NT, KB, PX, strict), (RAT, AB, R, inclusive),
                                           (RKT, KB, R, inclusive)):
                yield
                at, ps, free = banks.take(2)
                for hd in range(RK_H):
                    j, lo = hd // 2, RK_N * (hd % 2)
                    for t in range(TT):
                        s = slice(j * T + t * P, j * T + (t + 1) * P)
                        i = place(hd, t)
                        done = pe.do(mm(ps[:, i * P:(i + 1) * P], left[lo:lo + RK_N, s], right[lo:lo + RK_N, s]), *free)
                yield
                v = dve.do(lambda e, ps=ps, dst=dst, mask=mask: e.tensor_tensor(
                    dst, ps.rearrange("p (a b) -> p a b", b=P), mask.unsqueeze(1).broadcast_to([P, 8, P]), ALU.mult),
                    done)
                banks.release(at, 2, v)
            eye4 = ident.unsqueeze(1).broadcast_to([P, 4, P])
            halves = [slice(0, 4), slice(4, 8)]
            masked_at = lambda level, *needs: pool.do(lambda e: e.tensor_tensor(
                ML, MT, masks[:, level, :].unsqueeze(1).broadcast_to([P, 8, P]), ALU.mult), *needs)
            masked = masked_at(0, dve.now())
            yield
            for half in halves:
                at, ps, free = banks.take()
                for i in range(4):
                    done = pe.do(mm(ps[:, i * P:(i + 1) * P], ML[:, half, :][:, i, :], ident), masked, *free)
                yield
                v = dve.do(lambda e, ps=ps, half=half: e.tensor_tensor(
                    MX[:, half, :], eye4, ps.rearrange("p (a b) -> p a b", b=P), ALU.subtract), done)
                banks.release(at, 1, v)
                v = dve.do(lambda e, half=half: e.tensor_tensor(MXT[:, half, :], eye4, ML[:, half, :], ALU.subtract),
                           masked)
            masked = masked_at(1, done, v)
            updated = [v, v]
            for level in range(1, LEVELS):
                yield
                copied = []
                for h2, half in enumerate(halves):
                    at, ps, free = banks.take()
                    for i in range(4):
                        done = pe.do(mm(ps[:, i * P:(i + 1) * P], ML[:, half, :][:, i, :], MX[:, half, :][:, i, :]),
                                     masked, updated[h2], *free)
                    copied.append(act.do(lambda e, ps=ps, half=half: e.activation(flat(Y1[:, half, :]), ps, ACT.Copy),
                                         done))
                    banks.release(at, 1, copied[-1])
                    yield
                if level < LEVELS - 1:
                    masked = masked_at(level + 1, done)
                for h2, half in enumerate(halves):
                    sums = []
                    for dst, left, right in ((MX, MXT, Y1), (MXT, Y1, MXT)):
                        if dst is MX and level == LEVELS - 1:
                            continue
                        at, ps, free = banks.take()
                        for i in range(4):
                            done = pe.do(mm(ps[:, i * P:(i + 1) * P], left[:, half, :][:, i, :],
                                            right[:, half, :][:, i, :]), copied[h2], *free)
                        sums.append((at, ps, dst))
                    yield
                    for at, ps, dst in sums:
                        v = dve.do(lambda e, ps=ps, dst=dst, half=half: e.tensor_tensor(
                            flat(dst[:, half, :]), flat(dst[:, half, :]), ps, ALU.subtract), done)
                        banks.release(at, 1, v)
                    updated[h2] = v
            dve.do(lambda e: e.memset(S0, 0.0))
            for n in range(T // RK_C):
                t, lo = n // 2, RK_C * (n % 2)
                tok = slice(lo, lo + RK_C)
                heads = [(hd, hd // 2, RK_N * (hd % 2)) for hd in (0, 2, 1, 3)]
                col_of = lambda j, n=n: slice(j * T + n * RK_C, j * T + (n + 1) * RK_C)
                vs = lambda hd: slice(hd * RK_N, (hd + 1) * RK_N)
                yield
                at, ps, free = banks.take()
                ready = dve.now()
                for hd, j, kb in heads:
                    done = pe.do(mm(ps[tok, vs(hd)], PX[kb:kb + RK_N, col_of(j)], S0[kb:kb + RK_N, j, :], hd == 0, False),
                                 ready, *free, rows_from(kb))
                for hd, j, kb in heads:
                    done = pe.do(mm(ps[tok, vs(hd)], NT[tok, place(hd, t), tok], VT[tok, t, vs(hd)], False, True), done,
                                 rows_from(lo))
                yield
                v = dve.do(lambda e, ps=ps, tok=tok: e.tensor_scalar(RH[tok, :], ps[tok, 0:T], -1.0, None, ALU.mult),
                           done)
                banks.release(at, 1, v)
                yield
                at, ps, free = banks.take()
                for hd, j, kb in heads:
                    done = pe.do(mm(ps[tok, vs(hd)], MXT[tok, place(hd, t), tok], RH[tok, vs(hd)]), v, *free, rows_from(lo))
                yield
                v = dve.do(lambda e, ps=ps, tok=tok: e.tensor_copy(U[tok, :], ps[tok, 0:T]), done)
                banks.release(at, 1, v)
                yield
                at, ps, free = banks.take()
                for hd, j, kb in heads:
                    done = pe.do(mm(ps[tok, vs(hd)], R[kb:kb + RK_N, col_of(j)], S0[kb:kb + RK_N, j, :], hd == 0, False),
                                 *free, rows_from(kb))
                for hd, j, kb in heads:
                    pe.do(mm(ps[tok, vs(hd)], RAT[tok, place(hd, t), tok], U[tok, vs(hd)], False, False), done, v, rows_from(lo))
                    ydone = pe.do(mm(ps[tok, vs(hd)], RKT[tok, place(hd, t), tok], VT[tok, t, vs(hd)], False, True))
                yield
                a = act.do(lambda e, ps=ps, tok=tok, t=t: e.activation(Y[tok, t, :], ps[tok, 0:T], ACT.Copy), ydone)
                banks.release(at, 1, a)
                if n < T // RK_C - 1:
                    yield
                    at, ps, free = banks.take()
                    for hd, j, kb in heads:
                        o = ps[kb:kb + RK_N, j * RK_N:(j + 1) * RK_N]
                        pe.do(mm(o, ABT[tok, t, vs(hd)], U[tok, vs(hd)], True, False), *free)
                        done = pe.do(mm(o, KBT[tok, t, vs(hd)], VT[tok, t, vs(hd)], False, True))
                    dve.do(lambda e, ps=ps: e.tensor_tensor(flat(S0), flat(S0), ps[:, 0:P], ALU.add), done)
                    e_last = EL.rearrange("p (j n) -> p j n", j=2)[:, :, n:n + 1].broadcast_to([P, 2, RK_N])
                    yield
                    v = dve.do(lambda e, e_last=e_last: e.tensor_tensor(S0, S0, e_last, ALU.mult))
                    banks.release(at, 1, v)
            Y8 = flat(Y).rearrange("p (a b) -> p a b", b=RK_N)
            wide = lambda a: a.unsqueeze(2).broadcast_to([P, 8, RK_N])
            m, sq = EL, X1.rearrange("p (a b) -> p a b", b=RK_N)
            dve.do(lambda e: e.tensor_reduce(m, Y8, AX.X, ALU.add), act.now())
            dve.do(lambda e: e.tensor_scalar(m, m, 1.0 / RK_N, None, ALU.mult))
            dve.do(lambda e: e.tensor_tensor(Y8, Y8, wide(m), ALU.subtract))
            dve.do(lambda e: e.tensor_tensor(sq, Y8, Y8, ALU.mult))
            yield
            v = dve.do(lambda e: e.tensor_reduce(m, sq, AX.X, ALU.add))
            yield
            a = act.do(lambda e: e.activation(m, m, ACT.Sqrt, scale=1.0 / RK_N, bias=c("gn_eps")), v)
            dve.do(lambda e: e.reciprocal(m, m), a)
            dve.do(lambda e: e.tensor_tensor(Y8, Y8, wide(m), ALU.mult))
            across = lambda name: r(ROWS_1, name).unsqueeze(1).broadcast_to([P, TT, T])
            dve.do(lambda e: e.tensor_tensor(Y, Y, across("rwkv_ln_w"), ALU.mult))
            dve.do(lambda e: e.tensor_tensor(Y, Y, across("rwkv_ln_b"), ALU.add))
            dve.do(lambda e: e.tensor_tensor(sq, flat(VT).rearrange("p (a b) -> p a b", b=RK_N), wide(BS), ALU.mult),
                   turned)
            dve.do(lambda e: e.tensor_tensor(Y8, Y8, sq, ALU.add))
            dve.do(lambda e: e.tensor_tensor(mixed[:, :, 768:1024], Y, G, ALU.mult), g_tok)

        def hgrn_and_windows():
            yield from hgrn()
            yield from windows()

        interleave(rwkv=(4, 4, rwkv(), 1), windows=(2, 2, windows(), 1), hgrn=(0, 2, hgrn(), 1))
        fence()
        x_again = load("x_again", h[:, :, :], x.rearrange("(t p) n -> p t n", p=P))

        plain = lambda k: c("one")

        sp_out = [0]

        t = feature_major(mixed, plain, [dve.now()])
        dve.wait(x_again)
        summed = add_projection("w_out", *t)
        fence()

        def ffn():
            phase("ffn", ("GT_hi", [P, NF, T], F32R), ("GT_lo", [P, NF, T], F32R), ("arena", [P, 8192], F32))
            GT_hi, GT_lo = places["GT_hi"], places["GT_lo"]
            UC = cut(2, 4, T)
            GV = cut(2, 512)
            scaled = rms_scale(h)
            t = feature_major(xn, lambda k: c("norm_ffn_g", k), scaled)
            first, count = multiply("ffn_up", False, *t)
            tap0 = COLS["ffn_conv"][0]
            s_tap, s_sum, s_gv, s_gt = (sem(n) for n in ("s_tap", "s_sum", "s_gv", "s_gt"))

            def newest_tap(e, slot, m):
                i = m - first
                e.wait_ge(s_use, m * UNITS + UNITS)
                if not isinstance(i, int) or i > 1:
                    e.wait_ge(s_gv, i - 1)
                for piece in range(4):
                    at = i * 16 + (tap0 + 4 * piece)
                    last = e.activation(UC[:, slot, piece, :], ps_chunk[slot][:, piece * T:(piece + 1) * T],
                                        ACT.Identity, scale=col[:, bass.ds(at + 2, 1)], bias=col[:, bass.ds(at + 3, 1)])
                    if piece % 2:
                        last.then_inc(s_tap, 1)

            def older_taps(e, slot, m):
                i = m - first
                for lag in (1, 2):
                    for piece in range(4):
                        at = i * 16 + (tap0 + 4 * piece)
                        if lag == 1 and piece % 2 == 0:
                            e.wait_ge(s_tap, i * 2 + (piece // 2 + 1))
                        if lag == 2:
                            e.wait_ge(s_sum, i * 8 + (piece + 1))
                        o = UC[:, slot, piece, lag:T]
                        e.scalar_tensor_tensor(out=o, in0=ps_chunk[slot][:, piece * T:(piece + 1) * T - lag],
                                               scalar=col[:, bass.ds(at + (2 - lag), 1)], in1=o, op0=ALU.mult,
                                               op1=ALU.add).then_inc(s_sum, 1)
                e.wait_ge(s_sum, i * 8 + 8)
                e.sem_inc(s_ev, 1)

            def gate_silu(e, slot, m):
                i = m - first
                e.wait_ge(s_sum, i * 8 + 8)
                gates = UC[:, slot, 0:2, :]
                e.activation(gates, gates, ACT.Silu).then_inc(s_silu, 1)

            s_silu, s_gl = sem("s_silu"), sem("s_gl")

            def gated(e, slot, m):
                i = m - first
                e.wait_ge(s_silu, i + 1)
                if not isinstance(i, int) or i > 1:
                    e.wait_ge(s_gl, i - 1)
                gv = GV[:, slot, :].rearrange("p (a t) -> p a t", a=2)
                e.tensor_tensor(gv, UC[:, slot, 0:2, :], UC[:, slot, 2:4, :], ALU.mult).then_inc(s_gv, 1)
                e.wait_ge(s_gv, i + 1)
                e.tensor_copy(GT_hi[:, bass.ds(i * 2, 2), :], gv).then_inc(s_gt, 1)

            def low_parts(e):
                def one(i, slot):
                    e.wait_ge(s_gt, i + 1)
                    e.tensor_tensor(GT_lo[:, bass.ds(i * 2, 2), :], GV[:, slot, :].rearrange("p (a t) -> p a t", a=2),
                                    GT_hi[:, bass.ds(i * 2, 2), :].bitcast(F32), ALU.subtract).then_inc(s_gl, 1)

                with e.Fori(0, count // 2) as c:
                    for q in range(2):
                        one(c * 2 + q, (first + q) % 2)
                for i in range(count // 2 * 2, count):
                    one(i, (first + i) % 2)

            pool.steps.append(low_parts)
            split_chunks(first, count, act_hooks=(newest_tap, gate_silu), dve_hooks=(older_taps, gated))
            ffn_down(GT_hi, GT_lo, s_gl)

        def ffn_down(GT_hi, GT_lo, s_gl):
            first, count = STREAM["ffn_down, ple_proj"]
            PL = cut(2 * T)
            got = load("p", PL, p_t)
            act.wait(got)
            dve.wait(got)
            split_chunks(first, count)
            for lane in (act, dve):
                lane.wait((s_use, UNITS * first))
            into_p = into_x(PL, 0, plain, [])
            pe.wait(*[x for b in range(4, 8) for x in banks.free[b]])

            def rows_of(e, u, x, k, begin, end):
                for half, made, used_up in halves_of_unit:
                    e.wait_ge(made, UNITS * first + u + 1)
                    for t in range(TT):
                        last = product3(e, ps_misc[:, 2 * t + half, :], [a[:, k, t * P:(t + 1) * P] for a in x],
                                        [w[u % 2][:, half * CW:(half + 1) * CW] for w in (w_hi, w_lo)], begin, end)
                    last.then_inc(used_up, 1)

            def down(e):
                for k in range(NF):
                    if k % 2 == 0:
                        e.wait_ge(s_gl, k // 2 + 1)
                    rows_of(e, k, (GT_hi, GT_lo), k, k == 0, k == NF - 1)

            def proj(e):
                for k in range(2):
                    rows_of(e, NF + k, (x_hi, x_lo), k, k == 0, k == 1)

            pe.steps.append(down)
            dve.wait((s_use, UNITS * first + NF))
            sums = ps_misc[:, :, :].rearrange("p b n -> p (b n)")
            hf = h[:, :, :].rearrange("p t n -> p (t n)")
            v = dve.do(lambda e: e.tensor_tensor(hf, hf, sums, ALU.add))
            pe.wait(v, *into_p)
            pe.steps.append(proj)
            act.wait((s_use, UNITS * (first + count)))
            places["ple"] = cut(2 * D)
            a = act.do(lambda e: e.activation(places["ple"], sums, ACT.Copy))
            act.quiet(lambda e: e.sem_inc(s_ev, count), a)
            fence()
        ffn()
        def ple_and_norm():
            ple = places["ple"].rearrange("p (t n) -> p t n", t=TT)
            gate = cut(TT, D)
            have_gain = load("gain", row[:, :], rows[1:2, :].broadcast_to([P, D]))
            scaled = rms_scale(h)
            t = feature_major(xn, lambda k: c("norm_ple_g", k), scaled)
            first, count = multiply("ple_gate", True, *t)

            def hook(e, slot, m):
                e.wait_ge(s_use, m * UNITS + UNITS)
                at = (m - first) * CW
                e.activation(gate[:, :, at:at + CW], ps_chunk[slot][:, :].rearrange("p (t n) -> p t n", t=TT),
                             ACT.Sigmoid).then_inc(s_ev, 1)

            def gated_sum(e, slot, m):
                e.wait_ge(s_ev, m + 1)
                cols = slice((m - first) * CW, (m - first + 1) * CW)
                e.tensor_tensor(gate[:, :, cols], gate[:, :, cols], ple[:, :, cols], ALU.mult).then_inc(s_ple, 1)
                e.wait_ge(s_ple, m - first + 1)
                for t in range(TT):
                    e.tensor_tensor(h[:, t, cols], h[:, t, cols], gate[:, t, cols], ALU.add).then_inc(s_ple_sum[t], 1)

            s_ple, s_ple_sum = sem("s_ple"), [sem(f"s_ple_sum{t}") for t in range(TT)]
            split_chunks(first, count, act_hooks=(hook,), dve_hooks=(gated_sum,))
            summed = [(s, count) for s in s_ple_sum]
            for lane in (act, dve):
                lane.wait(*summed)
            tokens = rms_gain(h, h, have_gain)
            return tokens

        normed = ple_and_norm()
        def mixers_2():
            phase("mixers_2", ("arena", [P, 31232], F32), ("tokens", [P, TT, D], F32))
            Z2 = cut(5, 1024)
            cmpw1, cmpw2 = cut(2, 16, P), cut(2 * NSA_D)
            load("second", cmpw1.rearrange("p a b c -> p (a b c)"), cmp_w1)
            load("second", cmpw2, cmp_w2)
            have_tokens = load("memory", places["tokens"][:, :, :], mem.rearrange("(t p) n -> p t n", p=P))
            k2 = cut(consts2.shape[1])
            pos_raw = cut(TT)
            load("second", k2, consts2)
            load("second", pos_raw.bitcast(I32), positions)
            causal = k2[:, 0:512].rearrange("p (t n) -> p t n", t=TT)
            seen = k2[:, 512:544].rearrange("p (t n) -> p t n", t=TT)
            seen_add = k2[:, 544:576].rearrange("p (t n) -> p t n", t=TT)
            inv = k2[:, 576:584]
            scaled = rms_scale(h, tiles=normed)
            have = load("second", row[:, :], rows[2:3, :].broadcast_to([P, D]), *normed)
            t = feature_major(xn, lambda k: c("mix_norm_g_2", k), scaled)
            first, _ = multiply("w_in_2 feature", False, *t)
            multiply("w_in_2 token", True)
            split_chunks(first, 5, act_hooks=(copy_hook(first, chunk_rows(Z2)),))
            for lane in (act, pe, dve):
                lane.wait(have)
            got = [(s_ev, first + 5)] * 5
            conv = conv_module(Z2, got)
            attend = []
            interleave(conv=(0, 2, conv, 2),
                       keys=(4, 4, nsa(Z2, got, causal, seen, seen_add, inv, pos_raw, cmpw1, cmpw2, attend), 1),
                       memory=(2, 2, memory_norm(places["tokens"], have_tokens), 1), until="keys")
            tile, NS = attend
            interleave(tile1=(4, 4, tile(1), 1), conv=(0, 2, conv, 2), tile0=(2, 2, tile(0), 1))
            feature_major(NS, plain, [dve.now()], k0=4, tiles=4)

        def memory_norm(M, have):
            scratch = ps_chunk[1][:, :]
            yield
            act.wait(have)
            dve.wait(have)
            for t in range(TT):
                a = act.do(lambda e, t=t: e.activation(scratch, M[:, t, :], ACT.Square, accum_out=ss[:, t:t + 1]))
            yield
            a = act.do(lambda e: e.activation(ss[:, 2:4], ss[:, 0:2], ACT.Sqrt, scale=1.0 / D, bias=c("eps")))
            yield
            v = dve.do(lambda e: e.reciprocal(ss[:, 4:6], ss[:, 2:4]), a)
            yield
            dve.do(lambda e: e.tensor_scalar(M[:, 0, :], M[:, 0, :], ss[:, 4:5], None, ALU.mult))
            act.do(lambda e: e.activation(M[:, 1, :], M[:, 1, :], ACT.Copy, scale=ss[:, 5:6]), v)

        def conv_module(Z2, got):
            pad = CONV_K - 1
            U = cut(CONV_T, T + pad)
            Y = cut(CONV_T, T)
            half = 16
            diagonals = [cut(half, P), Z2[:, 0:2, :].rearrange("p a (j n) -> p (a j) n", n=P)]
            tiles = lambda n: Z2[:, n, :].rearrange("p (k t) -> p k t", t=T)
            a = act.do(lambda e: e.activation(Z2[:, 1, :], Z2[:, 1, :], ACT.Sigmoid), got[1])
            dve.do(lambda e: e.memset(U[:, :, 0:pad], 0.0))
            made = dve.do(lambda e: e.tensor_tensor(U[:, :, pad:pad + T], tiles(0), tiles(1), ALU.mult), a, got[0])
            yield
            taps = col[:, COLS["conv_dw_w_2"][0]:COLS["conv_dw_w_2"][0] + CONV_K * CONV_T].rearrange(
                "p (j k) -> p k j", k=CONV_T)
            used_up = [None, None]
            for k in range(CONV_T):
                at, ps, free = banks.take()
                for part in range(2):
                    lo = half * part
                    n = min(half, CONV_K - lo)
                    D_part = diagonals[part]
                    m = pool.do(lambda e, D_part=D_part, k=k, lo=lo, n=n: e.tensor_tensor(
                        D_part[:, 0:n, :], ident.unsqueeze(1).broadcast_to([P, n, P]),
                        taps[:, k, lo:lo + n].unsqueeze(2).broadcast_to([P, n, P]), ALU.mult), made, used_up[part])
                    for some in range(0, n, 2):
                        for j in range(some, min(some + 2, n)):
                            used_up[part] = pe.do(mm(ps[:, 0:T], D_part[:, j, :], U[:, k, lo + j:lo + j + T],
                                                     lo + j == 0, lo + j == CONV_K - 1), m, made, *free)
                        yield
                a = act.do(lambda e, k=k, ps=ps: e.activation(Y[:, k, :], ps[:, 0:T], ACT.Identity,
                                                              bias=c("conv_dw_b_2", k)), used_up[1])
                banks.release(at, 1, a)
            ready = a
            YT, SQ = (xn[:, i, :].rearrange("p (t n) -> p t n", t=TT) for i in range(2))
            st = cut(8)
            for t in range(TT):
                yield
                turn([Y[:, k, t * P:(t + 1) * P] for k in range(CONV_T)], [ready], copy_evac(act, YT[:, t, :]))
            m, q = st[:, 0:2], st[:, 2:4]
            wide = lambda a: a.unsqueeze(2).broadcast_to([P, TT, 512])
            dve.do(lambda e: e.tensor_reduce(m, YT, AX.X, ALU.add), act.now())
            dve.do(lambda e: e.tensor_scalar(m, m, 1.0 / 512, None, ALU.mult))
            dve.do(lambda e: e.tensor_tensor(YT, YT, wide(m), ALU.subtract))
            dve.do(lambda e: e.tensor_tensor(SQ, YT, YT, ALU.mult))
            yield
            v = dve.do(lambda e: e.tensor_reduce(q, SQ, AX.X, ALU.add))
            yield
            a = act.do(lambda e: e.activation(q, q, ACT.Sqrt, scale=1.0 / 512, bias=c("eps")), v)
            dve.do(lambda e: e.reciprocal(q, q), a)
            yield
            v = dve.do(lambda e: e.tensor_tensor(YT, YT, wide(q), ALU.mult))
            SF = SQ.rearrange("p t n -> p (t n)")
            for b in range(2):
                def evac(ps, done, b=b):
                    for i in range(2):
                        k = 2 * b + i
                        last = act.do(lambda e, k=k, i=i: e.activation(
                            SF[:, k * T:(k + 1) * T], ps[:, i * T:(i + 1) * T], ACT.Silu, scale=c("conv_ln_g_2", k),
                            bias=c("conv_ln_b_2", k)), done, own=False)
                    return (last,)
                turn([YT[:, t, k * P:(k + 1) * P] for k in (2 * b, 2 * b + 1) for t in range(TT)], [v], evac)
            into_x(SF, 0, plain, [act.now()])

        def nsa(Z2, got, causal, seen, seen_add, inv, pos_raw, cmpw1, cmpw2, attend):
            zq = Z2[:, 2, :].rearrange("p (t h d) -> p t h d", t=TT, h=NSA_H)
            zkv = Z2[:, 3, :].rearrange("p (t n) -> p t n", t=TT)
            zw = Z2[:, 4, :].rearrange("p (t n) -> p t n", t=TT)
            rope_at = cut(TT)
            angle, CS, N1 = cut(TT, 8), cut(2, TT, 8), cut(TT, 8)
            QR = cut(1024)
            QU, QT = cut(NSA_H, T), cut(NSA_H, T)
            KST, KWT = cut(NSA_G, T), cut(NSA_G, T)
            GA = cut(TT, 24)
            W = [cut(4, T) for _ in range(2)]
            stats = [cut(16) for _ in range(2)]
            PT = cut(4, NSA_H * P)
            PC, PCT = cut(NSA_H, P), cut(NSA_H * P)
            VC = cut(NSA_G, NSA_D)
            NS = cut(TT, 512)
            R4 = cut(4, 128)
            for n in (2, 3, 4):
                dve.wait(got[n])
            dve.do(lambda e: e.tensor_copy(rope_at, pos_raw.bitcast(I32)))
            dve.do(lambda e: e.tensor_tensor(angle, rope_at.unsqueeze(2).broadcast_to([P, TT, 8]),
                                             inv.unsqueeze(1).broadcast_to([P, TT, 8]), ALU.mult))
            two_pi, high = 2 * np.pi, 6.28125
            magic = 1.5 * 2.0 ** 23
            for i, quarter in ((0, 0.25), (1, 0.0)):
                dve.do(lambda e, quarter=quarter: e.tensor_scalar(N1, angle, 1 / two_pi, quarter, ALU.mult, ALU.add))
                dve.do(lambda e: e.tensor_scalar(N1, N1, magic, None, ALU.add))
                dve.do(lambda e: e.tensor_scalar(N1, N1, -magic, None, ALU.add))
                dve.do(lambda e, i=i: e.scalar_tensor_tensor(out=CS[:, i, :, :], in0=N1, scalar=-high, in1=angle,
                                                             op0=ALU.mult, op1=ALU.add))
                dve.do(lambda e, i=i: e.scalar_tensor_tensor(out=CS[:, i, :, :], in0=N1, scalar=high - two_pi,
                                                             in1=CS[:, i, :, :], op0=ALU.mult, op1=ALU.add))
                dve.do(lambda e, i=i, quarter=quarter: e.tensor_scalar(CS[:, i, :, :], CS[:, i, :, :],
                                                                       quarter * two_pi, None, ALU.add))
            flat_cs = CS.rearrange("p i t d -> p (i t d)")
            yield
            v = dve.do(lambda e: e.tensor_scalar(flat_cs, flat_cs, 3.1415925, -3.1415925, ALU.min, ALU.max))
            cs_ready = act.do(lambda e: e.activation(flat_cs, flat_cs, ACT.Sin), v)
            gates_ready = act.do(lambda e: e.activation(GA, zw[:, :, 256:280], ACT.Sigmoid))

            def heads_turned(src, count, dst, needs):
                for hd in range(0, count, 2):
                    turn([src(hd + i, t) for i in range(2) for t in range(TT)], needs,
                         copy_evac(act, dst[0:64, hd:hd + 2, :].rearrange("p h t -> p (h t)")), rows_out=64)

            heads_turned(lambda hd, t: zq[:, t, hd, :], NSA_H, QU, [got[2]])

            def rope(x, count):
                r4 = [R4[:, i, 0:TT * count * 8].rearrange("p (t h d) -> p t h d", t=TT, h=count) for i in range(4)]
                x1, x2 = x[:, :, :, 0:8], x[:, :, :, 8:16]
                cos, sin = (CS[:, i, :, :].unsqueeze(2).broadcast_to([P, TT, count, 8]) for i in range(2))
                dve.wait(cs_ready)
                for o, a, b in ((r4[0], x1, cos), (r4[1], x2, sin), (r4[2], x2, cos), (r4[3], x1, sin)):
                    dve.do(lambda e, o=o, a=a, b=b: e.tensor_tensor(o, a, b, ALU.mult))
                dve.do(lambda e: e.tensor_tensor(x1, r4[0], r4[1], ALU.subtract))
                return dve.do(lambda e: e.tensor_tensor(x2, r4[2], r4[3], ALU.add))

            dve.do(lambda e: e.tensor_copy(QR, Z2[:, 2, :]))
            qr = QR.rearrange("p (t h d) -> p t h d", t=TT, h=NSA_H)
            group = lambda z, at: z[:, :, at:at + 128].rearrange("p t (g d) -> p t g d", g=NSA_G)
            v = rope(qr, NSA_H)
            heads_turned(lambda hd, t: qr[:, t, hd, :], NSA_H, QT, [v])
            ks, kw = group(zkv, 256), group(zw, 0)
            v = rope(ks, NSA_G)
            heads_turned(lambda g, t: ks[:, t, g, :], NSA_G, KST, [v])
            v = rope(kw, NSA_G)
            heads_turned(lambda g, t: kw[:, t, g, :], NSA_G, KWT, [v])

            spare = PT.rearrange("p a b -> p (a b)")
            KD2 = spare[:, 0:1024].rearrange("p (t m n) -> p t m n", t=TT, m=4)
            XK = spare[:, 1024:2048].rearrange("p (m t) -> p m t", t=T)
            X = spare[:, 2048:3008].rearrange("p (a m n) -> p a m n", a=2, m=16)
            HD, KCT = cut(60), cut(30)
            for copy in range(2):
                yield
                v = dve.do(lambda e, copy=copy: e.tensor_copy(
                    KD2[:, :, :, copy * 64:copy * 64 + 64], zkv[:, :, 0:256].rearrange("p t (m d) -> p t m d", d=64)))
            dve.do(lambda e: e.memset(VC, 0.0))
            dve.do(lambda e: e.memset(PC, 0.0))
            for m in (0, 2):
                def evac(ps, done, m=m):
                    ps = ps.rearrange("p (m t) -> p m t", t=T)
                    act.do(lambda e: e.activation(XK[0:64, m:m + 2, :], ps[0:64, :, :], ACT.Copy), done)
                    return (act.do(lambda e: e.activation(XK[64:128, m:m + 2, 0:T - 1], ps[64:128, :, 1:T], ACT.Copy)),)
                turn([KD2[:, t, i, :] for i in (m, m + 1) for t in range(TT)], [v], evac)
            for kv in range(2):
                for mh in range(2):
                    x_in = XK[:, 2 * kv:2 * kv + 2, 16 * mh:16 * mh + 240].rearrange(
                        "p g (c m two) -> p m g c two", c=N_CMP, two=2)[:, :, :, :, 0]
                    pos = c("cmp_pos_2", kv * 16 + mh * 8, 8).unsqueeze(2).unsqueeze(3).broadcast_to([P, 8, 2, N_CMP])
                    x_out = X[:, kv, mh * 8:mh * 8 + 8, :].rearrange("p m (g c) -> p m g c", g=2)
                    yield
                    v = dve.do(lambda e, x_in=x_in, pos=pos, x_out=x_out: e.tensor_tensor(x_out, x_in, pos, ALU.add),
                               act.now())
            yield
            at, ps, free = banks.take()
            for kv in range(2):
                for m in range(16):
                    done = pe.do(mm(ps[:, kv * 30:kv * 30 + 30], cmpw1[:, kv, m, :], X[:, kv, m, :], m == 0, m == 15),
                                 v, *free)
            for kv in range(2):
                yield
                a = act.do(lambda e, kv=kv, ps=ps: e.activation(
                    HD[:, kv * 30:kv * 30 + 30], ps[:, kv * 30:kv * 30 + 30], ACT.Gelu_apprx_tanh,
                    bias=c("cmp_b1_2", kv)), done)
            banks.release(at, 1, a)
            yield
            at, ps, free = banks.take()
            pe.do(mm(ps[0:64, 0:30], cmpw2[:, 0:64], HD[:, 0:30]), a, *free)
            for g in range(NSA_G):
                done = pe.do(mm(ps[0:N_CMP, 64 + g * 64:128 + g * 64], HD[:, 30 + g * N_CMP:30 + (g + 1) * N_CMP],
                                cmpw2[:, 64:128]))
            dve.do(lambda e, ps=ps: e.tensor_scalar(KCT[0:64, :], ps[0:64, 0:30], c("cmp_b2_2")[0:64, :], None,
                                                    ALU.add), done)
            yield
            v = dve.do(lambda e, ps=ps: e.tensor_tensor(
                VC[0:N_CMP, :, :], ps[0:N_CMP, 64:192].rearrange("p (g d) -> p g d", g=NSA_G),
                row[0:N_CMP, 0:64].unsqueeze(1).broadcast_to([N_CMP, NSA_G, NSA_D]), ALU.add))
            banks.release(at, 1, v)

            scale = NSA_D ** -0.5
            gate = lambda t, b, lo, hi: GA[:, t, :].rearrange("p (h b) -> p h b", b=3)[:, lo:hi, b]
            dve.wait(gates_ready)
            free0 = cmpw1.rearrange("p a b c -> p (a b c)")
            buffers = [(free0[:, 0:1024].rearrange("p (h n) -> p h n", n=P), free0[:, 1024:2048],
                        free0[:, 2048:4096].rearrange("p (a n) -> p a n", a=2),
                        [cut(4, P)], [cut(16)]), (PC, PCT, PT, W, stats)]
            v = dve.do(lambda e: e.memset(buffers[0][0], 0.0))

            def tile(t, v=v):
                PC, PCT, PT, W, stats = buffers[t]
                turn_w, length = 0, (t + 1) * P

                def products(ps, needs, t=t):
                    for hd in range(NSA_H):
                        done = pe.do(mm(ps[:, hd * N_CMP:(hd + 1) * N_CMP], QU[0:64, hd, t * P:(t + 1) * P],
                                        KCT[0:64, (hd // 4) * N_CMP:(hd // 4 + 1) * N_CMP]), *needs)
                    return done
                pc = PC[:, :, 0:N_CMP]
                yield from softmax(products, NSA_H, N_CMP, scale, seen_add[:, t, 0:N_CMP], None, gate(t, 0, 0, 8), pc,
                        [v, act.now()], stats[0])
                yield
                v = dve.do(lambda e, t=t, pc=pc: e.tensor_tensor(
                    pc, pc, seen[:, t, 0:N_CMP].unsqueeze(1).broadcast_to([P, NSA_H, N_CMP]), ALU.mult))
                for half in range(2):
                    turn([PC[:, 4 * half + i, :] for i in range(4)], [v],
                         copy_evac(act, PCT[:, half * 512:(half + 1) * 512]))
                for b, keys in ((0, KST), (1, KWT)):
                    for g in range(NSA_G):
                        def products(ps, needs, t=t, keys=keys, g=g, length=length):
                            for i in range(4):
                                done = pe.do(mm(ps[:, i * length:(i + 1) * length],
                                                QT[0:64, 4 * g + i, t * P:(t + 1) * P], keys[0:64, g, 0:length]),
                                             *needs)
                            return done
                        w = W[turn_w % len(W)][:, :, 0:length]
                        v = yield from softmax(products, 4, length, scale, causal[:, t, 0:length], None,
                                    gate(t, 1 + b, 4 * g, 4 * g + 4), w, [act.now()], stats[turn_w % len(W)])
                        turn_w += 1
                        yield
                        for k in range(t + 1):
                            turn([w[:, i, k * P:(k + 1) * P] for i in range(4)], [v],
                                 copy_evac(act, PT[:, (t + 1) * b + k, g * 512:(g + 1) * 512]))
                yield
                at, ps, free = banks.take()
                for hd in range(NSA_H):
                    g = hd // 4
                    s = slice(hd * P, (hd + 1) * P)
                    o = ps[:, hd * 64:(hd + 1) * 64]
                    terms = [(PCT[:, s], VC[:, g, :])]
                    for k in range(t + 1):
                        terms.append((PT[:, k, s], zkv[:, k, 384 + g * 64:448 + g * 64]))
                        terms.append((PT[:, t + 1 + k, s], zw[:, k, 128 + g * 64:192 + g * 64]))
                    for i, (a, b) in enumerate(terms):
                        done = pe.do(mm(o, a, b, i == 0, i == len(terms) - 1), act.now(), *free)
                yield
                v = dve.do(lambda e, ps=ps, t=t: e.tensor_copy(NS[:, t, :], ps), done)
                banks.release(at, 1, v)

            attend += [tile, NS]

        def memory():
            used[0] = 0
            M = places["tokens"]
            QM, KM, VM = cut(8, T), cut(8, T), cut(TT, D)
            buffers = [(cut(MEM_H, T), cut(TT, MEM_H * P), cut(8)) for _ in range(TT)]
            OM = cut(TT, D)
            t = feature_major(M, lambda k: c("mem_kv_norm_g_2", k), [])
            k_first, _ = multiply("mem_k", False, *t)
            v_first, _ = multiply("mem_v", True)
            four = lambda dst: lambda at: dst[:, 4 * at:4 * at + 4, :].rearrange("p k t -> p (k t)")
            halves = lambda dst: lambda at: dst[:, :, at * CW:(at + 1) * CW].rearrange("p t n -> p (t n)")

            def v_hook(e, slot, m):
                e.wait_ge(s_use, m * UNITS + UNITS)
                at = (m - v_first) * CW
                e.activation(VM[:, :, at:at + CW], ps_chunk[slot][:, :].rearrange("p (t n) -> p t n", t=TT),
                             ACT.Copy).then_inc(s_ev, 1)

            split_chunks(k_first, 2, act_hooks=(copy_hook(k_first, four(KM)),))
            split_chunks(v_first, 2, act_hooks=(v_hook,))
            for lane in (act, dve):
                lane.wait((s_use, UNITS * (v_first + 2)))
            scaled = rms_scale(h)
            t = feature_major(xn, lambda k: c("mem_q_norm_g_2", k), scaled)
            q_first, _ = multiply("mem_q", False, *t)
            split_chunks(q_first, 2, act_hooks=(copy_hook(q_first, four(QM)),))
            ready = (s_ev, q_first + 2)

            def tile(t):
                W, PT, stats = buffers[t]

                def products(ps, needs):
                    for hd in range(MEM_H):
                        for k in range(2):
                            done = pe.do(mm(ps[:, hd * T:(hd + 1) * T], QM[:, 2 * hd + k, t * P:(t + 1) * P],
                                            KM[:, 2 * hd + k, :], k == 0, k == 1), *needs)
                    return done

                v = yield from softmax(products, MEM_H, T, 256 ** -0.5, None, None, None, W, [ready], stats)
                yield
                for k in range(TT):
                    turn([W[:, hd, k * P:(k + 1) * P] for hd in range(MEM_H)], [v], copy_evac(act, PT[:, k, :]))
                yield
                at, ps, free = banks.take(2)
                for hd in range(MEM_H):
                    for k in range(TT):
                        done = pe.do(mm(ps[:, hd * T:(hd + 1) * T], PT[:, k, hd * P:(hd + 1) * P],
                                        VM[:, k, hd * T:(hd + 1) * T], k == 0, k == 1), act.now(), *free)
                yield
                v = dve.do(lambda e, ps=ps: e.tensor_copy(OM[:, t, :], ps), done)
                banks.release(at, 2, v)

            interleave(memory0=(0, 4, tile(0), 1), memory1=(4, 4, tile(1), 1))
            t = feature_major(OM, plain, [dve.now()])
            add_projection("mem_o", *t)

        def peer_select():
            used[0] = 0
            QP = cut(16, T)
            SC, SR = cut(32, P), cut(32, P)
            V16 = cut(32, 16)
            I16 = cut(32, 16)
            IU = cut(32, 16)
            C, CR = cut(16, T), cut(16, T)
            B16, PU = cut(16, 16), cut(16, 16)
            EQ = cut(2048)
            AB = cut(2, T)
            PK = cut(3, T)
            st = cut(32)
            keys = cut(2048)
            have_keys = load("keys", keys, peer_keys)
            scaled = rms_scale(h)
            t = feature_major(xn, lambda k: c("peer_norm_g_2", k), scaled)
            first, count = multiply("peer_q", False, *t)
            split_chunks(first, count, act_hooks=(copy_hook(first, chunk_rows(
                QP.rearrange("p (c k) t -> p c (k t)", k=4))),))
            pe.wait(have_keys)
            scored = [None] * 32
            for t in range(TT):
                for b in range(4):
                    at, ps, free = banks.take()
                    for i in range(4):
                        hp = 4 * b + i
                        done = pe.do(mm(ps[:, i * P:(i + 1) * P], QP[:, hp, t * P:(t + 1) * P],
                                        keys[:, hp * P:(hp + 1) * P]), (s_ev, first + count), *free)
                    lo = 16 * t + 4 * b
                    a = act.do(lambda e, ps=ps, lo=lo: e.activation(
                        SC[:, lo:lo + 4, :].rearrange("p a b -> p (a b)"), ps, ACT.Copy), done)
                    banks.release(at, 1, a)
                    scored[lo:lo + 4] = [a] * 4

            def top16(src, rest, count, values, indices, ready=None):
                iu = indices.bitcast(U32)
                passes = (
                    lambda e, i: e.max(values[:, i, 0:8], src[:, i, :]),
                    lambda e, i: e.match_replace(out=rest[:, i, :], in_to_replace=values[:, i, 0:8],
                                                 in_values=src[:, i, :], imm_value=-3e38),
                    lambda e, i: e.max(values[:, i, 8:16], rest[:, i, :]),
                    lambda e, i: e.max_index(iu[:, i, 0:8], values[:, i, 0:8], src[:, i, :]),
                    lambda e, i: e.max_index(iu[:, i, 8:16], values[:, i, 8:16], rest[:, i, :]))
                for n, step in enumerate(passes):
                    before = dve.now()
                    for i in range(count):
                        dve.do(lambda e, step=step, i=i: step(e, i), before, ready[i] if ready and n == 0 else None,
                               own=False)

            early_rows()
            top16(SC, SR, 32, V16, IU, scored)
            dve.do(lambda e: e.tensor_copy(I16, IU.bitcast(U32)))
            wide = [P, PEER_H, 16, 16]
            half = lambda a, t, s: a[:, 16 * t:16 * t + 16, :].rearrange("p (h s) k -> p h s k", s=2)[:, :, s, :]
            for t in range(TT):
                dve.do(lambda e, t=t: e.tensor_tensor(
                    C[:, 8 * t:8 * t + 8, :].rearrange("p h (a b) -> p h a b", a=16),
                    half(V16, t, 0).unsqueeze(3).broadcast_to(wide), half(V16, t, 1).unsqueeze(2).broadcast_to(wide),
                    ALU.add))
            top16(C, CR, 16, B16, PU)
            pos = PU.rearrange("p a b -> p (a b)").bitcast(U32)
            ab_u = CR[:, 0:2, :].bitcast(U32)
            dve.do(lambda e: e.tensor_scalar(ab_u[:, 0, :], pos, 4, None, ALU.logical_shift_right))
            dve.do(lambda e: e.tensor_scalar(ab_u[:, 1, :], pos, 15, None, ALU.bitwise_and))
            dve.do(lambda e: e.tensor_copy(AB, ab_u))
            eq = EQ.rearrange("p (h k j) -> p h k j", h=PEER_H, k=16)
            for s in range(2):
                for t in range(TT):
                    which = AB[:, s, t * P:(t + 1) * P].rearrange("p (h k) -> p h k", h=PEER_H)
                    dve.do(lambda e, which=which: e.tensor_tensor(
                        eq, iota[:, 0:16].unsqueeze(1).unsqueeze(1).broadcast_to(wide),
                        which.unsqueeze(3).broadcast_to(wide), ALU.is_equal))
                    dve.do(lambda e, t=t, s=s: e.tensor_tensor(
                        eq, eq, half(I16, t, s).unsqueeze(2).broadcast_to(wide), ALU.mult))
                    dve.do(lambda e, t=t, s=s: e.tensor_reduce(
                        PK[:, s, t * P:(t + 1) * P], EQ.rearrange("p (r j) -> p r j", j=16), AX.X, ALU.add))
            rows16 = PK[:, 2, :].rearrange("p (r k) -> p r k", k=16)
            v = dve.do(lambda e: e.tensor_tensor(rows16, B16, B16[:, :, 0:1].broadcast_to([P, 16, 16]), ALU.subtract))
            a = act.do(lambda e: e.activation(PK[:, 2, :], PK[:, 2, :], ACT.Exp), v)
            dve.do(lambda e: e.tensor_reduce(st[:, 0:16], rows16, AX.X, ALU.add), a)
            dve.do(lambda e: e.reciprocal(st[:, 0:16], st[:, 0:16]))
            v = dve.do(lambda e: e.tensor_tensor(rows16, rows16, st[:, 0:16].unsqueeze(2).broadcast_to([P, 16, 16]),
                                                 ALU.mult))
            for what in ((0, 1), (2,)):
                turn([PK[:, i, t * P:(t + 1) * P] for i in what for t in range(TT)], [v],
                     copy_evac(act, picks[:, what[0]:what[-1] + 1, :].rearrange("p a t -> p (a t)")))

        early = nc.dram_tensor("early_rows", [EARLY, P, T], F32, kind="Internal").ap()
        s_spill = [sem(f"s_spill{b}") for b in range(2)]
        s_gel, s_own, s_hih, s_hid = (sem(n) for n in ("s_gel", "s_own", "s_hih", "s_hid"))
        gel = [row[:, s * T:(s + 1) * T] for s in range(4)]
        u_early = UNITS * STREAM["peer early u"][0]
        chunk_early = STREAM["peer early u"][0]

        def u_products(e, b, w, u, tiles, part):
            _, made, used_up = halves_of_unit[part]
            e.wait_ge(made, u + 1)
            for k in tiles:
                last = product3(e, ps_chunk[b][:, 0:T], [a[w][:, k * P:(k + 1) * P] for a in (w_hi, w_lo)],
                                [x[:, k, :] for x in (x_hi, x_lo)], k == 0, k == KD - 1)
            if k % 4 == 3:
                last.then_inc(used_up, 1)

        def bank_left(e, i):
            if not isinstance(i, int) or i > 1:
                e.wait_ge(s_gel, i - 1)

        def early_gelu(e, q, i):
            e.wait_ge(s_use, i + (u_early + 1))
            if not isinstance(i, int) or i > 1:
                e.wait_ge(s_spill[q % 2], (i - q) * 8 + (q // 2) * 16)
            e.activation(gel[q % 2], ps_chunk[q % 2][:, 0:T], ACT.Gelu_apprx_tanh).then_inc(s_gel, 1)
            e.wait_ge(s_gel, i + 1)
            dst = early[i, :, :] if isinstance(i, int) else early[bass.ds(i, 1), :, :].rearrange("a p n -> p (a n)")
            e.dma_start(dst, gel[q % 2]).then_inc(s_spill[q % 2], 16)

        def ahead(e, q, chunk, i):
            split_hi(e, (q + 1) % 4, chunk + (chunk_early + (q + 1) // 4))

        s_back = [sem(f"s_back{q}") for q in range(4)]

        def fetch(e, q, c=0):
            i = c * 4 + q
            src = early[i, :, :] if isinstance(i, int) else early[bass.ds(i, 1), :, :].rearrange("a p n -> p (a n)")
            e.dma_start(gel[(q + 2) % 4], src).then_inc(s_back[q % 4], 16)

        def early_rows():
            def tensor_rows(e):
                def four(c):
                    for q in range(UNITS):
                        bank_left(e, c * 4 + q)
                        for part in range(2):
                            u_products(e, q % 2, q % 2, c * 4 + (u_early + q), range(4 * part, 4 * part + 4), part)
                four(0)
                with e.Fori(1, EARLY_SELECT // 4) as c:
                    four(c)

            def activation_rows(e):
                def four(c):
                    for q in range(UNITS):
                        ahead(e, q, c, None)
                        early_gelu(e, q, c * 4 + q)
                split_hi(e, 0, chunk_early)
                four(0)
                with e.Fori(1, EARLY_SELECT // 4) as c:
                    four(c)

            def pool_rows(e):
                with e.Fori(0, EARLY // 4) as c:
                    for q in range(UNITS):
                        split_lo(e, q, c + chunk_early)

            pe.steps.append(tensor_rows)
            act.steps.append(activation_rows)
            pool.wait((s_lo1, u_early), (s_lo, u_early))
            pool.steps.append(pool_rows)

        def peer_gates():
            phase("peer", ("arena", [P, P * T], F32))
            G = places["arena"][:, :].rearrange("p (s n) -> p s n", n=4 * P)
            cols_hot = [xn[:, 0, 512 * s:512 * s + 512].rearrange("p (a b) -> p a b", b=P) for s in range(2)]
            rows_hot = [xn[:, 1, 512 * s:512 * s + 512].rearrange("p (a b) -> p a b", b=P) for s in range(2)]
            s_rows, s_cols, s_made, s_kept = (sem(n) for n in ("s_rows", "s_cols", "s_made", "s_kept"))
            groups = T // 4
            wide = [P, 4, P]

            def loop(e, body):
                for g in range(4):
                    body(e, g, g)
                with e.Fori(1, groups // 4) as i:
                    for g in range(4):
                        body(e, i * 4 + g, g)

            def after(e, s, n, back):
                if not isinstance(n, int) or n >= back:
                    e.wait_ge(s, n - (back - 1))

            def hot_body(e, n, g):
                after(e, s_made, n, 2)
                r = picks[:, 0, bass.ds(n * 4, 4)] if not isinstance(n, int) else picks[:, 0, 4 * n:4 * n + 4]
                e.tensor_tensor(rows_hot[g % 2], iota.unsqueeze(1).broadcast_to(wide),
                                r.unsqueeze(2).broadcast_to(wide), ALU.is_equal).then_inc(s_rows, 1)

                for i in range(4):
                    at = n * 4 + i
                    pick = (lambda q: picks[:, q, at:at + 1]) if isinstance(at, int) else (
                        lambda q: picks[:, q, bass.ds(at, 1)])
                    last = e.tensor_scalar(cols_hot[g % 2][:, i, :], iota, pick(1), pick(2), ALU.is_equal, ALU.mult)
                last.then_inc(s_cols, 1)

            def made_body(e, n, g):
                e.wait_ge(s_rows, n + 1)
                e.wait_ge(s_cols, n + 1)
                after(e, s_kept, n, 4)
                for i in range(4):
                    last = e.matmul(ps_misc[:, g, i * P:(i + 1) * P], cols_hot[g % 2][:, i, :],
                                    rows_hot[g % 2][:, i, :], start=True, stop=True)
                last.then_inc(s_made, 1)

            def kept_body(e, n, g):
                e.wait_ge(s_made, n + 1)
                o = G[:, n, :] if isinstance(n, int) else G[:, bass.ds(n, 1), :].rearrange("p a n -> p (a n)")
                e.activation(o, ps_misc[:, g, :], ACT.Copy).then_inc(s_kept, 1)

            def four_rows(c, group, row):
                for q in range(UNITS):
                    for g in range(4):
                        group(c * 16 + (4 * q + g), g)
                        row(c, q, g)

            def tensor_gates(e):
                def row(c, q, g):
                    i = c * 4 + (EARLY_SELECT + q)
                    if g == 0:
                        bank_left(e, i)
                    u_products(e, q % 2, q % 2, c * 4 + (u_early + EARLY_SELECT + q), (2 * g, 2 * g + 1), g // 2)
                group = lambda n, g: made_body(e, n, g)
                four_rows(0, group, row)
                with e.Fori(1, EARLY_GATES // 4) as c:
                    four_rows(c, group, row)

            def activation_gates(e):
                def row(c, q, g):
                    if g == 1:
                        ahead(e, q, c + EARLY_SELECT // 4, None)
                    if g == 3:
                        early_gelu(e, q, c * 4 + (EARLY_SELECT + q))
                group = lambda n, g: kept_body(e, n, g)
                for i in range(2):
                    fetch(e, i)
                four_rows(0, group, row)
                with e.Fori(1, EARLY_GATES // 4) as c:
                    four_rows(c, group, row)

            dve.steps.append(lambda e: loop(e, hot_body))
            pe.steps.append(tensor_gates)
            act.steps.append(activation_gates)
            for lane in work:
                lane.wait((s_kept, groups))

        def peer_experts():
            v_chunk = STREAM["peer early v"][0]
            v0 = UNITS * v_chunk
            first, count = STREAM["peer"]
            chunk_at[0] = first + count
            u0 = UNITS * first
            rest = P - EARLY
            G = places["arena"][:, :].rearrange("p (t i) -> p t i", i=P)
            own = [xn[:, 1, s * T:(s + 1) * T] for s in range(2)]

            def v_unit(e, b, w, i, u, begin=False, end=False):
                e.wait_ge(s_hid, i + 1)
                for half, made, used_up in halves_of_unit:
                    e.wait_ge(made, u + 1)
                    for t in range(TT):
                        last = product3(e, ps_misc[:, 2 * t + half, :],
                                        [x[:, b, t * P:(t + 1) * P] for x in (hid_hi, hid_lo)],
                                        [a[w][:, half * CW:(half + 1) * CW] for a in (w_hi, w_lo)], begin, end)
                    last.then_inc(used_up, 1)

            def gate_row(e, b, slot, i):
                g = G[:, :, i] if isinstance(i, int) else G[:, :, bass.ds(i, 1)].rearrange("p t a -> p (t a)")
                e.tensor_tensor(own[b], gel[slot], g, ALU.mult).then_inc(s_own, 1)
                e.wait_ge(s_own, i + 1)
                e.tensor_copy(hid_hi[:, b, :], own[b]).then_inc(s_hih, 1)
                e.wait_ge(s_hih, i + 1)
                e.tensor_tensor(hid_lo[:, b, :], own[b], hid_hi[:, b, :].bitcast(F32), ALU.subtract).then_inc(s_hid, 1)

            def tensor_early(e):
                def two(c, begin=False):
                    for q in range(2):
                        v_unit(e, q, q, c * 2 + q, c * 2 + (v0 + q), begin=begin and q == 0)
                two(0, True)
                with e.Fori(1, EARLY // 2) as c:
                    two(c)

            def activation_early(e):
                def four(c, end=False):
                    for q in range(UNITS):
                        if not (isinstance(c, int) and c == 0 and q == 0):
                            split_hi(e, q, c + v_chunk)
                            if not (end and q):
                                e.wait_ge(s_own, c * 4 + q)
                        if not (end and q):
                            fetch(e, q + 3, c)
                for b in range(2):
                    e.wait_ge(s_spill[b], EARLY // 2 * 16)
                fetch(e, 2)
                four(0)
                with e.Fori(1, EARLY // 4 - 1) as c:
                    four(c)
                four(EARLY // 4 - 1, True)

            def vector_early(e):
                def four(c):
                    for q in range(UNITS):
                        if not isinstance(c, int) or c * 4 + q >= 2:
                            e.wait_ge(s_use, c * 4 + (v0 + q - 1))
                        e.wait_ge(s_back[q], c * 16 + 16)
                        gate_row(e, q % 2, (q + 2) % 4, c * 4 + q)
                        split_lo(e, q, c + v_chunk)
                four(0)
                with e.Fori(1, EARLY // 4) as c:
                    four(c)

            def unused(e, u):
                e.wait_ge(s_lo, u + 1)
                e.wait_ge(s_use, u)
                e.sem_inc(s_use1, 1)
                e.sem_inc(s_use, 1)

            def tensor_rest(e):
                def u_row(b, j):
                    bank_left(e, j + EARLY)
                    for part in range(2):
                        u_products(e, b, 0, j * 2 + u0, range(4 * part, 4 * part + 4), part)

                def v_row(b, j, end=False):
                    v_unit(e, b, 1, j + EARLY, j * 2 + (u0 + 3), end=end)

                u_row(0, 0)
                unused(e, u0 + 1)
                u_row(1, 1)
                v_row(0, 0)
                with e.Fori(1, rest // 2) as m:
                    for b in range(2):
                        u_row(b, m * 2 + b)
                        v_row(1 - b, m * 2 + (b - 1))
                unused(e, u0 + 2 * rest)
                v_row(1, rest - 1, end=True)
                unused(e, u0 + 2 * rest + 2)
                unused(e, u0 + 2 * rest + 3)

            def gelu(e, b, j):
                e.wait_ge(s_use, j * 2 + (u0 + 1))
                e.wait_ge(s_own, j + (EARLY - 1))
                e.activation(gel[b], ps_chunk[b][:, 0:T], ACT.Gelu_apprx_tanh).then_inc(s_gel, 1)

            def gated(e, b, j):
                e.wait_ge(s_gel, j + (EARLY + 1))
                gate_row(e, b, b, j + EARLY)

            def rows(split, work_on_row):
                def run(e):
                    def pair(m):
                        for b in range(2):
                            split(e, 2 * b + 1, m + first)
                            split(e, (2 * b + 2) % 4, m + (first + b))
                            work_on_row(e, b, m * 2 + b)
                    split(e, 0, first)
                    pair(0)
                    with e.Fori(1, rest // 2) as m:
                        pair(m)
                    for q in range(1, UNITS):
                        split(e, q, first + rest // 2)
                return run

            dve.wait((s_lo1, v0), (s_lo, v0))
            pe.steps += [tensor_early, tensor_rest]
            act.steps += [activation_early, rows(split_hi, gelu)]
            dve.steps += [vector_early, rows(split_lo, gated)]
            dve.wait((s_use, u0 + UNITS * count))
            hf = h[:, :, :].rearrange("p t n -> p (t n)")
            summed = dve.do(lambda e: e.tensor_tensor(hf, hf, ps_misc[:, :, :].rearrange("p b n -> p (b n)"), ALU.add))
            act.wait(summed)

        def finish():
            have_gain = load("gain_2", row[:, :], rows[3:4, :].broadcast_to([P, D]))
            for t, v in enumerate(rms_gain(h, xn, have_gain)):
                sp_out[0] += 16
                act.quiet(lambda e, t=t: e.dma_start(out[t * P:(t + 1) * P, :], xn[:, t, :]).then_inc(s_out, 16), v)

        mixers_2()
        add_projection("w_out_2", act.now(), dve.now())
        fence()
        memory()
        fence()
        peer_select()
        fence()
        peer_gates()
        peer_experts()
        finish()
        act.wait((s_out, sp_out[0]))

        memory_of.close()
        with nc.Block() as block:
            @block.sync
            def _(e):
                sp.emit(e)

            @block.tensor
            def _(e):
                pe.emit(e)

            @block.vector
            def _(e):
                dve.emit(e)

            @block.scalar
            def _(e):
                act.emit(e)

            @block.gpsimd
            def _(e):
                pool.emit(e)



def feature_units(w):
    return w.reshape(KD, P, -1, P).transpose(2, 1, 0, 3).reshape(-1, P, UNIT)


def token_units(w):
    n = -(-w.shape[1] // CW)
    full = np.zeros((D, n * CW), w.dtype)
    full[:, :w.shape[1]] = w
    return full.reshape(UNITS, 2, P, n, CW).transpose(3, 0, 2, 1, 4).reshape(-1, P, UNIT)


def lay_out(a):
    w = a["w_in"][0]
    aq, af, ai, ag = (w[:, 512 * n:512 * (n + 1)] for n in range(4))
    bq, bk, bv, cc = w[:, 2048:2304], w[:, 2304:2560], w[:, 2560:2816], w[:, 2816:]
    parts = {}
    parts["w_in feature"] = feature_units(np.concatenate([cc, aq, af, bq, bk], 1))
    parts["w_in token"] = token_units(np.concatenate([ai, ag, bv], 1))
    parts["w_out"] = token_units(a["w_out"][0])
    up = a["ffn_up"][0].reshape(D, 2, NF // 2, 2 * P).transpose(0, 2, 1, 3).reshape(D, 2 * D_FF)
    parts["ffn_up"] = feature_units(up)
    parts["ffn_down, ple_proj"] = np.concatenate([a["ffn_down"][0], a["ple_proj"][0]], 0).reshape(-1, P, D)
    parts["ple_gate"] = token_units(a["ple_gate"][0])
    w = a["w_in_2"][0]
    parts["w_in_2 feature"] = feature_units(w[:, :2 * CW])
    parts["w_in_2 token"] = token_units(w[:, 2 * CW:])
    parts["w_out_2"] = token_units(a["w_out_2"][0])
    for n, units in (("q", feature_units), ("k", feature_units), ("v", token_units), ("o", token_units)):
        parts["mem_" + n] = units(a["w_mem_%s_2" % n][0])
    parts["peer_q"] = feature_units(a["peer_w_q_2"][0])
    stream = np.zeros((UNITS * N_CHUNKS, P, UNIT), np.float32)
    for name, (first, count) in STREAM.items():
        if not name.startswith("peer ") and name != "peer":
            assert parts[name].shape[0] == UNITS * count, (name, parts[name].shape, count)
            stream[UNITS * first:UNITS * (first + count)] = parts[name]
    u = a["peer_u_2"][0].reshape(P, P, KD, P).transpose(0, 3, 2, 1).reshape(P, P, UNIT)
    v = a["peer_v_2"][0].reshape(P, P, D)
    peer = stream[UNITS * STREAM["peer early u"][0]:]
    peer[0:EARLY], peer[EARLY:2 * EARLY] = u[:EARLY], v[:EARLY]
    rest = peer[2 * EARLY:]
    rest[0:2 * (P - EARLY):2] = u[EARLY:]
    rest[3:2 * (P - EARLY) + 3:2] = v[EARLY:]

    cols = np.zeros((P, N_COLS), np.float32)

    def put(name, value):
        at, n = COLS[name]
        cols[:, at:at + n] = value

    tiles = lambda v: v.reshape(-1, P).T
    for name, (at, n) in COLS.items():
        if name in a and name not in ("conv_dw_w_2", "cmp_b1_2", "cmp_b2_2", "cmp_pos_2"):
            put(name, tiles(a[name]))
    taps = np.concatenate([a["ffn_conv_w"][0], a["ffn_conv_b"]], 0)
    put("ffn_conv", taps.reshape(4, 2, NF // 2, 2, P).transpose(4, 2, 1, 3, 0).reshape(P, -1))
    put("conv_dw_w_2", a["conv_dw_w_2"][0].reshape(CONV_K, CONV_T, P).transpose(2, 0, 1).reshape(P, -1))
    put("cmp_b1_2", a["cmp_b1_2"][0].T)
    put("cmp_b2_2", np.concatenate([a["cmp_b2_2"][0, 0], np.zeros(64, np.float32)])[:, None])
    put("cmp_pos_2", a["cmp_pos_2"][0].reshape(2, CMP_B // 2, P).transpose(2, 0, 1).reshape(P, 32))
    put("eps", EPS)
    put("gn_eps", RK_GN_EPS)
    put("one", 1.0)
    rows = np.zeros((4, D), np.float32)
    for name, (at, n) in ROWS_1.items():
        rows[0, at:at + n] = a[name].reshape(-1)
    rows[1] = a["final_norm_g"]
    rows[2, 0:64] = a["cmp_b2_2"][0, 1]
    rows[3] = a["final_norm_g_2"]
    w1 = a["cmp_w1_2"][0].reshape(2, CMP_B // 2, P, P).transpose(2, 0, 1, 3).reshape(P, -1)
    keys = a["peer_sub_keys_2"][0].reshape(16, P, P).transpose(2, 0, 1).reshape(P, 16 * P)
    p_t = a["p"][0, 0].T.reshape(2, P, T).transpose(1, 0, 2).reshape(P, 2 * T)
    small = np.zeros((P, 512), np.float32)
    small[:64, :256], small[64:, :256], small[:, 256:] = a["rwkv_w2"][0], a["rwkv_a2"][0], a["rwkv_g2"][0]
    return {"stream": stream, "cols": cols, "rows": rows, "consts0": CONSTS[0], "consts1": CONSTS[1],
            "consts2": CONSTS[2], "x": a["x"][0], "mem": a["mem_2"][0],
            "positions": np.ascontiguousarray(a["positions_2"].reshape(TT, P).T),
            "small_w": small, "cmp_w1": np.ascontiguousarray(w1), "peer_keys": np.ascontiguousarray(keys),
            "p_t": np.ascontiguousarray(p_t), "cmp_w2": np.ascontiguousarray(a["cmp_w2_2"][0].transpose(1, 0, 2).reshape(P, 128))}


def kernel(**inputs):
    import concourse.bacc as bacc
    from concourse.bass_utils import run_bass_kernel_spmd

    arrays = lay_out({name: np.asarray(value) for name, value in inputs.items()})
    nc = bacc.Bacc("TRN2", target_bir_lowering=False, num_devices=1)
    aps = {name: nc.dram_tensor("in_" + name, a.shape, mybir.dt.from_np(a.dtype), kind="ExternalInput").ap()
           for name, a in arrays.items()}
    out = nc.dram_tensor("out", (T, D), F32, kind="ExternalOutput").ap()
    build(nc, out=out, **aps)
    result = run_bass_kernel_spmd(nc, [{"in_" + name: a for name, a in arrays.items()}], core_ids=[0])
    return result.results[0]["out"].reshape(1, T, D)
```
